# Optimizing a Trainium2 kernel written in Bass

```python
import jax, jax.numpy as jnp
from jax import lax
import numpy as np
import math
import jax
import jax.numpy as jnp

D_MODEL = 1024
BATCH = 1
SEQ = 1024
DEPTH = 1

CHUNK = 64
Q_BLOCK = 128
EPS = 1e-6

POOL_WIDTH = D_MODEL // 4
POOL_WINDOWS = (2, 4, 8, 16)
POOL_GROUPS = len(POOL_WINDOWS)
POOL_GROUP = POOL_WIDTH // POOL_GROUPS
GLA_WIDTH = D_MODEL // 4
GLA_HEADS = 4
GLA_HEAD_DIM = GLA_WIDTH // GLA_HEADS
GLA_GATE_RANK = 16
GLA_TAU = 16.0
FOX_WIDTH = D_MODEL - POOL_WIDTH - GLA_WIDTH
FOX_HEAD_DIM = 64
FOX_HEADS = FOX_WIDTH // FOX_HEAD_DIM
D_FF = ((-(-8 * D_MODEL // 3)) + 255) // 256 * 256

IN_SIZES = (POOL_WIDTH,
            GLA_WIDTH, GLA_WIDTH, GLA_WIDTH, GLA_WIDTH,
            GLA_GATE_RANK,
            FOX_WIDTH, FOX_WIDTH, FOX_WIDTH,
            FOX_HEADS)
IN_WIDTH = sum(IN_SIZES)


def _split_points():
    pts, acc = [], 0
    for s in IN_SIZES[:-1]:
        acc += s
        pts.append(acc)
    return pts

def rmsnorm(x, g):
    x32 = x.astype(jnp.float32)
    y = x32 * lax.rsqrt(jnp.mean(x32 * x32, axis=-1, keepdims=True) + EPS) * g.astype(jnp.float32)
    return y.astype(x.dtype)

def pool_mixer(u, w_pool, pool_scale):
    B, T, _ = u.shape
    u32 = u.astype(jnp.float32)
    cs = jnp.cumsum(u32, axis=1)
    cs_pad = jnp.concatenate([jnp.zeros((B, 1, POOL_WIDTH), jnp.float32), cs], axis=1)
    t1 = jnp.arange(1, T + 1)
    means = []
    for gi, w in enumerate(POOL_WINDOWS):
        lo, hi = gi * POOL_GROUP, (gi + 1) * POOL_GROUP
        lagged = jnp.concatenate([jnp.zeros((B, w - 1, POOL_GROUP), jnp.float32),
                                  cs_pad[:, :T - w + 1, lo:hi]], axis=1)
        cnt = jnp.minimum(t1, w).astype(jnp.float32)
        means.append((cs[:, :, lo:hi] - lagged) / cnt[None, :, None])
    d = (jnp.concatenate(means, axis=-1) - u32).astype(u.dtype)
    d = d.reshape(B, T, POOL_GROUPS, POOL_GROUP)
    y = jnp.einsum('btgc,gcd->btgd', d, w_pool).reshape(B, T, POOL_WIDTH)
    return y * pool_scale

def gla_mixer(q, k, v, g, a_low, w_a_up, b_a, gla_gn):
    B, T, _ = q.shape
    H, Dh, C = GLA_HEADS, GLA_HEAD_DIM, CHUNK
    NC = T // C

    def heads(z):
        return z.astype(jnp.float32).reshape(B, NC, C, H, Dh).transpose(0, 3, 1, 2, 4)

    log_a = jax.nn.log_sigmoid(jnp.einsum('btr,rd->btd', a_low.astype(jnp.float32),
                                          w_a_up.astype(jnp.float32)) + b_a.astype(jnp.float32)) / GLA_TAU
    qh = heads(q) * (Dh ** -0.5)
    kh, vh, la = heads(k), heads(v), heads(log_a)
    bcum = jnp.cumsum(la, axis=3)
    b_last = bcum[:, :, :, -1:, :]
    ref = bcum[:, :, :, C // 2 - 1:C // 2, :]

    q_in = qh * jnp.exp(bcum - ref)
    k_in = kh * jnp.exp(ref - bcum)
    causal = jnp.tril(jnp.ones((C, C), dtype=bool))
    att = jnp.where(causal, jnp.einsum('bhncd,bhnsd->bhncs', q_in, k_in), 0.0)
    o_intra = jnp.einsum('bhncs,bhnse->bhnce', att, vh)

    kv = jnp.einsum('bhncd,bhnce->bhnde', kh * jnp.exp(b_last - bcum), vh)
    dec = jnp.exp(b_last[:, :, :, 0, :])

    def step(S, inp):
        kv_n, dec_n = inp
        return dec_n[..., None] * S + kv_n, S

    S0 = jnp.zeros((B, H, Dh, Dh), jnp.float32)
    _, S_prev = lax.scan(step, S0, (kv.transpose(2, 0, 1, 3, 4), dec.transpose(2, 0, 1, 3)))
    S_prev = S_prev.transpose(1, 2, 0, 3, 4)
    o_inter = jnp.einsum('bhncd,bhnde->bhnce', qh * jnp.exp(bcum), S_prev)

    o = o_intra + o_inter
    o = o * lax.rsqrt(jnp.mean(o * o, axis=-1, keepdims=True) + EPS)
    o = o.transpose(0, 2, 3, 1, 4).reshape(B, T, GLA_WIDTH) * gla_gn.astype(jnp.float32)
    return (o * jax.nn.silu(g.astype(jnp.float32))).astype(q.dtype)

def fox_mixer(q, k, v, f_logit, b_f):
    B, T, _ = q.shape
    H, Dh = FOX_HEADS, FOX_HEAD_DIM
    nb = T // Q_BLOCK

    def heads(z):
        return z.astype(jnp.float32).reshape(B, T, H, Dh).transpose(0, 2, 1, 3)

    qh = heads(q) * (Dh ** -0.5)
    kh, vh = heads(k), heads(v)
    logf = jax.nn.log_sigmoid(f_logit.astype(jnp.float32) + b_f.astype(jnp.float32))
    F = jnp.cumsum(logf, axis=1).transpose(0, 2, 1)
    q_blocks = qh.reshape(B, H, nb, Q_BLOCK, Dh).transpose(2, 0, 1, 3, 4)
    F_blocks = F.reshape(B, H, nb, Q_BLOCK).transpose(2, 0, 1, 3)
    kpos = jnp.arange(T)

    def block(args):
        qb, Fb, i = args
        s = jnp.einsum('bhqd,bhkd->bhqk', qb, kh) + Fb[..., None] - F[:, :, None, :]
        qpos = i * Q_BLOCK + jnp.arange(Q_BLOCK)
        s = jnp.where(kpos[None, :] <= qpos[:, None], s, -jnp.inf)
        p = jax.nn.softmax(s, axis=-1)
        return jnp.einsum('bhqk,bhkd->bhqd', p, vh)

    o = lax.map(block, (q_blocks, F_blocks, jnp.arange(nb)))
    return o.transpose(1, 0, 3, 2, 4).reshape(B, T, FOX_WIDTH).astype(q.dtype)

def first_inputs(seed: int = 0) -> dict:
    key = jax.random.key(seed)
    ks = jax.random.split(key, 16)
    f32 = jnp.float32
    nrm = lambda k, shape: jax.random.normal(k, shape, f32)
    return {
        "x": nrm(ks[0], (BATCH, SEQ, D_MODEL)),
        "ln1": 1.0 + 0.02 * nrm(ks[1], (DEPTH, D_MODEL)),
        "w_in": nrm(ks[2], (DEPTH, D_MODEL, IN_WIDTH)) * D_MODEL ** -0.5,
        "w_pool": nrm(ks[3], (DEPTH, POOL_GROUPS, POOL_GROUP, POOL_GROUP)) * POOL_GROUP ** -0.5,
        "pool_scale": 0.5 + 0.1 * nrm(ks[4], (DEPTH, POOL_WIDTH)),
        "w_a_up": nrm(ks[5], (DEPTH, GLA_GATE_RANK, GLA_WIDTH)) * GLA_GATE_RANK ** -0.5,
        "b_a": 0.1 * nrm(ks[6], (DEPTH, GLA_WIDTH)),
        "gla_gn": 1.0 + 0.02 * nrm(ks[7], (DEPTH, GLA_WIDTH)),
        "b_f": 3.0 + 0.5 * nrm(ks[8], (DEPTH, FOX_HEADS)),
        "w_o": nrm(ks[9], (DEPTH, D_MODEL, D_MODEL)) * D_MODEL ** -0.5,
        "ln2": 1.0 + 0.02 * nrm(ks[10], (DEPTH, D_MODEL)),
        "w_gu": nrm(ks[11], (DEPTH, D_MODEL, 2 * D_FF)) * D_MODEL ** -0.5,
        "w_down": nrm(ks[12], (DEPTH, D_FF, D_MODEL)) * D_FF ** -0.5,
        "ln_f": 1.0 + 0.02 * nrm(ks[13], (D_MODEL,)),
    }

def first_block(x, ln1, w_in, w_pool, pool_scale, w_a_up, b_a, gla_gn, b_f, w_o, ln2, w_gu, w_down, ln_f):
    pts = _split_points()
    for l in range(DEPTH):
        h = rmsnorm(x, ln1[l])
        z = jnp.einsum('btd,de->bte', h, w_in[l])
        u_pool, gq, gk, gv, gg, ga, fq, fk, fv, ff = jnp.split(z, pts, axis=-1)
        y_pool = pool_mixer(u_pool, w_pool[l], pool_scale[l])
        y_gla = gla_mixer(gq, gk, gv, gg, ga, w_a_up[l], b_a[l], gla_gn[l])
        y_fox = fox_mixer(fq, fk, fv, ff, b_f[l])
        mix = jnp.concatenate([y_pool.astype(x.dtype), y_gla.astype(x.dtype), y_fox.astype(x.dtype)], axis=-1)
        x = x + jnp.einsum('btd,de->bte', mix, w_o[l])
        h = rmsnorm(x, ln2[l])
        gate, up = jnp.split(jnp.einsum('btd,df->btf', h, w_gu[l]), 2, axis=-1)
        x = x + jnp.einsum('btf,fd->btd', jax.nn.silu(gate) * up, w_down[l])
    return rmsnorm(x, ln_f)


CTX_LEN = 256
GRID_W = 64
N_MIXERS = 3
N_ATTN = (DEPTH + 2) // N_MIXERS
N_FNET = (DEPTH + 1) // N_MIXERS
N_RWKV = DEPTH // N_MIXERS
NORM_EPS = 1e-6

DA_HEADS = 8
DA_HEAD_DIM = D_MODEL // DA_HEADS // 2
ROPE_BASE = 10000.0
SUBLN_EPS = 1e-5

FN_GROUPS = 8
FN_GROUP_DIM = D_MODEL // FN_GROUPS

RW_HEAD_DIM = 64
RW_HEADS = D_MODEL // RW_HEAD_DIM
RW_DECAY_RANK = 64
RW_ICLR_RANK = 64
RW_GN_EPS = 64e-5


def rms_norm(x, gain, eps=NORM_EPS):
    xf = x.astype(jnp.float32)
    y = xf * lax.rsqrt(jnp.mean(xf * xf, axis=-1, keepdims=True) + eps)
    return (y * gain.astype(jnp.float32)).astype(x.dtype)

def ada_modulation(cond, w, b):
    m = jax.nn.silu(cond) @ w + b
    return jnp.split(m, 3, axis=-1)

def axial_rope_tables(n):
    rows = n // GRID_W
    row = jnp.repeat(jnp.arange(rows), GRID_W).astype(jnp.float32)
    col = jnp.tile(jnp.arange(GRID_W), rows).astype(jnp.float32)
    axis_dim = DA_HEAD_DIM // 2
    inv_freq = ROPE_BASE ** (-jnp.arange(0, axis_dim, 2, dtype=jnp.float32) / axis_dim)
    ang = jnp.stack([row[:, None] * inv_freq, col[:, None] * inv_freq], axis=1)
    return jnp.cos(ang), jnp.sin(ang)

def apply_axial_rope(t, cos, sin):
    quarter = DA_HEAD_DIM // 4
    tf = t.astype(jnp.float32).reshape(t.shape[:-1] + (2, 2, quarter))
    t1, t2 = tf[..., 0, :], tf[..., 1, :]
    c = cos[:, None, None]
    s = sin[:, None, None]
    out = jnp.stack([t1 * c - t2 * s, t2 * c + t1 * s], axis=-2)
    return out.reshape(t.shape).astype(t.dtype)

def diff_attend(q, k, v, lam):
    s = jnp.einsum('bqhzd,bkhzd->bhzqk', q, k).astype(jnp.float32)
    p = jax.nn.softmax(s, axis=-1)
    a = p[:, :, 0] - lam * p[:, :, 1]
    return jnp.einsum('bhqk,bkhe->bqhe', a.astype(v.dtype), v)

def diff_attention(h_lat, h_ctx, cos, sin, w_in, lam_q, lam_k, subln_gain, w_out, lambda_init, need_ctx_out):
    B, N, D = h_lat.shape
    H, d = DA_HEADS, DA_HEAD_DIM
    scale = d ** -0.5

    def project(h):
        L = h.shape[1]
        q, k, v, z = jnp.split(h @ w_in, 4, axis=-1)
        return (q.reshape(B, L, H, 2, d) * scale, k.reshape(B, L, H, 2, d),
                v.reshape(B, L, H, 2 * d), z)

    q_l, k_l, v_l, z_l = project(h_lat)
    q_c, k_c, v_c, z_c = project(h_ctx)
    q_l = apply_axial_rope(q_l, cos, sin)
    k_l = apply_axial_rope(k_l, cos, sin)
    lq = lam_q.astype(jnp.float32)
    lk = lam_k.astype(jnp.float32)
    lam = jnp.exp(jnp.sum(lq[0] * lk[0])) - jnp.exp(jnp.sum(lq[1] * lk[1])) + lambda_init

    def finish(o, z):
        L = o.shape[1]
        of = o.astype(jnp.float32)
        of = of * lax.rsqrt(jnp.mean(of * of, axis=-1, keepdims=True) + SUBLN_EPS)
        of = of * subln_gain.astype(jnp.float32) * (1.0 - lambda_init)
        return (of.reshape(B, L, D).astype(z.dtype) * jax.nn.silu(z)) @ w_out

    k_all = jnp.concatenate([k_c, k_l], axis=1)
    v_all = jnp.concatenate([v_c, v_l], axis=1)
    n_blocks = N // Q_BLOCK
    q_blocks = q_l.reshape(B, n_blocks, Q_BLOCK, H, 2, d).swapaxes(0, 1)
    o_l = lax.map(lambda qb: diff_attend(qb, k_all, v_all, lam), q_blocks)
    o_l = o_l.swapaxes(0, 1).reshape(B, N, H, 2 * d)
    y_l = finish(o_l, z_l)
    y_c = finish(diff_attend(q_c, k_c, v_c, lam), z_c) if need_ctx_out else None
    return y_l, y_c

def fourier_mix(h, w_in, w_group, w_out):
    B, L, D = h.shape
    u, z = jnp.split(h @ w_in, 2, axis=-1)
    ug = u.astype(jnp.float32).reshape(B, L, FN_GROUPS, FN_GROUP_DIM)
    f = jnp.fft.fftn(ug, axes=(1, 3), norm='ortho').real.astype(h.dtype)
    y = jnp.einsum('blgc,gce->blge', f, w_group).reshape(B, L, D)
    return (y * jax.nn.silu(z)) @ w_out

def centred_shift(s):
    sp = jnp.pad(s, ((0, 0), (1, 1), (0, 0)))
    return 0.5 * (sp[:, :-2] + sp[:, 2:])

def rwkv7_features(h, w_in, mu, w0, w_up, a0, a_up, k_k, k_a):
    B, L, D = h.shape
    p = h @ w_in
    s, z = p[..., :-D], p[..., -D:]
    s = s + mu * (centred_shift(s) - s)
    r, k, v = s[..., :D], s[..., D:2 * D], s[..., 2 * D:3 * D]
    wd = s[..., 3 * D:3 * D + 2 * RW_DECAY_RANK].reshape(B, L, 2, RW_DECAY_RANK)
    ad = s[..., 3 * D + 2 * RW_DECAY_RANK:].reshape(B, L, 2, RW_ICLR_RANK)
    w_pre = (w0 + jnp.einsum('blzr,zrd->blzd', jnp.tanh(wd), w_up)).astype(jnp.float32)
    decay = jnp.exp(-jnp.exp(-jax.nn.softplus(-w_pre) - 0.5))
    a = jax.nn.sigmoid((a0 + jnp.einsum('blzr,zrd->blzd', ad, a_up)).astype(jnp.float32))
    kk = (k * k_k).astype(jnp.float32).reshape(B, L, RW_HEADS, RW_HEAD_DIM)
    kk = (kk * lax.rsqrt(jnp.sum(kk * kk, axis=-1, keepdims=True) + 1e-12)).reshape(B, L, D)
    k_dir = k.astype(jnp.float32)[:, :, None] * (1.0 + (a - 1.0) * k_a.astype(jnp.float32))
    b = kk[:, :, None] * a
    return r.astype(jnp.float32), v.astype(jnp.float32), z, decay, kk, k_dir, b

def to_scan_layout(t):
    B, L = t.shape[:2]
    t = jnp.stack([t[:, :, 0], jnp.flip(t[:, :, 1], axis=1)], axis=0)
    return t.transpose(2, 0, 1, 3).reshape(L, 2, B, RW_HEADS, RW_HEAD_DIM)

def wkv7_step(S, inp):
    r, w, k, v, a, b = inp
    sa = jnp.einsum('zbhij,zbhj->zbhi', S, a)
    S = S * w[..., None, :] + sa[..., :, None] * b[..., None, :] + v[..., :, None] * k[..., None, :]
    return S, jnp.einsum('zbhij,zbhj->zbhi', S, r)

def wkv7_bidirectional(S0, r, decay, k_dir, v, kk, b):
    both = lambda t: jnp.stack([t, t], axis=2)
    seqs = (to_scan_layout(both(r)), to_scan_layout(decay), to_scan_layout(k_dir),
            to_scan_layout(both(v)), to_scan_layout(both(-kk)), to_scan_layout(b))
    S, y = lax.scan(wkv7_step, S0, seqs)
    y = y[:, 0] + jnp.flip(y[:, 1], axis=0)
    return S, y.transpose(1, 0, 2, 3)

def rwkv7_output(y, r, k_dir, v, z, r_k, ln_w, ln_b, w_out):
    B, L = y.shape[:2]
    yc = y - jnp.mean(y, axis=-1, keepdims=True)
    yn = yc * lax.rsqrt(jnp.mean(yc * yc, axis=-1, keepdims=True) + RW_GN_EPS)
    yn = yn.reshape(B, L, D_MODEL) * ln_w.astype(jnp.float32) + ln_b.astype(jnp.float32)
    heads = lambda t: t.reshape(B, L, RW_HEADS, RW_HEAD_DIM)
    bonus = jnp.sum(heads(r * jnp.mean(k_dir, axis=2) * r_k.astype(jnp.float32)), axis=-1, keepdims=True) * heads(v)
    o = (yn + bonus.reshape(B, L, D_MODEL)).astype(z.dtype) * jax.nn.silu(z)
    return o @ w_out

def rwkv7_mix(h_lat, h_ctx, w_in, mu, w0, w_up, a0, a_up, k_k, k_a, r_k, ln_w, ln_b, w_out, need_ctx_out):
    B = h_lat.shape[0]
    r_c, v_c, z_c, dec_c, kk_c, kd_c, b_c = rwkv7_features(h_ctx, w_in, mu, w0, w_up, a0, a_up, k_k, k_a)
    r_l, v_l, z_l, dec_l, kk_l, kd_l, b_l = rwkv7_features(h_lat, w_in, mu, w0, w_up, a0, a_up, k_k, k_a)
    S0 = jnp.zeros((2, B, RW_HEADS, RW_HEAD_DIM, RW_HEAD_DIM), jnp.float32)
    S_c, y_c = wkv7_bidirectional(S0, r_c, dec_c, kd_c, v_c, kk_c, b_c)
    _, y_l = wkv7_bidirectional(S_c, r_l, dec_l, kd_l, v_l, kk_l, b_l)
    out_l = rwkv7_output(y_l, r_l, kd_l, v_l, z_l, r_k, ln_w, ln_b, w_out)
    out_c = rwkv7_output(y_c, r_c, kd_c, v_c, z_c, r_k, ln_w, ln_b, w_out) if need_ctx_out else None
    return out_l, out_c

def second_inputs(seed: int = 0) -> dict:
    key = jax.random.key(seed)
    ks = iter(jax.random.split(key, 32))
    D = D_MODEL
    R_ALL = 2 * RW_DECAY_RANK + 2 * RW_ICLR_RANK

    def nrm(shape, scale):
        return jax.random.normal(next(ks), shape, jnp.float32) * scale

    inputs = {}
    inputs['x'] = nrm((BATCH, SEQ, D), 1.0)
    inputs['c'] = nrm((BATCH, D), 1.0)
    inputs['ctx'] = nrm((BATCH, CTX_LEN, D), 1.0)
    inputs['c_ctx'] = nrm((D,), 1.0)
    inputs['norm_gain'] = 1.0 + nrm((DEPTH, D), 0.02)
    inputs['ada_w'] = nrm((DEPTH, D, 3 * D), 0.3 * D ** -0.5)
    inputs['ada_b'] = nrm((DEPTH, 3 * D), 0.02)
    inputs['final_gain'] = 1.0 + nrm((D,), 0.02)
    inputs['da_w_in'] = nrm((N_ATTN, D, 4 * D), D ** -0.5)
    inputs['da_lam_q'] = nrm((N_ATTN, 2, DA_HEAD_DIM), 0.1)
    inputs['da_lam_k'] = nrm((N_ATTN, 2, DA_HEAD_DIM), 0.1)
    inputs['da_subln_gain'] = 1.0 + nrm((N_ATTN, 2 * DA_HEAD_DIM), 0.02)
    inputs['da_w_out'] = nrm((N_ATTN, D, D), D ** -0.5)
    inputs['fn_w_in'] = nrm((N_FNET, D, 2 * D), D ** -0.5)
    inputs['fn_w_group'] = nrm((N_FNET, FN_GROUPS, FN_GROUP_DIM, FN_GROUP_DIM), FN_GROUP_DIM ** -0.5)
    inputs['fn_w_out'] = nrm((N_FNET, D, D), D ** -0.5)
    inputs['rw_w_in'] = nrm((N_RWKV, D, 4 * D + R_ALL), D ** -0.5)
    inputs['rw_mu'] = jax.random.uniform(next(ks), (N_RWKV, 3 * D + R_ALL), jnp.float32, 0.0, 1.0)
    inputs['rw_w0'] = jax.random.uniform(next(ks), (N_RWKV, 2, D), jnp.float32, -6.5, -1.5)
    inputs['rw_w_up'] = nrm((N_RWKV, 2, RW_DECAY_RANK, D), 0.1)
    inputs['rw_a0'] = nrm((N_RWKV, 2, D), 0.1)
    inputs['rw_a_up'] = nrm((N_RWKV, 2, RW_ICLR_RANK, D), RW_ICLR_RANK ** -0.5)
    inputs['rw_k_k'] = 0.85 + nrm((N_RWKV, D), 0.02)
    inputs['rw_k_a'] = 1.0 + nrm((N_RWKV, D), 0.02)
    inputs['rw_r_k'] = nrm((N_RWKV, D), 0.1)
    inputs['rw_ln_w'] = 1.0 + nrm((N_RWKV, D), 0.02)
    inputs['rw_ln_b'] = nrm((N_RWKV, D), 0.02)
    inputs['rw_w_out'] = nrm((N_RWKV, D, D), D ** -0.5)
    return inputs

def second_block(x, c, ctx, c_ctx, norm_gain, ada_w, ada_b, final_gain,
              da_w_in, da_lam_q, da_lam_k, da_subln_gain, da_w_out,
              fn_w_in, fn_w_group, fn_w_out,
              rw_w_in, rw_mu, rw_w0, rw_w_up, rw_a0, rw_a_up, rw_k_k, rw_k_a, rw_r_k,
              rw_ln_w, rw_ln_b, rw_w_out):
    cos, sin = axial_rope_tables(x.shape[1])
    x_lat, x_ctx = x, ctx
    for i in range(DEPTH):
        last = i == DEPTH - 1
        kind = i % N_MIXERS
        j = i // N_MIXERS
        sh, sc, gt = ada_modulation(c, ada_w[i], ada_b[i])
        sh_c, sc_c, gt_c = ada_modulation(c_ctx, ada_w[i], ada_b[i])
        h_lat = rms_norm(x_lat, norm_gain[i]) * (1.0 + sc[:, None, :]) + sh[:, None, :]
        h_ctx = rms_norm(x_ctx, norm_gain[i]) * (1.0 + sc_c) + sh_c
        if kind == 0:
            lambda_init = 0.8 - 0.6 * math.exp(-0.3 * i)
            y_lat, y_ctx = diff_attention(h_lat, h_ctx, cos, sin, da_w_in[j], da_lam_q[j], da_lam_k[j],
                                          da_subln_gain[j], da_w_out[j], lambda_init, not last)
        elif kind == 1:
            y_lat = fourier_mix(h_lat, fn_w_in[j], fn_w_group[j], fn_w_out[j])
            y_ctx = None if last else fourier_mix(h_ctx, fn_w_in[j], fn_w_group[j], fn_w_out[j])
        else:
            y_lat, y_ctx = rwkv7_mix(h_lat, h_ctx, rw_w_in[j], rw_mu[j], rw_w0[j], rw_w_up[j], rw_a0[j],
                                     rw_a_up[j], rw_k_k[j], rw_k_a[j], rw_r_k[j], rw_ln_w[j], rw_ln_b[j],
                                     rw_w_out[j], not last)
        x_lat = x_lat + gt[:, None, :] * y_lat
        if not last:
            x_ctx = x_ctx + gt_c * y_ctx
    return rms_norm(x_lat, final_gain)


def setup_inputs(seed=0):
    out = dict(first_inputs(seed))
    for name, value in second_inputs(seed + 1).items():
        if name != "x":
            out[name + "_2"] = value
    return out


def reference(
    x, ln1, w_in, w_pool, pool_scale, w_a_up, b_a, gla_gn, b_f, w_o, ln2, w_gu, w_down, ln_f,
    c_2, ctx_2, c_ctx_2, norm_gain_2, ada_w_2, ada_b_2, final_gain_2, da_w_in_2, da_lam_q_2,
    da_lam_k_2, da_subln_gain_2, da_w_out_2, fn_w_in_2, fn_w_group_2, fn_w_out_2, rw_w_in_2,
    rw_mu_2, rw_w0_2, rw_w_up_2, rw_a0_2, rw_a_up_2, rw_k_k_2, rw_k_a_2, rw_r_k_2, rw_ln_w_2,
    rw_ln_b_2, rw_w_out_2,
):
    x = first_block(
        x, ln1, w_in, w_pool, pool_scale, w_a_up, b_a, gla_gn, b_f, w_o, ln2, w_gu, w_down,
        ln_f,
    )
    return second_block(
        x, c_2, ctx_2, c_ctx_2, norm_gain_2, ada_w_2, ada_b_2, final_gain_2, da_w_in_2,
        da_lam_q_2, da_lam_k_2, da_subln_gain_2, da_w_out_2, fn_w_in_2, fn_w_group_2,
        fn_w_out_2, rw_w_in_2, rw_mu_2, rw_w0_2, rw_w_up_2, rw_a0_2, rw_a_up_2, rw_k_k_2,
        rw_k_a_2, rw_r_k_2, rw_ln_w_2, rw_ln_b_2, rw_w_out_2,
    )


_drawn_inputs = setup_inputs


def setup_inputs(seed=0):
    import zlib

    import numpy as np

    out = dict(_drawn_inputs(seed))
    spreads = {}
    factors = {'ln1': 3.414,
     'b_a': 3.943,
     'gla_gn': 8.0,
     'ln2': 4.226,
     'ln_f': 2.736,
     'ctx_2': 4.021,
     'c_ctx_2': 2.996,
     'norm_gain_2': 8.0,
     'ada_b_2': 3.912,
     'final_gain_2': 7.858,
     'da_lam_q_2': 8.0,
     'da_lam_k_2': 8.0,
     'da_subln_gain_2': 22.206}
    for name, (base, spread) in spreads.items():
        noise = np.random.default_rng([zlib.crc32(name.encode()), seed]).standard_normal(out[name].shape)
        drawn = base * np.exp(spread * noise) if base else spread * noise
        out[name] = jnp.asarray(drawn.astype(out[name].dtype))
    for name, factor in factors.items():
        out[name] = (out[name] * factor).astype(out[name].dtype)
    return out
```

```python
import math
from contextlib import ExitStack

import numpy as np

import concourse.bass as bass
from concourse import mybir

F32 = mybir.dt.float32
F32R = mybir.dt.float32r
U32 = mybir.dt.uint32
ACT = mybir.ActivationFunctionType
ALU = mybir.AluOpType
AX = mybir.AxisListType

P = 128
D = 1024
KT = D // P
SEQ = 1024
NT = SEQ // P
HALF = SEQ // 2
CTX = 256
NKEY = SEQ + CTX
NKT = NKEY // P
DH = 64
HEADS2 = 8
D_FF = 2816
FT = D_FF // P
CHUNK = 64
NCH = SEQ // CHUNK
EPS = 1e-6
SUB_EPS = 1e-5
LAMBDA_INIT = 0.8 - 0.6 * math.exp(-0.3 * 0)
NEG = -2.0 ** 120

C_LN1, C_LN2, C_NG, C_POOL, C_BA, C_GN, C_ADA, C_SUB, C_C, C_CC, C_BF = 0, 8, 16, 24, 26, 28, 30, 54, 55, 63, 71
NCOLS = 72
K_ID, K_BLK, K_NEG, K_INVC, K_INVW, K_SEL = 0, 128, 256, 384, 416, 418
NK = 426


class Steps:

    def __init__(self, eng, sem, per=0, i=0):
        self.eng, self.sem, self.base, self.n, self.per = eng, sem, i * per, 0, per

    def __call__(self, ins):
        self.n += 1
        ins.then_inc(self.sem, 1)
        self.eng.wait_ge(self.sem, self.base + self.n)

    def end(self):
        assert self.n == self.per, (self.n, self.per)


class Core:

    def __init__(self, nc, ctx, dram):
        self.nc, self.ctx, self.d, self.sems = nc, ctx, dram, []
        self.hh = self.sb("h_hi", [P, KT, SEQ], F32R)
        self.hl = self.sb("h_lo", [P, KT, SEQ], F32R)
        self.raw = self.sb("w_raw", [P, 2, D], F32)
        self.wh = self.sb("w_hi", [P, 2, D], F32R)
        self.wl = self.sb("w_lo", [P, 2, D], F32R)
        self.cols = self.sb("cols_sb", [P, NCOLS], F32)
        self.ident = self.sb("ident", [P, P], F32)
        self.mods = self.sb("mods", [P, 24, 2], F32)
        self.eps = self.sb("eps_col", [P, 2], F32)
        self.neglam = self.sb("neglam", [P, 1], F32)
        self.subg = self.sb("subg", [P, 1], F32)
        self.psum = ctx.enter_context(nc.psum_tensor("psum", [P, 8 * 512], F32))
        self.ps = [self.psum[:, i * 512:(i + 1) * 512] for i in range(8)]

    def sb(self, name, shape, dt):
        return self.ctx.enter_context(self.nc.sbuf_tensor(name, shape, dt))

    def sem(self, name):
        self.sems.append(self.nc.alloc_semaphore(name))
        return self.sems[-1]

    def clear_semaphores(self):
        self.nc.clear_and_free_semaphores(self.sems)
        self.sems = []
        self.nc.all_engine_barrier()


class Phase:

    def __init__(self, core, name):
        self.core, self.name, self.stack = core, name, ExitStack()

    def __enter__(self):
        self.stack.__enter__()
        return self

    def __exit__(self, *a):
        return self.stack.__exit__(*a)

    def sb(self, name, shape, dt):
        return self.stack.enter_context(self.core.nc.sbuf_tensor(f"{self.name}_{name}", shape, dt))

    def sem(self, name):
        return self.core.sem(f"{self.name}_{name}")


class Weights:

    def __init__(self, ph, core, bufs, last, pieces):
        self.core, self.bufs, self.last, self.pieces = core, bufs, last, pieces
        self.loaded = [ph.sem(f"w_loaded{b}") for b in range(2)]
        self.hi = [ph.sem(f"w_hi{b}") for b in range(2)]
        self.lo = [ph.sem(f"w_lo{b}") for b in range(2)]
        self.piece_done = ph.sem("piece_done")
        self.uses = [max(bufs.count(b), 1) for b in range(2)]

    def nth(self, i, c):
        b = self.bufs[c]
        return i * self.uses[b] + self.bufs[:c].count(b)

    def load(self, sync, i, c, src):
        b = self.bufs[c]
        sync.wait_ge(self.lo[b], self.nth(i, c) + 1)
        sync.dma_start(self.core.raw[:, b, :], src).then_inc(self.loaded[b], 16)

    def round_hi(self, act, i, c):
        b = self.bufs[c]
        act.wait_ge(self.loaded[b], self.nth(i, c) * 16 + 16)
        before = [x for x in range(c) if self.bufs[x] == b]
        if before:
            act.wait_ge(self.piece_done, (i + 1) * self.pieces + self.last[before[-1]] + 1)
        else:
            final = [x for x in range(len(self.bufs)) if self.bufs[x] == b][-1]
            act.wait_ge(self.piece_done, i * self.pieces + self.last[final] + 1)
        act.activation(self.core.wh[:, b, :], self.core.raw[:, b, :], ACT.Copy).then_inc(self.hi[b], 1)

    def start_lo(self, pool):
        for b in range(2):
            pool.sem_inc(self.lo[b], 1)

    def subtract_lo(self, pool, i, c):
        b = self.bufs[c]
        pool.wait_ge(self.hi[b], self.nth(i, c) + 1)
        pool.tensor_tensor(self.core.wl[:, b, :], self.core.raw[:, b, :], self.core.wh[:, b, :].bitcast(F32),
                           ALU.subtract).then_inc(self.lo[b], 1)

    def start_pieces(self, pe):
        pe.sem_inc(self.piece_done, self.pieces)

    def wait_tile(self, pe, i, c):
        b = self.bufs[c]
        pe.wait_ge(self.lo[b], self.nth(i, c) + 2)

    def piece(self, pe, c, out, hi, lo, at, n):
        b = self.bufs[c]
        for k in range(KT):
            wh, wl = self.core.wh[:, b, k * P:(k + 1) * P], self.core.wl[:, b, k * P:(k + 1) * P]
            rh, rl = hi[:, k, at:at + n], lo[:, k, at:at + n]
            pe.matmul(out, wh, rh, start=(k == 0), stop=False)
            pe.matmul(out, wh, rl, start=False, stop=False)
            last = pe.matmul(out, wl, rh, start=False, stop=(k == KT - 1))
        last.then_inc(self.piece_done, 1)

    def done(self, i, p):
        return (i + 1) * self.pieces + p + 1


class Transposes:

    def __init__(self, ph, core, y, hi, lo, groups, width, gain, bias=None):
        self.core, self.y, self.hi_t, self.lo_t = core, y, hi, lo
        self.groups, self.width, self.gain, self.bias = groups, width, gain, bias
        self.ready = ph.sem("y_ready")
        self.turned = ph.sem("h_turned")
        self.hi = ph.sem("h_hi")
        self.lo = ph.sem("h_lo")
        self.tmp_done = ph.sem("h_tmp")
        self.tmp = ph.sb("h_tmp", [P, 2, width * P], F32) if bias else None

    def pe(self, pe, g):
        pe.wait_ge(self.ready, g + 1)
        for k in range(KT):
            n = g * KT + k
            if n >= 4:
                pe.wait_ge(self.lo, n - 3)
            for t in range(self.width):
                last = pe.transpose(self.core.ps[n % 4][:, t * P:(t + 1) * P],
                                    self.y[:, g * self.width + t, k * P:(k + 1) * P], self.core.ident[:, :])
            last.then_inc(self.turned, 1)

    def act(self, act, g):
        w = self.width * P
        for k in range(KT):
            n = g * KT + k
            act.wait_ge(self.turned, n + 1)
            act.activation(self.hi_t[:, k, g * w:(g + 1) * w], self.core.ps[n % 4][:, 0:w], ACT.Identity,
                           scale=self.gain(k), bias=self.bias(k) if self.bias else 0.0).then_inc(self.hi, 1)

    def dve(self, dve, g):
        w = self.width * P
        for k in range(KT):
            n = g * KT + k
            dve.wait_ge(self.hi, n + 1)
            src, hi, lo = self.core.ps[n % 4][:, 0:w], self.hi_t[:, k, g * w:(g + 1) * w], self.lo_t[:, k, g * w:(g + 1) * w]
            if self.bias:
                if n >= 2:
                    dve.wait_ge(self.lo, n - 1)
                dve.tensor_scalar(self.tmp[:, n % 2, :], src, self.gain(k), self.bias(k), ALU.mult, ALU.add)\
                   .then_inc(self.tmp_done, 1)
                dve.wait_ge(self.tmp_done, n + 1)
                dve.tensor_tensor(lo, self.tmp[:, n % 2, :], hi.bitcast(F32), ALU.subtract).then_inc(self.lo, 1)
            else:
                dve.scalar_tensor_tensor(lo, src, self.gain(k), hi.bitcast(F32), ALU.mult, ALU.subtract)\
                   .then_inc(self.lo, 1)


def modulation(core):
    nc, d = core.nc, core.d
    with Phase(core, "mod") as ph:
        cs = ph.sb("silu_c", [P, KT, 2], F32)
        lamr = ph.sb("lam_rows", [P, 4, DH], F32)
        lam = ph.sb("lam", [P, 8], F32)
        s_in, s_c, s_lam, s_lamsum, s_lamexp = (ph.sem(n) for n in ("in", "silu", "lam", "lam_sums", "lam_exp"))
        s_loaded = [ph.sem(f"loaded{b}") for b in range(2)]
        s_mm, s_ev, s_step, s_ready = ph.sem("mm"), ph.sem("read"), ph.sem("step"), ph.sem("ready")
        with nc.Block() as block:
            @block.sync
            def _(sync):
                sync.dma_start(core.cols[:, :], d["cols"]).then_inc(s_in, 16)
                sync.dma_start(core.ident[:, :], d["shape_consts"][:, K_ID:K_ID + P]).then_inc(s_in, 16)
                sync.dma_start(lamr[:, :, :], d["lam_rows"].partition_broadcast(P)).then_inc(s_in, 16)
                with sync.Fori(0, 12) as i:
                    for b in range(2):
                        sync.wait_ge(s_mm, i * 2 + b + 1)
                        sync.dma_start(core.raw[:, b, :], d["ada_w"][2 * i + b, :, :]).then_inc(s_loaded[b], 16)

            @block.scalar
            def _(act):
                act.wait_ge(s_in, 48)
                act.activation(cs[:, :, 0], core.cols[:, C_C:C_C + KT], ACT.Silu).then_inc(s_c, 1)
                act.activation(cs[:, :, 1], core.cols[:, C_CC:C_CC + KT], ACT.Silu).then_inc(s_c, 1)
                act.wait_ge(s_lamsum, 1)
                act.activation(lam[:, 2:4], lam[:, 0:2], ACT.Exp).then_inc(s_lamexp, 1)

            @block.tensor
            def _(pe):
                pe.wait_ge(s_c, 2)
                pe.sem_inc(s_mm, 2)
                with pe.Fori(0, 12) as i:
                    for b in range(2):
                        pe.wait_ge(s_loaded[b], i * 16 + 16)
                        pe.wait_ge(s_ev, i * 2 + b + 1)
                        for k in range(KT):
                            last = pe.matmul(core.ps[b][:, 0:2], core.raw[:, b, k * P:(k + 1) * P], cs[:, k, :],
                                             start=(k == 0), stop=(k == KT - 1))
                        last.then_inc(s_mm, 1)

            @block.vector
            def _(dve):
                step = Steps(dve, s_step)
                dve.sem_inc(s_ev, 2)
                dve.memset(core.eps[:, 0:1], EPS)
                step(dve.memset(core.eps[:, 1:2], SUB_EPS))
                dve.wait_ge(s_in, 48)
                step(dve.tensor_tensor(lamr[:, 0:2, :], lamr[:, 0:2, :], lamr[:, 2:4, :], ALU.mult))
                dve.tensor_reduce(lam[:, 0:2], lamr[:, 0:2, :], AX.X, ALU.add).then_inc(s_lamsum, 1)
                dve.wait_ge(s_lamexp, 1)
                step(dve.tensor_tensor(lam[:, 4:5], lam[:, 3:4], lam[:, 2:3], ALU.subtract))
                step(dve.tensor_scalar(core.neglam[:, :], lam[:, 4:5], -LAMBDA_INIT, None, ALU.add))
                step(dve.tensor_scalar(core.subg[:, :], core.cols[:, C_SUB:C_SUB + 1], 1.0 - LAMBDA_INIT, None, ALU.mult))
                with dve.Fori(0, 12) as i:
                    for b in range(2):
                        dve.wait_ge(s_mm, i * 2 + b + 3)
                        dve.tensor_copy(core.mods[:, 2 * i + b, :], core.ps[b][:, 0:2]).then_inc(s_ev, 1)
                dve.wait_ge(s_ev, 26)
                for j in range(2):
                    last = dve.tensor_tensor(core.mods[:, :, j], core.mods[:, :, j], core.cols[:, C_ADA:C_ADA + 24], ALU.add)
                step(last)
                for j in range(2):
                    last = dve.scalar_tensor_tensor(core.mods[:, 8:16, j], core.mods[:, 8:16, j], 1.0,
                                                    core.cols[:, C_NG:C_NG + KT], ALU.add, ALU.mult)
                step(last)


def norm_of_input(core):
    nc, d = core.nc, core.d
    with Phase(core, "in") as ph:
        y = ph.sb("y", [P, NT, D], F32)
        sq = ph.sb("sq", [P, D], F32)
        ss = ph.sb("ss", [P, NT], F32)
        s_x = [ph.sem(f"x{t}") for t in range(NT)]
        s_ss, s_ms, s_rt, s_step = ph.sem("squares"), ph.sem("means"), ph.sem("roots"), ph.sem("step")
        tr = Transposes(ph, core, y, core.hh, core.hl, 2, 4, lambda k: core.cols[:, C_LN1 + k:C_LN1 + k + 1])
        with nc.Block() as block:
            @block.sync
            def _(sync):
                for t in range(NT):
                    sync.dma_start(y[:, t, :], d["x"][t, :, :]).then_inc(s_x[t], 16)

            @block.scalar
            def _(act):
                for g in range(2):
                    for t in range(4 * g, 4 * g + 4):
                        act.wait_ge(s_x[t], 16)
                        act.activation(sq[:, :], y[:, t, :], ACT.Square, accum_out=ss[:, t:t + 1]).then_inc(s_ss, 1)
                        act.wait_ge(s_ss, t + 1)
                for g in range(2):
                    act.wait_ge(s_ms, g + 1)
                    act.activation(ss[:, 4 * g:4 * g + 4], ss[:, 4 * g:4 * g + 4], ACT.Sqrt).then_inc(s_rt, 1)
                    tr.act(act, g)

            @block.vector
            def _(dve):
                step = Steps(dve, s_step)
                for g in range(2):
                    c = slice(4 * g, 4 * g + 4)
                    dve.wait_ge(s_ss, 4 * g + 4)
                    dve.tensor_scalar(ss[:, c], ss[:, c], 1.0 / D, EPS, ALU.mult, ALU.add).then_inc(s_ms, 1)
                    dve.wait_ge(s_rt, g + 1)
                    step(dve.reciprocal(ss[:, c], ss[:, c]))
                    for t in range(4 * g, 4 * g + 4):
                        last = dve.tensor_scalar(y[:, t, :], y[:, t, :], ss[:, t:t + 1], None, ALU.mult)
                    last.then_inc(tr.ready, 1)
                    tr.dve(dve, g)

            @block.tensor
            def _(pe):
                for g in range(2):
                    tr.pe(pe, g)


def gates_and_pool(core, mix, la, tbase, rf):
    nc, d, ps = core.nc, core.d, core.ps
    with Phase(core, "gate") as ph:
        gaf = ph.sb("gaf", [P, SEQ], F32)
        u = ph.sb("u", [P, 2, SEQ], F32)
        pa = ph.sb("pool_a", [P, SEQ], F32)
        pb = ph.sb("pool_b", [P, SEQ], F32)
        wp = ph.sb("w_pool", [P, 2, P], F32)
        wa = ph.sb("w_a_up", [16, 2 * P], F32)
        kc = ph.sb("kc", [P, 34], F32)
        ab = ph.sb("abs", [P, HALF], F32)
        fl = ph.sb("logf", [P, 2, SEQ], F32)
        one = ph.sb("one", [P, SEQ], F32)
        ws = Weights(ph, core, [0, 1, 0], [1, 3, 5], 6)
        s_c, s_gaf, s_u, s_pool = ph.sem("consts"), ph.sem("gaf_copied"), ph.sem("u_copied"), ph.sem("pool_step")
        s_pooled, s_pm, s_pev = ph.sem("pooled"), ph.sem("pool_mm"), ph.sem("pool_out")
        s_lm, s_lact, s_ldve = ph.sem("la_mm"), ph.sem("la_act"), ph.sem("la_dve")
        s_f, s_fact = ph.sem("f_step"), ph.sem("f_act")
        with nc.Block() as block:
            @block.sync
            def _(sync):
                for c in range(3):
                    ws.load(sync, 0, c, d["w_in"][c, :, :])
                    if c == 1:
                        sync.dma_start(wp[:, :, :], d["w_pool"]).then_inc(s_c, 16)
                        sync.dma_start(wa[:, :], d["w_a_up"]).then_inc(s_c, 16)
                        sync.dma_start(kc[:, :], d["shape_consts"][:, K_INVC:K_INVC + 34]).then_inc(s_c, 16)

            @block.scalar
            def _(act):
                ws.round_hi(act, 0, 0)
                ws.round_hi(act, 0, 1)
                for p in range(2):
                    act.wait_ge(ws.piece_done, ws.done(0, p))
                    act.activation(gaf[:, p * HALF:(p + 1) * HALF], ps[6 + p % 2][:, :], ACT.Copy).then_inc(s_gaf, 1)
                ws.round_hi(act, 0, 2)
                for n, (func, scale, bias) in enumerate(((ACT.Abs, 1.0, core.cols[32:40, C_BF:C_BF + 1]),
                                                         (ACT.Exp, -1.0, 0.0), (ACT.Ln, 1.0, 1.0))):
                    act.wait_ge(s_gaf, 2) if n == 0 else act.wait_ge(s_fact, n)
                    act.activation(fl[32:40, 0, :], gaf[32:40, :] if n == 0 else fl[32:40, 0, :], func,
                                   bias=bias, scale=scale).then_inc(s_fact, 1)
                for p in range(2, 6):
                    act.wait_ge(ws.piece_done, ws.done(0, p))
                    act.activation(u[:, (p - 2) // 2, (p % 2) * HALF:(p % 2 + 1) * HALF], ps[6 + p % 2][:, :],
                                   ACT.Copy).then_inc(s_u, 1)
                for n in range(4):
                    pr, hf = n // 2, n % 2
                    act.wait_ge(s_lm, n + 1)
                    if n:
                        act.wait_ge(s_ldve, 2 * n)
                    for m, (func, scale, bias) in enumerate(((ACT.Abs, 1.0, core.cols[:, C_BA + pr:C_BA + pr + 1]),
                                                             (ACT.Exp, -1.0, 0.0), (ACT.Ln, 1.0, 1.0))):
                        act.activation(ab[:, :], ps[n][:, :] if m == 0 else ab[:, :], func, bias=bias, scale=scale)\
                           .then_inc(s_lact, 1)
                        act.wait_ge(s_lact, 3 * n + m + 1)
                for n in range(4):
                    c, hf = n // 2, n % 2
                    act.wait_ge(s_pm, n + 1)
                    act.activation(mix[:, c, hf * HALF:(hf + 1) * HALF], ps[4 + n % 2][:, :], ACT.Copy,
                                   scale=core.cols[:, C_POOL + c:C_POOL + c + 1]).then_inc(s_pev, 1)

            @block.vector
            def _(dve):
                f = Steps(dve, s_f)
                dve.memset(one[:, :], 1.0)
                dve.memset(tbase[:, :], 0.0)
                f(dve.memset(rf[:, :].bitcast(F32), 0.0))
                for q in (0, 64):
                    dve.memset(tbase[q:q + 8, :], 1.0)
                    last = dve.memset(rf[q + 32:q + 40, :].bitcast(F32), 1.0)
                f(last)
                dve.wait_ge(s_gaf, 2)
                f(dve.tensor_scalar(fl[32:40, 1, :], gaf[32:40, :], core.cols[32:40, C_BF:C_BF + 1], 0.0, ALU.add, ALU.min))
                dve.wait_ge(s_fact, 3)
                f(dve.tensor_tensor(fl[32:40, 1, :], fl[32:40, 1, :], fl[32:40, 0, :], ALU.subtract))
                f(dve.tensor_tensor_scan(fl[32:40, 0, :], one[32:40, :], fl[32:40, 1, :], 0.0, ALU.mult, ALU.add))
                f(dve.tensor_scalar(rf[0:8, :], fl[32:40, 0, :], -1.0, None, ALU.mult))
                f(dve.tensor_scalar(tbase[32:40, :], rf[0:8, :].bitcast(F32), -1.0, None, ALU.mult))
                f(dve.tensor_tensor(tbase[96:104, :], fl[32:40, 0, :], tbase[32:40, :], ALU.subtract))
                f(dve.tensor_scalar(rf[64:72, :], tbase[96:104, :], -1.0, None, ALU.mult))
                for n in range(4):
                    pr, hf = n // 2, n % 2
                    dst = la[:, pr, hf * HALF:(hf + 1) * HALF]
                    dve.wait_ge(s_lact, 3 * n + 3)
                    dve.tensor_scalar(dst, ps[n][:, :], core.cols[:, C_BA + pr:C_BA + pr + 1], 0.0, ALU.add, ALU.min)\
                       .then_inc(s_ldve, 1)
                    dve.wait_ge(s_ldve, 2 * n + 1)
                    dve.tensor_tensor(dst, dst, ab[:, :], ALU.subtract).then_inc(s_ldve, 1)

            @block.gpsimd
            def _(pool):
                ws.start_lo(pool)
                for c in range(3):
                    ws.subtract_lo(pool, 0, c)
                step = Steps(pool, s_pool)
                pool.wait_ge(s_c, 48)
                for c in range(2):
                    pool.wait_ge(s_u, 2 * c + 2)
                    src = u[:, c, :]
                    spans = ((1, 0), (2, 64)) if c == 0 else ((1, 0), (2, 0), (4, 0), (8, 64))
                    bufs = (pa, pb)
                    for n, (lag, q) in enumerate(spans):
                        dst = bufs[n % 2]
                        pool.tensor_copy(dst[q:P, 0:lag], src[q:P, 0:lag])
                        if q:
                            pool.tensor_copy(dst[0:q, :], src[0:q, :])
                        step(pool.tensor_tensor(dst[q:P, lag:SEQ], src[q:P, lag:SEQ], src[q:P, 0:SEQ - lag], ALU.add))
                        src = dst
                    dst = bufs[len(spans) % 2]
                    pool.tensor_tensor(dst[:, 0:16], src[:, 0:16], kc[:, 16 * c:16 * c + 16], ALU.mult)
                    step(pool.tensor_scalar(dst[:, 16:SEQ], src[:, 16:SEQ], kc[:, 32 + c:33 + c], 1.0, ALU.mult, ALU.mult))
                    step(pool.tensor_tensor(u[:, c, :], dst[:, :], u[:, c, :], ALU.subtract))
                    pool.sem_inc(s_pooled, 1)

            @block.tensor
            def _(pe):
                ws.start_pieces(pe)
                for p in range(6):
                    if p % 2 == 0:
                        ws.wait_tile(pe, 0, p // 2)
                    if p in (2, 3):
                        pe.wait_ge(s_gaf, p - 1)
                    if p in (4, 5):
                        pe.wait_ge(s_u, p - 3)
                    ws.piece(pe, p // 2, ps[6 + p % 2][:, :], core.hh, core.hl, (p % 2) * HALF, HALF)
                pe.wait_ge(s_c, 48)
                pe.wait_ge(s_gaf, 2)
                for n in range(4):
                    pr, hf = n // 2, n % 2
                    pe.matmul(ps[n][:, :], wa[:, pr * P:(pr + 1) * P], gaf[0:16, hf * HALF:(hf + 1) * HALF],
                              start=True, stop=True).then_inc(s_lm, 1)
                for n in range(4):
                    c, hf = n // 2, n % 2
                    pe.wait_ge(s_pooled, c + 1)
                    if n >= 2:
                        pe.wait_ge(s_pev, n - 1)
                    pe.matmul(ps[4 + n % 2][:, :], wp[:, c, :], u[:, c, hf * HALF:(hf + 1) * HALF],
                              start=True, stop=True).then_inc(s_pm, 1)


def linear_attention(core, mix, la):
    nc, d, ps = core.nc, core.d, core.ps
    with Phase(core, "gla") as ph:
        qkvg = ph.sb("qkvg", [P, 2, 4, SEQ], F32)
        e = ph.sb("exps", [P, SEQ], F32)
        qi = ph.sb("q_in", [P, SEQ], F32)
        qx = ph.sb("q_x", [P, SEQ], F32)
        ki = ph.sb("k_in", [P, SEQ], F32)
        kd = ph.sb("k_dec", [P, SEQ], F32)
        kdt = ph.sb("k_dec_tok", [P, NT, P], F32)
        vt = ph.sb("v_tok", [P, NT, P], F32)
        att = ph.sb("att", [P, 2, NT, P], F32)
        dec = ph.sb("dec", [P, NCH], F32)
        blk = ph.sb("blk", [P, P], F32)
        msk = ph.sb("mask", [P, 512], U32)
        ob, sq = qi, qx
        reset = e
        state = lambda pr: chunks(la[:, pr, :])
        ws = Weights(ph, core, [0, 1] * 4, [2 * c + 1 for c in range(8)], 16)
        s_c, s_ev, s_att0 = ph.sem("consts"), ph.sem("copied"), ph.sem("att_zeroed")
        s_dve, s_exp, s_tm, s_tev = ph.sem("dve_step"), ph.sem("exps"), ph.sem("turned"), ph.sem("turned_copied")
        s_arg, s_prod = ph.sem("exp_args"), ph.sem("products")
        s_am, s_aev, s_kv, s_st = ph.sem("att_mm"), ph.sem("att_masked"), ph.sem("kv_mm"), ph.sem("state_step")
        s_om, s_oev, s_sm, s_rs, s_y = ph.sem("o_mm"), ph.sem("o_act"), ph.sem("squares_mm"), ph.sem("rstd"), ph.sem("y_step")
        chunks = lambda ap: ap.rearrange("p (n c) -> p n c", c=CHUNK)
        with nc.Block() as block:
            @block.sync
            def _(sync):
                sync.dma_start(blk[:, :], d["shape_consts"][:, K_BLK:K_BLK + P]).then_inc(s_c, 16)
                sync.dma_start(msk[:, :], d["gla_mask"]).then_inc(s_c, 16)
                for c in range(8):
                    ws.load(sync, 0, c, d["w_in"][3 + c, :, :])

            @block.scalar
            def _(act):
                def copies(c):
                    for hf in range(2):
                        p = 2 * c + hf
                        act.wait_ge(ws.piece_done, ws.done(0, p))
                        act.activation(qkvg[:, c // 4, c % 4, hf * HALF:(hf + 1) * HALF], ps[6 + p % 2][:, :],
                                       ACT.Silu if c % 4 == 3 else ACT.Copy).then_inc(s_ev, 1)

                def exps(pr):
                    bc = la[:, pr, :]
                    for n, (src, scale) in enumerate(((e, 1.0), (e, -1.0), (e, 1.0), (bc, 1.0))):
                        if n < 3:
                            act.wait_ge(s_arg, 4 * pr + n + 1)
                        else:
                            act.wait_ge(s_prod, pr + 1)
                        dst = kd if n < 2 else e
                        act.wait_ge(s_exp, 5 * pr + n) if 5 * pr + n else None
                        act.activation(dst[:, :], src[:, :] if n < 3 else bc, ACT.Exp, scale=scale / 16.0).then_inc(s_exp, 1)
                    act.activation(dec[:, :], chunks(bc)[:, :, CHUNK - 1], ACT.Exp, scale=1.0 / 16.0).then_inc(s_exp, 1)

                def finish(pr):
                    for n in range(2):
                        act.wait_ge(s_om, 2 * pr + n + 1)
                        s = slice(n * HALF, (n + 1) * HALF)
                        act.activation(ob[:, s], ps[6 + n][:, :], ACT.Copy).then_inc(s_oev, 1)
                        act.activation(sq[:, s], ps[6 + n][:, :], ACT.Square).then_inc(s_oev, 1)
                    for n in range(2):
                        s = slice(n * HALF, (n + 1) * HALF)
                        act.wait_ge(s_sm, 2 * pr + n + 1)
                        act.activation(e[:, s], ps[4 + n][:, :], ACT.Ln, scale=1.0 / DH, bias=core.eps[:, 0:1]).then_inc(s_rs, 1)
                        act.wait_ge(s_rs, 4 * pr + 2 * n + 1)
                        act.activation(e[:, s], e[:, s], ACT.Exp, scale=-0.5).then_inc(s_rs, 1)

                act.wait_ge(s_c, 32)
                for c in range(8):
                    ws.round_hi(act, 0, c)
                    if c:
                        copies(c - 1)
                copies(7)
                for pr in range(2):
                    exps(pr)
                    finish(pr)

            @block.gpsimd
            def _(pool):
                ws.start_lo(pool)
                pool.memset(att[:, :, :, :], 0.0).then_inc(s_att0, 1)
                for c in range(8):
                    ws.subtract_lo(pool, 0, c)

            @block.vector
            def _(dve):
                step = Steps(dve, s_dve)
                step(dve.memset(reset[:, :], 1.0))
                step(dve.memset(chunks(reset[:, :])[:, :, 0:1], 0.0))
                for pr in range(2):
                    step(dve.tensor_tensor_scan(la[:, pr, :], reset[:, :], la[:, pr, :], 0.0, ALU.mult, ALU.add))
                for pr in range(2):
                    bc = la[:, pr, :]
                    q, k = qkvg[:, pr, 0, :], qkvg[:, pr, 1, :]
                    at = lambda col: chunks(bc)[:, :, col:col + 1].to_broadcast([P, NCH, CHUNK])
                    dve.tensor_tensor(chunks(e[:, :]), chunks(bc), at(CHUNK // 2 - 1), ALU.subtract).then_inc(s_arg, 1)
                    dve.wait_ge(s_ev, 8 * pr + 4)
                    dve.wait_ge(s_exp, 5 * pr + 1)
                    dve.scalar_tensor_tensor(qi[:, :], q, DH ** -0.5, kd[:, :], ALU.mult, ALU.mult).then_inc(s_arg, 1)
                    dve.wait_ge(s_exp, 5 * pr + 2)
                    step(dve.tensor_tensor(ki[:, :], k, kd[:, :], ALU.mult))
                    dve.tensor_tensor(chunks(e[:, :]), at(CHUNK - 1), chunks(bc), ALU.subtract).then_inc(s_arg, 1)
                    dve.wait_ge(s_exp, 5 * pr + 3)
                    dve.tensor_tensor(kd[:, :], k, e[:, :], ALU.mult).then_inc(s_prod, 1)
                    dve.wait_ge(s_exp, 5 * pr + 4)
                    dve.scalar_tensor_tensor(qx[:, :], q, DH ** -0.5, e[:, :], ALU.mult, ALU.mult).then_inc(s_arg, 1)
                    dve.wait_ge(s_att0, 1)
                    for n in range(4):
                        dve.wait_ge(s_tm, 4 * pr + n + 1)
                        dst = (kdt, vt)[n // 2][:, (n % 2) * 4:(n % 2) * 4 + 4, :]
                        dve.tensor_copy(dst, ps[n][:, :].rearrange("p (t m) -> p t m", t=4)).then_inc(s_tev, 1)
                    for n in range(4):
                        dve.wait_ge(s_am, 4 * pr + n + 1)
                        dve.copy_predicated(att[:, n // 2, (n % 2) * 4:(n % 2) * 4 + 4, :].rearrange("p t m -> p (t m)"),
                                            msk[:, :], ps[n][:, :]).then_inc(s_aev, 1)
                    dve.wait_ge(s_exp, 5 * pr + 5)
                    st = state(pr)
                    step(dve.memset(st[:, 0, :], 0.0))
                    for n in range(NCH - 1):
                        if n % 8 == 0:
                            dve.wait_ge(s_kv, 4 * pr + n // 4 + 2)
                        bank, c0 = ps[2 * (n // 8) + n % 2], n % 8 // 2 * P
                        for h in range(2):
                            r = slice(h * DH, (h + 1) * DH)
                            last = dve.scalar_tensor_tensor(
                                st[r, n + 1, :], st[r, n, :], dec[r, n:n + 1],
                                bank[r, c0 + h * DH:c0 + (h + 1) * DH], ALU.mult, ALU.add)
                        last.then_inc(s_st, 1)
                        dve.wait_ge(s_st, 15 * pr + n + 1)
                    for n in range(2):
                        s = slice(n * HALF, (n + 1) * HALF)
                        y = mix[:, 2 + pr, s]
                        dve.wait_ge(s_rs, 4 * pr + 2 * n + 2)
                        dve.scalar_tensor_tensor(y, ob[:, s], core.cols[:, C_GN + pr:C_GN + pr + 1], e[:, s],
                                                 ALU.mult, ALU.mult).then_inc(s_y, 1)
                        dve.wait_ge(s_y, 4 * pr + 2 * n + 1)
                        dve.tensor_tensor(y, y, qkvg[:, pr, 3, s], ALU.mult).then_inc(s_y, 1)
                        dve.wait_ge(s_y, 4 * pr + 2 * n + 2)

            @block.tensor
            def _(pe):
                ws.start_pieces(pe)
                for p in range(16):
                    if p % 2 == 0:
                        ws.wait_tile(pe, 0, p // 2)
                    if p >= 2:
                        pe.wait_ge(s_ev, p - 1)
                    ws.piece(pe, p // 2, ps[6 + p % 2][:, :], core.hh, core.hl, (p % 2) * HALF, HALF)
                for pr in range(2):
                    if pr == 0:
                        pe.wait_ge(s_ev, 16)
                    pe.wait_ge(s_prod, pr + 1)
                    if pr:
                        pe.wait_ge(s_st, 15)
                    for n in range(4):
                        src = kd[:, :] if n < 2 else qkvg[:, pr, 2, :]
                        for t in range(4):
                            at = ((n % 2) * 4 + t) * P
                            last = pe.transpose(ps[n][:, t * P:(t + 1) * P], src[:, at:at + P], core.ident[:, :])
                        last.then_inc(s_tm, 1)
                    pe.wait_ge(s_arg, 4 * pr + 4)
                    for n in range(4):
                        pe.wait_ge(s_tev, 4 * pr + n + 1)
                        r = slice((n // 2) * DH, (n // 2 + 1) * DH)
                        for t in range(4):
                            at = ((n % 2) * 4 + t) * P
                            last = pe.matmul(ps[n][:, t * P:(t + 1) * P], ki[r, at:at + P], qi[r, at:at + P],
                                             start=True, stop=True)
                        last.then_inc(s_am, 1)
                    for n in range(4):
                        pe.wait_ge(s_aev, 4 * pr + n + 1)
                        for c in range(4):
                            ch = 8 * (n // 2) + 2 * c + n % 2
                            r = slice((ch % 2) * CHUNK, (ch % 2 + 1) * CHUNK)
                            last = pe.matmul(ps[n][:, c * P:(c + 1) * P], kdt[r, ch // 2, :], vt[r, ch // 2, :],
                                             start=True, stop=True)
                        last.then_inc(s_kv, 1)
                    if pr:
                        pe.wait_ge(s_rs, 4)
                    st = state(pr)
                    for hf in range(2):
                        pe.wait_ge(s_st, 15 * pr + 7 + 8 * hf)
                        for h in range(2):
                            r = slice(h * DH, (h + 1) * DH)
                            for t in range(4 * hf, 4 * hf + 4):
                                o = ps[6 + hf][r, (t % 4) * P:(t % 4 + 1) * P]
                                pe.matmul(o, vt[:, t, r], att[:, h, t, :], start=True, stop=False)
                                for c in range(2):
                                    ch = 2 * t + c
                                    last = pe.matmul(ps[6 + hf][r, (ch % 8) * CHUNK:(ch % 8 + 1) * CHUNK], st[r, ch, :],
                                                     qx[r, ch * CHUNK:(ch + 1) * CHUNK], start=False, stop=(c == 1))
                        last.then_inc(s_om, 1)
                    for n in range(2):
                        pe.wait_ge(s_oev, 4 * pr + 2 * n + 2)
                        pe.matmul(ps[4 + n][:, :], blk[:, :], sq[:, n * HALF:(n + 1) * HALF], start=True, stop=True)\
                          .then_inc(s_sm, 1)


def forgetting_attention(core, mix, tbase, rf):
    nc, d, ps = core.nc, core.d, core.ps
    PAIRS, UNITS = 4, 16
    with Phase(core, "fox") as ph:
        q = [ph.sb(n, [P, SEQ], F32R) for n in ("q_hi", "q_lo")]
        k = [ph.sb(n, [P, SEQ], F32R) for n in ("k_hi", "k_lo")]
        v = [ph.sb(n, [P, NT, P], F32R) for n in ("v_hi", "v_lo")]
        vT = ph.sb("v_feat", [P, SEQ], F32)
        th = ph.sb("f_rows", [P, SEQ], F32R)
        pe_s = ph.sb("p_small", [P, 4, HALF], F32)
        pe_l = ph.sb("p_large", [P, 4, SEQ], F32)
        pt = [ph.sb(n, [P, 2, HALF], F32R) for n in ("pt_hi", "pt_lo")]
        sel = ph.sb("sel", [P, 8, 1], F32)
        idr = ph.sb("ident_r", [P, P], F32R)
        ngr = ph.sb("causal_r", [P, P], F32R)
        cst = ph.sb("causal", [P, P], F32)
        nm = ph.sb("neg_max", [P, 2], F32)
        rs = ph.sb("row_sum", [P, 2], F32)
        ws = Weights(ph, core, [0, 1, 0], [1, 3, 5], 6)
        names = ("consts consts_r q_hi k_hi q_done k_done v_copied v_turned v_hi v_done f_rows scored maxed probs recips scaled "
                 "pt_turned pt_hi pt_lo pv_done o_read")
        s = {n: ph.sem(n) for n in names.split()}
        nkt = (4, 8)
        nth_pt = lambda i, h, g, kt: i * 24 + h * 12 + g * 4 + kt
        def slot(qb):
            return pe_s[:, qb, :] if qb < 4 else pe_l[:, qb - 4, :]
        with nc.Block() as block:
            @block.sync
            def _(sync):
                sync.dma_start(sel[:, :, 0], d["shape_consts"][:, K_SEL:K_SEL + 8]).then_inc(s["consts"], 16)
                sync.dma_start(cst[:, :], d["shape_consts"][:, K_NEG:K_NEG + P]).then_inc(s["consts"], 16)
                with sync.Fori(0, PAIRS) as i:
                    for c in range(3):
                        ws.load(sync, i, c, d["w_in"][11 + 3 * i + c, :, :])

            @block.gpsimd
            def _(pool):
                ws.start_lo(pool)
                pool.sem_inc(s["scaled"], 2)
                with pool.Fori(0, PAIRS) as i:
                    for c in range(3):
                        ws.subtract_lo(pool, i, c)
                    for h in range(2):
                        for qb in range(8):
                            u = i * UNITS + h * 8 + qb
                            n = (qb + 1) * P
                            pool.wait_ge(s["recips"], u + 1)
                            pool.nop(nofuse=True)
                            pool.tensor_scalar(slot(qb)[:, 0:n], slot(qb)[:, 0:n], rs[:, qb % 2:qb % 2 + 1], 1.0,
                                               ALU.mult, ALU.mult).then_inc(s["scaled"], 1)

            @block.scalar
            def _(act):
                act.sem_inc(s["probs"], 2)
                act.wait_ge(s["consts"], 32)
                act.activation(idr[:, :], core.ident[:, :], ACT.Copy)
                act.activation(ngr[:, :], cst[:, :], ACT.Copy).then_inc(s["consts_r"], 1)
                with act.Fori(0, PAIRS) as i:
                    def split_hi(p, dst, scale, name):
                        act.wait_ge(ws.piece_done, ws.done(i, p))
                        act.activation(dst[:, (p % 2) * HALF:(p % 2 + 1) * HALF], ps[6 + p % 2][:, :], ACT.Copy,
                                       scale=scale).then_inc(s[name], 1)
                    ws.round_hi(act, i, 0)
                    ws.round_hi(act, i, 1)
                    for p in range(2):
                        split_hi(p, q[0], DH ** -0.5, "q_hi")
                    ws.round_hi(act, i, 2)
                    for p in range(2, 4):
                        split_hi(p, k[0], 1.0, "k_hi")
                    for p in range(4, 6):
                        split_hi(p, vT, 1.0, "v_copied")
                    for n in range(2):
                        act.wait_ge(s["v_turned"], 2 * i + n + 1)
                        act.activation(v[0][:, 4 * n:4 * n + 4, :], ps[n][:, :].rearrange("p (t m) -> p t m", t=4),
                                       ACT.Copy).then_inc(s["v_hi"], 1)

                    def probs(h, qb):
                        u = i * UNITS + h * 8 + qb
                        n = (qb + 1) * P
                        act.wait_ge(s["maxed"], u + 1)
                        g = qb // 4
                        act.wait_ge(s["pt_turned"], nth_pt(i, h, g, nkt[g] - 1) + 1)
                        act.wait_ge(s["scaled"], u + 1)
                        src = core.psum[:, 1024 * (qb % 2):1024 * (qb % 2) + n]
                        act.activation(slot(qb)[:, 0:n], src, ACT.Exp, bias=nm[:, qb % 2:qb % 2 + 1],
                                       accum_out=rs[:, qb % 2:qb % 2 + 1]).then_inc(s["probs"], 1)

                    def turned(h, g, kt):
                        n = nth_pt(i, h, g, kt)
                        c0 = max(kt - 4 * g, 0) * P
                        act.wait_ge(s["pt_turned"], n + 13)
                        act.wait_ge(s["pv_done"], n + 1)
                        act.activation(pt[0][:, kt % 2, c0:HALF], ps[4 + kt % 2][:, c0:HALF], ACT.Copy).then_inc(s["pt_hi"], 1)

                    for h in range(2):
                        for qb in range(4):
                            probs(h, qb)
                        for qb in range(4, 8):
                            probs(h, qb)
                            turned(h, 0, qb - 4)
                        for kt in range(8):
                            turned(h, 1, kt)

            @block.vector
            def _(dve):
                dve.sem_inc(s["pt_lo"], 2)
                dve.sem_inc(s["o_read"], 2)
                dve.wait_ge(s["consts"], 32)
                with dve.Fori(0, PAIRS) as i:
                    def gate_rows(h):
                        dve.tensor_scalar(th[:, :], tbase[:, :], sel[:, 2 * i + h, :], None, ALU.mult)\
                           .then_inc(s["f_rows"], 1)

                    def split_lo(p, dst, scale, hi_name, name):
                        o = slice((p % 2) * HALF, (p % 2 + 1) * HALF)
                        dve.wait_ge(s[hi_name], 2 * i + p % 2 + 1)
                        dve.scalar_tensor_tensor(dst[1][:, o], ps[6 + p % 2][:, :], scale, dst[0][:, o].bitcast(F32),
                                                 ALU.mult, ALU.subtract).then_inc(s[name], 1)

                    def maxes(h, qb):
                        u = i * UNITS + h * 8 + qb
                        dve.wait_ge(s["scored"], u + 1)
                        at = 1024 * (qb % 2)
                        dve.tensor_reduce(nm[:, qb % 2:qb % 2 + 1], core.psum[:, at:at + (qb + 1) * P], AX.X, ALU.max,
                                          negate=True).then_inc(s["maxed"], 1)

                    def recip(h, qb):
                        u = i * UNITS + h * 8 + qb
                        dve.wait_ge(s["probs"], u + 3)
                        dve.reciprocal(rs[:, qb % 2:qb % 2 + 1], rs[:, qb % 2:qb % 2 + 1]).then_inc(s["recips"], 1)

                    def turned(h, g, kt):
                        n = nth_pt(i, h, g, kt)
                        c0 = max(kt - 4 * g, 0) * P
                        dve.wait_ge(s["pt_hi"], n + 1)
                        dve.tensor_tensor(pt[1][:, kt % 2, c0:HALF], ps[4 + kt % 2][:, c0:HALF],
                                          pt[0][:, kt % 2, c0:HALF].bitcast(F32), ALU.subtract).then_inc(s["pt_lo"], 1)

                    def output(h, g):
                        dve.wait_ge(s["pv_done"], nth_pt(i, h, g, nkt[g] - 1) + 3)
                        r = slice(h * DH, (h + 1) * DH)
                        dve.tensor_copy(mix[r, 4 + i, g * HALF:(g + 1) * HALF], ps[6 + g][r, :]).then_inc(s["o_read"], 1)

                    gate_rows(0)
                    for p in range(2):
                        split_lo(p, q, DH ** -0.5, "q_hi", "q_done")
                    for p in range(2, 4):
                        split_lo(p, k, 1.0, "k_hi", "k_done")
                    for n in range(2):
                        dve.wait_ge(s["v_hi"], 2 * i + n + 1)
                        dve.tensor_tensor(v[1][:, 4 * n:4 * n + 4, :], ps[n][:, :].rearrange("p (t m) -> p t m", t=4),
                                          v[0][:, 4 * n:4 * n + 4, :].bitcast(F32), ALU.subtract).then_inc(s["v_done"], 1)
                    for h in range(2):
                        for qb in range(8):
                            maxes(h, qb)
                            if qb:
                                recip(h, qb - 1)
                            if qb >= 4:
                                turned(h, 0, qb - 4)
                        recip(h, 7)
                        if h == 0:
                            gate_rows(1)
                        output(h, 0)
                        for kt in range(8):
                            turned(h, 1, kt)
                        output(h, 1)

            @block.tensor
            def _(pe):
                ws.start_pieces(pe)
                pe.sem_inc(s["pt_turned"], 12)
                pe.sem_inc(s["pv_done"], 2)
                pe.wait_ge(s["consts_r"], 1)
                with pe.Fori(0, PAIRS) as i:
                    for p in range(6):
                        if p % 2 == 0:
                            ws.wait_tile(pe, i, p // 2)
                        if p == 0:
                            pe.wait_ge(s["o_read"], i * 4 + 2)
                        elif p >= 2:
                            pe.wait_ge(s["q_done" if p < 4 else "k_done"], 2 * i + p % 2 + 1)
                        ws.piece(pe, p // 2, ps[6 + p % 2], core.hh, core.hl, (p % 2) * HALF, HALF)
                    pe.wait_ge(s["probs"], i * UNITS + 2)
                    for n in range(2):
                        pe.wait_ge(s["v_copied"], 2 * i + n + 1)
                        for t in range(4):
                            at = (4 * n + t) * P
                            last = pe.transpose(ps[n][:, t * P:(t + 1) * P], vT[:, at:at + P], core.ident[:, :])
                        last.then_inc(s["v_turned"], 1)
                    pe.wait_ge(s["k_done"], 2 * i + 2)
                    pe.wait_ge(s["v_done"], 2 * i + 2)

                    def score(h, qb):
                        u = i * UNITS + h * 8 + qb
                        pe.wait_ge(s["probs"], u + 1)
                        r, c0 = slice(h * DH, (h + 1) * DH), slice(qb * P, (qb + 1) * P)
                        keys = (qb + 1) * P
                        for a in range(0, keys, HALF):
                            n = min(HALF, keys - a)
                            at = 1024 * (qb % 2) + a
                            out = core.psum[:, at:at + n]
                            pe.matmul(out, q[0][r, c0], k[0][r, a:a + n], start=True, stop=False)
                            pe.matmul(out, q[0][r, c0], k[1][r, a:a + n], start=False, stop=False)
                            pe.matmul(out, q[1][r, c0], k[0][r, a:a + n], start=False, stop=False)
                            pe.matmul(out, th[:, c0], rf[:, a:a + n], start=False, stop=(a + n < keys))
                        last = pe.matmul(core.psum[:, at + n - P:at + n], idr[:, :], ngr[:, :], start=False, stop=True)
                        last.then_inc(s["scored"], 1)

                    def turn(h, g, kt):
                        n = nth_pt(i, h, g, kt)
                        if kt == 0:
                            pe.wait_ge(s["scaled"], i * UNITS + h * 8 + 4 * g + 6)
                        pe.wait_ge(s["pt_lo"], n + 1)
                        for b in range(max(kt - 4 * g, 0), 4):
                            last = pe.transpose(ps[4 + kt % 2][:, b * P:(b + 1) * P],
                                                slot(4 * g + b)[:, kt * P:(kt + 1) * P], core.ident[:, :])
                        last.then_inc(s["pt_turned"], 1)

                    def times_v(h, g, kt):
                        n = nth_pt(i, h, g, kt)
                        c0 = max(kt - 4 * g, 0) * P
                        if kt == 0:
                            pe.wait_ge(s["o_read"], i * 4 + h * 2 + g + 1)
                        pe.wait_ge(s["pt_lo"], n + 3)
                        out, b = ps[6 + g][:, c0:HALF], kt % 2
                        pe.matmul(out, v[0][:, kt, :], pt[0][:, b, c0:HALF], start=(kt == 0), stop=False)
                        pe.matmul(out, v[0][:, kt, :], pt[1][:, b, c0:HALF], start=False, stop=False)
                        pe.matmul(out, v[1][:, kt, :], pt[0][:, b, c0:HALF], start=False, stop=(kt == nkt[g] - 1))\
                          .then_inc(s["pv_done"], 1)

                    for h in range(2):
                        pe.wait_ge(s["f_rows"], 2 * i + h + 1)
                        for qb in range(8):
                            score(h, qb)
                            if qb > 4:
                                times_v(h, 0, qb - 5)
                            if qb >= 4:
                                turn(h, 0, qb - 4)
                        times_v(h, 0, 3)
                        turn(h, 1, 0)
                        for kt in range(8):
                            if kt < 7:
                                turn(h, 1, kt + 1)
                            times_v(h, 1, kt)


class OutProjection:

    def __init__(self, ph, core, feat, w_src):
        self.core, self.feat, self.w_src = core, feat, w_src
        self.wh = ph.sb("w_all_hi", [P, KT, D], F32R)
        self.wl = ph.sb("w_all_lo", [P, KT, D], F32R)
        self.loaded = [ph.sem(f"row_loaded{b}") for b in range(2)]
        self.fhi, self.flo, self.whi, self.wlo = (ph.sem(n) for n in ("feat_hi", "feat_lo", "row_hi", "row_lo"))
        self.mm, self.read = ph.sem("tile_mm"), ph.sem("tile_read")

    def sync(self, sync):
        for k in range(KT):
            if k >= 2:
                sync.wait_ge(self.wlo, k - 1)
            sync.dma_start(self.core.raw[:, k % 2, :], self.w_src[k, :, :]).then_inc(self.loaded[k % 2], 16)

    def act(self, act, feat_ready):
        for k in range(KT):
            feat_ready(act, k)
            act.activation(self.core.hh[:, k, :], self.feat[:, k, :], ACT.Copy).then_inc(self.fhi, 1)
            act.wait_ge(self.loaded[k % 2], 16 * (k // 2) + 16)
            act.activation(self.wh[:, k, :], self.core.raw[:, k % 2, :], ACT.Copy).then_inc(self.whi, 1)

    def pool(self, pool):
        for k in range(KT):
            pool.wait_ge(self.whi, k + 1)
            pool.tensor_tensor(self.wl[:, k, :], self.core.raw[:, k % 2, :], self.wh[:, k, :].bitcast(F32),
                               ALU.subtract).then_inc(self.wlo, 1)

    def dve(self, dve):
        for k in range(KT):
            dve.wait_ge(self.fhi, k + 1)
            dve.tensor_tensor(self.core.hl[:, k, :], self.feat[:, k, :], self.core.hh[:, k, :].bitcast(F32),
                              ALU.subtract).then_inc(self.flo, 1)

    def pe(self, pe):
        ps, hh, hl = self.core.ps, self.core.hh, self.core.hl
        for g in range(2):
            for k in range(KT):
                if g == 0:
                    pe.wait_ge(self.flo, k + 1)
                    pe.wait_ge(self.wlo, k + 1)
                for t in range(4):
                    if g and k == 0:
                        pe.wait_ge(self.read, t + 1)
                    c0 = (4 * g + t) * P
                    for f, w, m in ((hh, self.wh, 0), (hh, self.wl, 1), (hl, self.wh, 2)):
                        for c in range(2):
                            last = pe.matmul(ps[2 * t + c][:, :], f[:, k, c0:c0 + P], w[:, k, c * 512:(c + 1) * 512],
                                             start=(k == 0 and m == 0), stop=(k == KT - 1 and m == 2))
                    if k == KT - 1:
                        last.then_inc(self.mm, 1)

    def banks(self, t):
        return self.core.psum[:, (t % 4) * 1024:(t % 4) * 1024 + 1024]


def mixer_output(core, mix):
    nc, d = core.nc, core.d
    with Phase(core, "wo") as ph:
        op = OutProjection(ph, core, mix, d["w_o"])
        x = ph.sb("x", [P, 2, D], F32)
        sq = ph.sb("sq", [P, D], F32)
        ss = ph.sb("ss", [P, NT], F32)
        y = mix
        s_x = [ph.sem(f"x_loaded{b}") for b in range(2)]
        s_st = ph.sem("x1_stored")
        s_ss, s_ms, s_rt, s_step = ph.sem("squares"), ph.sem("means"), ph.sem("roots"), ph.sem("step")
        tr = Transposes(ph, core, y, core.hh, core.hl, 2, 4, lambda k: core.cols[:, C_LN2 + k:C_LN2 + k + 1])
        with nc.Block() as block:
            @block.sync
            def _(sync):
                op.sync(sync)

            @block.gpsimd
            def _(pool):
                op.pool(pool)
                for t in range(NT):
                    if t >= 2:
                        pool.wait_ge(op.read, t - 1)
                    pool.dma_start(x[:, t % 2, :], d["x"][t, :, :]).then_inc(s_x[t % 2], 16)
                    if t >= 1:
                        pool.wait_ge(op.read, t)
                        pool.dma_start(d["x1"][t - 1, :, :], y[:, t - 1, :]).then_inc(s_st, 16)
                pool.wait_ge(op.read, NT)
                pool.dma_start(d["x1"][NT - 1, :, :], y[:, NT - 1, :]).then_inc(s_st, 16)
                pool.wait_ge(s_st, 16 * NT)

            @block.scalar
            def _(act):
                op.act(act, lambda act, k: None)
                for t in range(NT):
                    act.wait_ge(op.read, t + 1)
                    act.activation(sq[:, :], y[:, t, :], ACT.Square, accum_out=ss[:, t:t + 1]).then_inc(s_ss, 1)
                    act.wait_ge(s_ss, t + 1)
                act.wait_ge(s_ms, 1)
                act.activation(ss[:, :], ss[:, :], ACT.Sqrt).then_inc(s_rt, 1)
                for g in range(2):
                    tr.act(act, g)

            @block.vector
            def _(dve):
                op.dve(dve)
                for t in range(NT):
                    dve.wait_ge(op.mm, t + 1)
                    dve.wait_ge(s_x[t % 2], 16 * (t // 2) + 16)
                    dve.tensor_tensor(y[:, t, :], op.banks(t), x[:, t % 2, :], ALU.add).then_inc(op.read, 1)
                step = Steps(dve, s_step)
                dve.wait_ge(s_ss, NT)
                dve.tensor_scalar(ss[:, :], ss[:, :], 1.0 / D, EPS, ALU.mult, ALU.add).then_inc(s_ms, 1)
                dve.wait_ge(s_rt, 1)
                step(dve.reciprocal(ss[:, :], ss[:, :]))
                dve.wait_ge(s_st, 16 * NT)
                for g in range(2):
                    for t in range(4 * g, 4 * g + 4):
                        last = dve.tensor_scalar(y[:, t, :], y[:, t, :], ss[:, t:t + 1], None, ALU.mult)
                    last.then_inc(tr.ready, 1)
                    tr.dve(dve, g)

            @block.tensor
            def _(pe):
                op.pe(pe)
                pe.wait_ge(op.read, NT)
                for g in range(2):
                    tr.pe(pe, g)


def gate_and_up(core, hid):
    nc, d, ps = core.nc, core.d, core.ps
    with Phase(core, "gu") as ph:
        ws = Weights(ph, core, [0, 1], [1, 3], 4)
        s_silu, s_prod = ph.sem("silu_done"), ph.sem("product_done")
        with nc.Block() as block:
            @block.sync
            def _(sync):
                with sync.Fori(0, FT) as i:
                    for c in range(2):
                        ws.load(sync, i, c, d["w_gu"][2 * i + c, :, :])

            @block.gpsimd
            def _(pool):
                ws.start_lo(pool)
                with pool.Fori(0, FT) as i:
                    for c in range(2):
                        ws.subtract_lo(pool, i, c)

            @block.scalar
            def _(act):
                act.sem_inc(s_silu, 2)
                with act.Fori(0, FT) as i:
                    for c in range(2):
                        ws.round_hi(act, i, c)
                    for p in range(2):
                        act.wait_ge(ws.piece_done, ws.done(i, p))
                        act.activation(hid[:, i, p * HALF:(p + 1) * HALF], ps[p][:, :], ACT.Silu).then_inc(s_silu, 1)

            @block.vector
            def _(dve):
                dve.sem_inc(s_prod, 2)
                with dve.Fori(0, FT) as i:
                    for p in range(2):
                        dve.wait_ge(s_silu, 2 * i + p + 3)
                        dve.wait_ge(ws.piece_done, ws.done(i, p + 2))
                        o = slice(p * HALF, (p + 1) * HALF)
                        dve.tensor_tensor(hid[:, i, o], ps[2 + p][:, :], hid[:, i, o], ALU.mult).then_inc(s_prod, 1)

            @block.tensor
            def _(pe):
                ws.start_pieces(pe)
                with pe.Fori(0, FT) as i:
                    for p in range(4):
                        if p % 2 == 0:
                            ws.wait_tile(pe, i, p // 2)
                        pe.wait_ge(s_silu if p < 2 else s_prod, 2 * i + p % 2 + 1)
                        ws.piece(pe, p // 2, ps[p][:, :], core.hh, core.hl, (p % 2) * HALF, HALF)


def down(core, hid):
    nc, d = core.nc, core.d
    with Phase(core, "down") as ph:
        y0 = ph.sb("y", [P, 4, D], F32)
        lnf = ph.sb("ln_f", [P, D], F32)
        ss = ph.sb("ss", [P, NT], F32)
        loaded = [ph.sem(f"w_loaded{b}") for b in range(2)]
        whi, wlo, ahi, alo, mm = (ph.sem(n) for n in ("w_hi", "w_lo", "act_hi", "act_lo", "mm"))
        s_x = [ph.sem(f"x{t}") for t in range(NT)]
        s_row, s_add, s_ss, s_ms, s_rt, s_step = (ph.sem(n) for n in ("row", "added", "squares", "means", "roots", "step"))
        s_x3, s_st = ph.sem("x3_ready"), ph.sem("x3_stored")

        class Tiles:
            def __getitem__(self, at):
                _, t, c = at
                return y0[:, t, c] if t < 4 else hid[:, t, c]
        y = Tiles()
        ah = [core.hh[:, b, HALF:SEQ] for b in range(2)]
        al = [core.hl[:, b, HALF:SEQ] for b in range(2)]
        tr = Transposes(ph, core, y, core.hh, core.hl, 2, 4,
                        lambda k: core.mods[:, 8 + k, 0:1], lambda k: core.mods[:, k, 0:1])

        def rounds(eng, g, body):
            body(0, True, False)
            with eng.Fori(1, FT // 2 - 1) as i:
                body(i, False, False)
            body(FT // 2 - 1, False, True)
        with nc.Block() as block:
            @block.sync
            def _(sync):
                sync.dma_start(lnf[:, :], d["ln_f"].partition_broadcast(P)).then_inc(s_row, 16)
                for t in range(4):
                    sync.dma_start(y0[:, t, :], d["x1"][t, :, :]).then_inc(s_x[t], 16)
                for g in range(2):
                    def body(i, first, last):
                        for b in range(2):
                            sync.wait_ge(wlo, g * FT + 2 * i + b + 1)
                            sync.dma_start(core.raw[:, b, :], d["w_down"][2 * i + b, :, :]).then_inc(loaded[b], 16)
                    rounds(sync, g, body)
                sync.wait_ge(ahi, 2 * FT)
                sync.wait_ge(alo, 2 * FT)
                for t in range(4, NT):
                    sync.dma_start(y[:, t, slice(0, D)], d["x1"][t, :, :]).then_inc(s_x[t], 16)
                for t in range(NT):
                    sync.wait_ge(s_x3, t + 1)
                    sync.dma_start(d["x3"][t, :, :], y[:, t, slice(0, D)]).then_inc(s_st, 16)
                sync.wait_ge(s_st, 16 * NT)

            @block.scalar
            def _(act):
                for g in range(2):
                    def body(i, first, last):
                        for b in range(2):
                            n = g * FT + 2 * i + b
                            act.wait_ge(loaded[b], (g * (FT // 2) + i) * 16 + 16)
                            act.wait_ge(mm, n + 1)
                            act.activation(core.wh[:, b, :], core.raw[:, b, :], ACT.Copy).then_inc(whi, 1)
                            act.activation(ah[b], hid[:, 2 * i + b, g * HALF:(g + 1) * HALF], ACT.Copy).then_inc(ahi, 1)
                    rounds(act, g, body)
                    for t in range(4 * g, 4 * g + 4) if g == 0 else ():
                        act.wait_ge(s_add, t + 1)
                        act.activation(core.psum[:, (t % 4) * 1024:(t % 4 + 1) * 1024], y[:, t, slice(0, D)], ACT.Square,
                                       accum_out=ss[:, t:t + 1]).then_inc(s_ss, 1)
                for t in range(4, NT):
                    act.wait_ge(s_add, t + 1)
                    act.activation(core.psum[:, (t % 4) * 1024:(t % 4 + 1) * 1024], y[:, t, slice(0, D)], ACT.Square,
                                   accum_out=ss[:, t:t + 1]).then_inc(s_ss, 1)
                act.wait_ge(s_ms, 1)
                act.activation(ss[:, :], ss[:, :], ACT.Sqrt).then_inc(s_rt, 1)
                for t in range(NT):
                    act.wait_ge(s_x3, t + 1)
                    act.activation(core.psum[:, (t % 4) * 1024:(t % 4 + 1) * 1024], y[:, t, slice(0, D)], ACT.Square,
                                   accum_out=ss[:, t:t + 1]).then_inc(s_ss, 1)
                    act.wait_ge(s_ss, NT + t + 1)
                act.wait_ge(s_ms, 2)
                act.activation(ss[:, :], ss[:, :], ACT.Sqrt).then_inc(s_rt, 1)
                for g in range(2):
                    tr.act(act, g)

            @block.gpsimd
            def _(pool):
                pool.sem_inc(wlo, 2)
                for g in range(2):
                    def body(i, first, last):
                        for b in range(2):
                            pool.wait_ge(whi, g * FT + 2 * i + b + 1)
                            pool.tensor_tensor(core.wl[:, b, :], core.raw[:, b, :], core.wh[:, b, :].bitcast(F32),
                                               ALU.subtract).then_inc(wlo, 1)
                    rounds(pool, g, body)

            @block.vector
            def _(dve):
                step = Steps(dve, s_step)
                for g in range(2):
                    def body(i, first, last):
                        for b in range(2):
                            dve.wait_ge(ahi, g * FT + 2 * i + b + 1)
                            dve.tensor_tensor(al[b], hid[:, 2 * i + b, g * HALF:(g + 1) * HALF], ah[b].bitcast(F32),
                                              ALU.subtract).then_inc(alo, 1)
                    rounds(dve, g, body)
                    dve.wait_ge(mm, (g + 1) * FT + 2)
                    for t in range(4 * g, 4 * g + 4):
                        dve.wait_ge(s_x[t], 16)
                        yt = y[:, t, slice(0, D)]
                        dve.tensor_tensor(yt, core.psum[:, (t % 4) * 1024:(t % 4 + 1) * 1024], yt, ALU.add)\
                           .then_inc(s_add, 1)
                dve.wait_ge(s_ss, NT)
                dve.tensor_scalar(ss[:, :], ss[:, :], 1.0 / D, EPS, ALU.mult, ALU.add).then_inc(s_ms, 1)
                dve.wait_ge(s_rt, 1)
                step(dve.reciprocal(ss[:, :], ss[:, :]))
                dve.wait_ge(s_row, 16)
                for t in range(NT):
                    yt = y[:, t, slice(0, D)]
                    dve.scalar_tensor_tensor(yt, yt, ss[:, t:t + 1], lnf[:, :], ALU.mult, ALU.mult).then_inc(s_x3, 1)
                dve.wait_ge(s_ss, 2 * NT)
                dve.tensor_scalar(ss[:, :], ss[:, :], 1.0 / D, EPS, ALU.mult, ALU.add).then_inc(s_ms, 1)
                dve.wait_ge(s_rt, 2)
                step(dve.reciprocal(ss[:, :], ss[:, :]))
                dve.wait_ge(s_st, 16 * NT)
                for g in range(2):
                    for t in range(4 * g, 4 * g + 4):
                        yt = y[:, t, slice(0, D)]
                        last = dve.tensor_scalar(yt, yt, ss[:, t:t + 1], None, ALU.mult)
                    last.then_inc(tr.ready, 1)
                    tr.dve(dve, g)

            @block.tensor
            def _(pe):
                pe.sem_inc(mm, 2)
                for g in range(2):
                    def body(i, first, last):
                        for b in range(2):
                            n = g * FT + 2 * i + b
                            pe.wait_ge(wlo, n + 3)
                            pe.wait_ge(alo, n + 1)
                            if g and first and b == 0:
                                pe.wait_ge(s_ss, 4)
                            for t in range(4):
                                for f, w, m in ((ah, core.wh, 0), (ah, core.wl, 1), (al, core.wh, 2)):
                                    for c in range(2):
                                        mmul = pe.matmul(core.ps[2 * t + c][:, :], f[b][:, t * P:(t + 1) * P],
                                                         w[:, b, c * 512:(c + 1) * 512],
                                                         start=(first and b == 0 and m == 0), stop=(last and b == 1 and m == 2))
                            mmul.then_inc(mm, 1)
                    rounds(pe, g, body)
                pe.wait_ge(s_ss, 2 * NT)
                for g in range(2):
                    tr.pe(pe, g)


def context_norm(core, hc):
    nc, d = core.nc, core.d
    with Phase(core, "ctx") as ph:
        y = ph.sb("y", [P, 2, D], F32)
        sq = ph.sb("sq", [P, D], F32)
        ss = ph.sb("ss", [P, 2], F32)
        s_x, s_ss, s_ms, s_rt, s_step = (ph.sem(n) for n in ("x", "squares", "means", "roots", "step"))
        tr = Transposes(ph, core, y, hc[0], hc[1], 1, 2,
                        lambda k: core.mods[:, 8 + k, 1:2], lambda k: core.mods[:, k, 1:2])
        with nc.Block() as block:
            @block.sync
            def _(sync):
                sync.dma_start(y[:, :, :], d["ctx"].rearrange("t p n -> p t n")).then_inc(s_x, 16)

            @block.scalar
            def _(act):
                act.wait_ge(s_x, 16)
                for t in range(2):
                    act.activation(sq[:, :], y[:, t, :], ACT.Square, accum_out=ss[:, t:t + 1]).then_inc(s_ss, 1)
                    act.wait_ge(s_ss, t + 1)
                act.wait_ge(s_ms, 1)
                act.activation(ss[:, :], ss[:, :], ACT.Sqrt).then_inc(s_rt, 1)
                tr.act(act, 0)

            @block.vector
            def _(dve):
                step = Steps(dve, s_step)
                dve.wait_ge(s_ss, 2)
                dve.tensor_scalar(ss[:, :], ss[:, :], 1.0 / D, EPS, ALU.mult, ALU.add).then_inc(s_ms, 1)
                dve.wait_ge(s_rt, 1)
                step(dve.reciprocal(ss[:, :], ss[:, :]))
                for t in range(2):
                    last = dve.tensor_scalar(y[:, t, :], y[:, t, :], ss[:, t:t + 1], None, ALU.mult)
                last.then_inc(tr.ready, 1)
                tr.dve(dve, 0)

            @block.tensor
            def _(pe):
                tr.pe(pe, 0)


def differential_attention(core, hc):
    nc, d, ps = core.nc, core.d, core.ps
    STEPS = 2 * NKT
    PIECES = 10
    TILE = (0, 0, 1, 1, 1, 2, 2, 2, 3, 3)
    with Phase(core, "diff") as ph:
        q = [ph.sb(n, [P, SEQ], F32R) for n in ("q_hi", "q_lo")]
        k = [ph.sb(n, [P, NKEY], F32R) for n in ("k_hi", "k_lo")]
        v = [ph.sb(n, [P, NKT, P], F32R) for n in ("v_hi", "v_lo")]
        zs = ph.sb("silu_z", [P, SEQ], F32)
        pr = ph.sb("probs", [P, 8, NKEY], F32)
        p1 = ph.sb("probs_1", [P, NKEY], F32)
        pt = [ph.sb(n, [P, 2, HALF], F32R) for n in ("pt_hi", "pt_lo")]
        rope = ph.sb("rope", [P, 2, SEQ], F32)
        ob = ph.sb("o", [P, HALF], F32)
        sq = ph.sb("sq", [P, HALF], F32)
        rt = ph.sb("rstd", [P, HALF], F32)
        ot = ph.sb("o_out", [P, HALF], F32)
        ones = ph.sb("ones", [P, P], F32)
        nm = ph.sb("neg_max", [P, 2, 2], F32)
        rs = ph.sb("row_sum", [P, 2, 2], F32)
        rr = ph.sb("recip", [P, 2, 2], F32)
        nl = ph.sb("neg_lam_recip", [P, 2], F32)
        vT = p1
        ws = Weights(ph, core, [0, 1, 0, 1], [1, 4, 7, 9], PIECES)
        names = ("consts qk_step qk_hi qk_done swapped act_read v_turned v_hi v_done score0 score1 max0 max1 prob0 prob1 "
                 "rsum nl p1 comb pt_turned pt_hi pt_lo pv_done o_copied ss_done rstd o_step o_ready o_stored")
        s = {n: ph.sem(n) for n in names.split()}
        swap = [(j + 16) % 32 for j in range(32)]

        def bank_turn(n):
            return 6 if n <= 6 or n % 2 == 0 else 2
        with nc.Block() as block:
            @block.sync
            def _(sync):
                sync.sem_inc(s["o_stored"], 16)
                sync.dma_start(rope[:, :, :], d["rope"]).then_inc(s["consts"], 16)
                with sync.Fori(0, HEADS2) as i:
                    for c in range(4):
                        ws.load(sync, i, c, d["da_w_in"][4 * i + c, :, :])
                    for g in range(2):
                        sync.wait_ge(s["o_ready"], 2 * i + g + 1)
                        sync.dma_start(d["o_feat"][i, :, g * HALF:(g + 1) * HALF], ot[:, :]).then_inc(s["o_stored"], 16)
                sync.wait_ge(s["o_stored"], 16 * (2 * HEADS2 + 1))

            @block.gpsimd
            def _(pool):
                ws.start_lo(pool)
                with pool.Fori(0, HEADS2) as i:
                    for c in range(4):
                        ws.subtract_lo(pool, i, c)
                    for qb in range(8):
                        pool.wait_ge(s["nl"], i * 8 + qb + 1)
                        pool.nop(nofuse=True)
                        pool.tensor_scalar(p1[:, :], p1[:, :], nl[:, qb % 2:qb % 2 + 1], 1.0, ALU.mult, ALU.mult)\
                            .then_inc(s["p1"], 1)

            @block.scalar
            def _(act):
                act.sem_inc(s["prob0"], 1)
                act.sem_inc(s["prob1"], 1)
                act.sem_inc(s["act_read"], 5)
                with act.Fori(0, HEADS2) as i:
                    def qk_hi(j):
                        if j < 4:
                            act.wait_ge(s["qk_step"], 12 * i + 3 * j + 3)
                            src = sq[:, :]
                        else:
                            act.wait_ge(ws.piece_done, ws.done(i, 4))
                            src = ps[6][:, 0:CTX]
                        dst = q[0][:, j * HALF:(j + 1) * HALF] if j < 2 else k[0][:, (j - 2) * HALF:min((j - 1) * HALF, NKEY)]
                        act.activation(dst, src, ACT.Copy, scale=DH ** -0.5 if j < 2 else 1.0).then_inc(s["qk_hi"], 1)

                    def hi(n):
                        b = n % 2
                        act.wait_ge(s["pt_turned"], STEPS * (i + 1) + n + 1)
                        act.wait_ge(s["pv_done"], STEPS * i + n + 1)
                        act.activation(pt[0][:, b, :], ps[bank_turn(n)][:, :], ACT.Copy).then_inc(s["pt_hi"], 1)

                    def prob(qb, z):
                        u = i * 8 + qb
                        act.wait_ge(s[f"max{z}"], u + 1)
                        if z == 0:
                            act.wait_ge(s["pt_turned"], STEPS * i + NKT * (qb // 4) + NKT)
                        else:
                            act.wait_ge(s["comb"], u + 1)
                        dst = pr[:, qb, :] if z == 0 else p1[:, :]
                        act.activation(dst, core.psum[:, 1536 * z:1536 * z + NKEY], ACT.Exp, bias=nm[:, qb % 2, z:z + 1],
                                       accum_out=rs[:, qb % 2, z:z + 1]).then_inc(s[f"prob{z}"], 1)

                    def outputs(g):
                        bank = (7, 4)[g]
                        act.wait_ge(s["pv_done"], STEPS * i + NKT * (g + 1) + 2)
                        act.wait_ge(s["o_step"], 2 * i + g + 1)
                        act.activation(ob[:, :], ps[bank][:, :], ACT.Copy).then_inc(s["o_copied"], 1)
                        act.activation(sq[:, :], ps[bank][:, :], ACT.Square).then_inc(s["o_copied"], 1)

                    def rstd(g):
                        act.wait_ge(s["ss_done"], 2 * i + g + 1)
                        act.activation(rt[:, :], ps[(3, 5)[g]][:, :], ACT.Ln, scale=1.0 / P, bias=core.eps[:, 1:2])\
                           .then_inc(s["rstd"], 1)
                        act.wait_ge(s["rstd"], 2 * (2 * i + g) + 1)
                        act.activation(rt[:, :], rt[:, :], ACT.Exp, scale=-0.5).then_inc(s["rstd"], 1)

                    ws.round_hi(act, i, 0)
                    ws.round_hi(act, i, 1)
                    qk_hi(0)
                    qk_hi(1)
                    ws.round_hi(act, i, 2)
                    for j in range(2, 5):
                        qk_hi(j)
                    ws.round_hi(act, i, 3)
                    act.wait_ge(s["comb"], i * 8 + 1)
                    for j, n in ((0, HALF), (1, HALF), (2, CTX)):
                        act.wait_ge(ws.piece_done, ws.done(i, 5 + j))
                        act.activation(vT[:, j * HALF:j * HALF + n], ps[6 + (5 + j) % 2][:, 0:n], ACT.Copy)\
                           .then_inc(s["act_read"], 1)
                    for j, n in ((0, 4), (1, 4), (2, 2)):
                        act.wait_ge(s["v_turned"], 3 * i + j + 1)
                        act.activation(v[0][:, 4 * j:4 * j + n, :], ps[j][:, 0:n * P].rearrange("p (t m) -> p t m", t=n),
                                       ACT.Copy).then_inc(s["v_hi"], 1)
                    for j in range(2):
                        act.wait_ge(ws.piece_done, ws.done(i, 8 + j))
                        act.activation(zs[:, j * HALF:(j + 1) * HALF], ps[6 + j][:, :], ACT.Silu).then_inc(s["act_read"], 1)
                    for qb in range(8):
                        prob(qb, 0)
                        if qb > 4:
                            hi(2 * (qb - 4) - 1)
                        prob(qb, 1)
                        if qb >= 4:
                            hi(2 * (qb - 4))
                    for n in range(7, STEPS):
                        hi(n)
                        if n == 10:
                            outputs(0)
                        if n == 13:
                            rstd(0)
                    outputs(1)
                    rstd(1)

            @block.vector
            def _(dve):
                dve.sem_inc(s["comb"], 1)
                dve.sem_inc(s["pt_lo"], 2)
                dve.sem_inc(s["o_step"], 1)
                dve.memset(ones[:, :], 1.0)
                dve.wait_ge(s["consts"], 16)
                with dve.Fori(0, HEADS2) as i:
                    def rotate(j):
                        o = slice((j % 2) * HALF, (j % 2 + 1) * HALF)
                        dve.wait_ge(ws.piece_done, ws.done(i, j))
                        if j:
                            dve.wait_ge(s["qk_done"], 5 * i + j)
                        dve.tensor_tensor(sq[:, :], ps[6 + j % 2][:, :], rope[:, 0, o], ALU.mult).then_inc(s["swapped"], 1)
                        dve.stream_shuffle(ob[:, :], ps[6 + j % 2][:, :], swap).then_inc(s["qk_step"], 1)
                        dve.wait_ge(s["qk_step"], 12 * i + 3 * j + 1)
                        dve.tensor_tensor(ob[:, :], ob[:, :], rope[:, 1, o], ALU.mult).then_inc(s["qk_step"], 1)
                        dve.wait_ge(s["qk_step"], 12 * i + 3 * j + 2)
                        dve.wait_ge(s["swapped"], 4 * i + j + 1)
                        dve.tensor_tensor(sq[:, :], sq[:, :], ob[:, :], ALU.add).then_inc(s["qk_step"], 1)
                        dve.wait_ge(s["qk_step"], 12 * i + 3 * j + 3)

                    def qk_lo(j):
                        src = sq[:, :] if j < 4 else ps[6][:, 0:CTX]
                        x = q if j < 2 else k
                        o = slice(j * HALF, (j + 1) * HALF) if j < 2 else slice((j - 2) * HALF, min((j - 1) * HALF, NKEY))
                        dve.wait_ge(s["qk_hi"], 5 * i + j + 1)
                        dve.scalar_tensor_tensor(x[1][:, o], src, DH ** -0.5 if j < 2 else 1.0, x[0][:, o].bitcast(F32),
                                                 ALU.mult, ALU.subtract).then_inc(s["qk_done"], 1)

                    def maxes(qb, z):
                        dve.wait_ge(s[f"score{z}"], i * 8 + qb + 1)
                        dve.tensor_reduce(nm[:, qb % 2, z:z + 1], core.psum[:, 1536 * z:1536 * z + NKEY], AX.X, ALU.max,
                                          negate=True).then_inc(s[f"max{z}"], 1)

                    def recips(qb):
                        u = i * 8 + qb
                        b = qb % 2
                        dve.wait_ge(s["prob0"], u + 2)
                        dve.wait_ge(s["prob1"], u + 2)
                        dve.reciprocal(rr[:, b, :], rs[:, b, :]).then_inc(s["rsum"], 1)
                        dve.wait_ge(s["rsum"], u + 1)
                        dve.tensor_tensor(nl[:, b:b + 1], rr[:, b, 1:2], core.neglam[:, :], ALU.mult).then_inc(s["nl"], 1)

                    def combine(qb):
                        u = i * 8 + qb
                        dve.wait_ge(s["p1"], u + 1)
                        dve.scalar_tensor_tensor(pr[:, qb, :], pr[:, qb, :], rr[:, qb % 2, 0:1], p1[:, :],
                                                 ALU.mult, ALU.add).then_inc(s["comb"], 1)

                    def lo(n):
                        b = n % 2
                        dve.wait_ge(s["pt_hi"], STEPS * i + n + 1)
                        dve.tensor_tensor(pt[1][:, b, :], ps[bank_turn(n)][:, :], pt[0][:, b, :].bitcast(F32), ALU.subtract)\
                           .then_inc(s["pt_lo"], 1)

                    def gated(g):
                        c = 2 * i + g
                        dve.wait_ge(s["rstd"], 2 * c + 2)
                        dve.wait_ge(s["o_stored"], 16 * c + 16)
                        dve.scalar_tensor_tensor(ot[:, :], ob[:, :], core.subg[:, 0:1], rt[:, :], ALU.mult, ALU.mult)\
                           .then_inc(s["o_step"], 1)
                        dve.wait_ge(s["o_step"], c + 2)
                        dve.tensor_tensor(ot[:, :], ot[:, :], zs[:, g * HALF:(g + 1) * HALF], ALU.mult).then_inc(s["o_ready"], 1)

                    for j in range(4):
                        rotate(j)
                        qk_lo(j)
                    qk_lo(4)
                    for j, n in ((0, 4), (1, 4), (2, 2)):
                        dve.wait_ge(s["v_hi"], 3 * i + j + 1)
                        dve.tensor_tensor(v[1][:, 4 * j:4 * j + n, :], ps[j][:, 0:n * P].rearrange("p (t m) -> p t m", t=n),
                                          v[0][:, 4 * j:4 * j + n, :].bitcast(F32), ALU.subtract).then_inc(s["v_done"], 1)
                    for qb in range(8):
                        maxes(qb, 0)
                        if qb > 4:
                            lo(2 * (qb - 4) - 1)
                        if qb:
                            recips(qb - 1)
                        maxes(qb, 1)
                        if qb:
                            combine(qb - 1)
                        if qb >= 4:
                            lo(2 * (qb - 4))
                    recips(7)
                    lo(7)
                    combine(7)
                    for n in range(8, STEPS):
                        lo(n)
                        if n == 14:
                            gated(0)
                    gated(1)

            @block.tensor
            def _(pe):
                ws.start_pieces(pe)
                pe.sem_inc(s["pt_turned"], STEPS)
                pe.sem_inc(s["pv_done"], 2)
                with pe.Fori(0, HEADS2) as i:
                    def piece(p):
                        c = TILE[p]
                        if p == 0 or TILE[p - 1] != c:
                            ws.wait_tile(pe, i, c)
                        if p == 0:
                            pe.wait_ge(s["act_read"], 5 * i + 4)
                            pe.wait_ge(s["pt_lo"], STEPS * i + 2)
                        elif p == 1:
                            pe.wait_ge(s["act_read"], 5 * i + 5)
                            if_outputs_read(i)
                        elif p < 7:
                            pe.wait_ge(s["qk_done"], 5 * i + p - 1)
                        else:
                            pe.wait_ge(s["act_read"], 5 * i + p - 1)
                        ctx = p in (4, 7)
                        first = TILE.index(c)
                        n = CTX if ctx else HALF
                        hi, lo = (hc[0], hc[1]) if ctx else (core.hh, core.hl)
                        ws.piece(pe, c, ps[6 + p % 2][:, 0:n], hi, lo, 0 if ctx else (p - first) * HALF, n)

                    def if_outputs_read(i):
                        pe.wait_ge(s["pv_done"], STEPS * i + 2)

                    def score(qb, z):
                        u = i * 8 + qb
                        pe.wait_ge(s[f"prob{z}"], u + 1)
                        r, c0 = slice(z * DH, (z + 1) * DH), slice(qb * P, (qb + 1) * P)
                        for a in range(0, NKEY, HALF):
                            n = min(HALF, NKEY - a)
                            out = core.psum[:, 1536 * z + a:1536 * z + a + n]
                            pe.matmul(out, q[0][r, c0], k[0][r, a:a + n], start=True, stop=False)
                            pe.matmul(out, q[0][r, c0], k[1][r, a:a + n], start=False, stop=False)
                            last = pe.matmul(out, q[1][r, c0], k[0][r, a:a + n], start=False, stop=True)
                        last.then_inc(s[f"score{z}"], 1)

                    def turn(n):
                        g, kt = n // NKT, n % NKT
                        if kt == 0:
                            pe.wait_ge(s["comb"], i * 8 + 4 * g + 5)
                        if n == 7:
                            pe.wait_ge(s["prob0"], i * 8 + 9)
                        pe.wait_ge(s["pt_lo"], STEPS * i + n + (2 if n <= 6 else 1))
                        for b in range(4):
                            last = pe.transpose(ps[bank_turn(n)][:, b * P:(b + 1) * P],
                                                pr[:, 4 * g + b, kt * P:(kt + 1) * P], core.ident[:, :])
                        last.then_inc(s["pt_turned"], 1)

                    def times_v(n):
                        g, kt, b = n // NKT, n % NKT, n % 2
                        if n == NKT:
                            pe.wait_ge(s["prob1"], i * 8 + 9)
                        pe.wait_ge(s["pt_lo"], STEPS * i + n + 3)
                        out = ps[(7, 4)[g]][:, :]
                        pe.matmul(out, v[0][:, kt, :], pt[0][:, b, :], start=(kt == 0), stop=False)
                        pe.matmul(out, v[0][:, kt, :], pt[1][:, b, :], start=False, stop=False)
                        pe.matmul(out, v[1][:, kt, :], pt[0][:, b, :], start=False, stop=(kt == NKT - 1))\
                          .then_inc(s["pv_done"], 1)

                    def squares(g):
                        pe.wait_ge(s["o_copied"], 2 * (2 * i + g) + 2)
                        pe.matmul(ps[(3, 5)[g]][:, :], ones[:, :], sq[:, :], start=True, stop=True)\
                          .then_inc(s["ss_done"], 1)

                    for p in range(8):
                        piece(p)
                    for j, n in ((0, 4), (1, 4), (2, 2)):
                        pe.wait_ge(s["act_read"], 5 * i + 5 + j + 1)
                        for t in range(n):
                            at = (4 * j + t) * P
                            last = pe.transpose(ps[j][:, t * P:(t + 1) * P], vT[:, at:at + P], core.ident[:, :])
                        last.then_inc(s["v_turned"], 1)
                    for p in (8, 9):
                        piece(p)
                    pe.wait_ge(s["qk_done"], 5 * i + 5)
                    pe.wait_ge(s["v_done"], 3 * i + 3)
                    for qb in range(8):
                        score(qb, 0)
                        if qb > 4:
                            times_v(2 * (qb - 4) - 2)
                            turn(2 * (qb - 4) - 1)
                        score(qb, 1)
                        if qb > 4:
                            times_v(2 * (qb - 4) - 1)
                        if qb >= 4:
                            turn(2 * (qb - 4))
                    for n in range(6, STEPS):
                        if n + 1 < STEPS:
                            turn(n + 1)
                        times_v(n)
                        if n == 11:
                            squares(0)
                    squares(1)


def block_output(core, feat):
    nc, d, ps = core.nc, core.d, core.ps
    with Phase(core, "out") as ph:
        op = OutProjection(ph, core, feat, d["da_w_out"])
        x = ph.sb("x", [P, 2, D], F32)
        gt = ph.sb("gt_row", [P, D], F32)
        fg = ph.sb("final_gain", [P, D], F32)
        diag = ph.sb("gt_diag", [P, P], F32)
        ones = ph.sb("ones", [P, P], F32)
        ss = ph.sb("ss", [P, NT], F32)
        y = feat
        s_f = [ph.sem(f"feat{k}") for k in range(KT)]
        s_x = [ph.sem(f"x_loaded{b}") for b in range(2)]
        s_row, s_ss, s_ms, s_rt, s_step, s_diag, s_gm, s_y = (
            ph.sem(n) for n in ("row", "squares", "means", "roots", "step", "diag", "gt_mm", "y_ready"))
        s_t, s_out, s_g = ph.sem("scaled"), ph.sem("stored"), ph.sem("gt_copied")
        with nc.Block() as block:
            @block.sync
            def _(sync):
                op.sync(sync)

            @block.gpsimd
            def _(pool):
                for k in range(KT):
                    pool.dma_start(feat[:, k, :], d["o_feat"][k, :, :]).then_inc(s_f[k], 16)
                pool.dma_start(fg[:, :], d["final_gain"].partition_broadcast(P)).then_inc(s_row, 16)
                op.pool(pool)
                for t in range(NT):
                    if t >= 2:
                        pool.wait_ge(s_ss, t - 1)
                    pool.dma_start(x[:, t % 2, :], d["x3"][t, :, :]).then_inc(s_x[t % 2], 16)
                for t in range(NT):
                    pool.wait_ge(s_y, t + 1)
                    pool.dma_start(d["out"][t, :, :], y[:, t, :]).then_inc(s_out, 16)
                pool.wait_ge(s_out, 16 * NT)

            @block.scalar
            def _(act):
                op.act(act, lambda act, k: act.wait_ge(s_f[k], 16))
                for t in range(NT):
                    act.wait_ge(s_t, t + 1)
                    act.activation(x[:, t % 2, :], y[:, t, :], ACT.Square, accum_out=ss[:, t:t + 1]).then_inc(s_ss, 1)
                    act.wait_ge(s_ms, t + 1)
                    act.activation(ss[:, t:t + 1], ss[:, t:t + 1], ACT.Sqrt).then_inc(s_rt, 1)

            @block.vector
            def _(dve):
                dve.memset(ones[:, :], 1.0)
                for k in range(KT):
                    if k:
                        dve.wait_ge(s_gm, k)
                    dve.tensor_scalar(diag[:, :], core.ident[:, :], core.mods[:, 16 + k, 0:1], None, ALU.mult)\
                       .then_inc(s_diag, 1)
                dve.wait_ge(s_gm, KT)
                dve.tensor_copy(gt[:, :], core.psum[:, 0:D]).then_inc(s_g, 1)
                op.dve(dve)
                step = Steps(dve, s_step)
                dve.wait_ge(s_row, 16)
                for t in range(NT):
                    dve.wait_ge(op.mm, t + 1)
                    dve.wait_ge(s_x[t % 2], 16 * (t // 2) + 16)
                    dve.tensor_tensor(y[:, t, :], op.banks(t), gt[:, :], ALU.mult).then_inc(op.read, 1)
                    dve.wait_ge(op.read, t + 1)
                    dve.tensor_tensor(y[:, t, :], y[:, t, :], x[:, t % 2, :], ALU.add).then_inc(s_t, 1)
                    dve.wait_ge(s_ss, t + 1)
                    dve.tensor_scalar(ss[:, t:t + 1], ss[:, t:t + 1], 1.0 / D, EPS, ALU.mult, ALU.add).then_inc(s_ms, 1)
                    dve.wait_ge(s_rt, t + 1)
                    step(dve.reciprocal(ss[:, t:t + 1], ss[:, t:t + 1]))
                    dve.scalar_tensor_tensor(y[:, t, :], y[:, t, :], ss[:, t:t + 1], fg[:, :], ALU.mult, ALU.mult)\
                       .then_inc(s_y, 1)

            @block.tensor
            def _(pe):
                for k in range(KT):
                    pe.wait_ge(s_diag, k + 1)
                    pe.matmul(core.psum[:, k * P:(k + 1) * P], ones[:, :], diag[:, :], start=True, stop=True)\
                      .then_inc(s_gm, 1)
                pe.wait_ge(s_g, 1)
                op.pe(pe)


def program(nc, d, upto="out"):
    with ExitStack() as ctx:
        core = Core(nc, ctx, d)
        modulation(core)
        norm_of_input(core)
        with ExitStack() as first:
            mix = first.enter_context(nc.sbuf_tensor("mix", [P, KT, SEQ], F32))
            with ExitStack() as gates:
                tbase = gates.enter_context(nc.sbuf_tensor("gate_rows", [P, SEQ], F32))
                rf = gates.enter_context(nc.sbuf_tensor("gate_rows_key", [P, SEQ], F32R))
                with ExitStack() as decays:
                    la = decays.enter_context(nc.sbuf_tensor("log_decay", [P, 2, SEQ], F32))
                    gates_and_pool(core, mix, la, tbase, rf)
                    linear_attention(core, mix, la)
                forgetting_attention(core, mix, tbase, rf)
            mixer_output(core, mix)
        core.clear_semaphores()
        with ExitStack() as mlp:
            hid = mlp.enter_context(nc.sbuf_tensor("hid", [P, FT, SEQ], F32))
            gate_and_up(core, hid)
            down(core, hid)
        with ExitStack() as second:
            hc = [second.enter_context(nc.sbuf_tensor(n, [P, KT, CTX], F32R)) for n in ("hc_hi", "hc_lo")]
            context_norm(core, hc)
            differential_attention(core, hc)
        with ExitStack() as last:
            feat = last.enter_context(nc.sbuf_tensor("feat", [P, KT, SEQ], F32))
            block_output(core, feat)


def feature_tiles(w):
    k, n = w.shape[0] // P, w.shape[1] // P
    return np.ascontiguousarray(w.reshape(k, P, n, P).transpose(2, 1, 0, 3).reshape(n, P, k * P))


def column(v):
    return v.reshape(-1, P).T


def shape_constants():
    c = np.zeros((P, NK), np.float32)
    p = np.arange(P)
    c[:, K_ID:K_ID + P] = np.eye(P)
    c[:, K_BLK:K_BLK + P] = p[:, None] // DH == p[None, :] // DH
    c[:, K_NEG:K_NEG + P] = np.where(p[None, :] > p[:, None], np.float32(NEG), 0)
    for t in range(2):
        window = np.where(p < 64, (2, 8)[t], (4, 16)[t])
        c[:, K_INVC + 16 * t:K_INVC + 16 * t + 16] = 1.0 / np.minimum(np.arange(1, 17)[None, :], window[:, None])
        c[:, K_INVW + t] = 1.0 / window
    c[:, K_SEL:K_SEL + 8] = p[:, None] % 32 == np.arange(8)[None, :]
    same = (p[:, None] // CHUNK == p[None, :] // CHUNK) & (p[:, None] <= p[None, :])
    mask = np.tile(same.astype(np.uint32), (1, 4))
    n = np.arange(SEQ)
    inv = (np.float32(10000.0) ** (-np.arange(0, 32, 2, dtype=np.float32) / np.float32(32))).astype(np.float32)
    pos = np.stack([n // 64, n % 64]).astype(np.float32)
    ang = (pos[(p % 64) // 32][:, :] * inv[p % 16][:, None]).astype(np.float32)
    sign = np.where((p % 32) < 16, -1.0, 1.0).astype(np.float32)[:, None]
    rope = np.ascontiguousarray(np.stack([np.cos(ang), sign * np.sin(ang)], axis=1).astype(np.float32))
    return c, mask, rope


def layout(i):
    f = lambda n: np.asarray(i[n])
    a = {}
    w = f("w_in")[0]
    pad = lambda *blocks: np.concatenate(blocks, axis=1)
    zeros = lambda n: np.zeros((D, n), w.dtype)
    pool, gq, gk, gv, gg, ga, fq, fk, fv, ff = np.split(w, np.cumsum([256, 256, 256, 256, 256, 16, 512, 512, 512]), axis=1)
    tile = lambda m, j: m[:, j * P:(j + 1) * P]
    order = [pad(ga, zeros(16), ff, zeros(88)), pool]
    for j in range(2):
        order += [tile(m, j) for m in (gq, gk, gv, gg)]
    for j in range(4):
        order += [tile(m, j) for m in (fq, fk, fv)]
    a["w_in"] = feature_tiles(np.concatenate(order, axis=1))
    wp = np.zeros((P, 2, P), w.dtype)
    for g in range(4):
        r = slice((g % 2) * 64, (g % 2 + 1) * 64)
        wp[r, g // 2, r] = f("w_pool")[0, g]
    a["w_pool"] = wp
    a["w_a_up"] = np.ascontiguousarray(f("w_a_up")[0])
    a["w_o"] = f("w_o")[0].reshape(KT, P, D)
    gu = f("w_gu")[0]
    a["w_gu"] = feature_tiles(np.concatenate([tile(m, j) for j in range(FT) for m in (gu[:, :D_FF], gu[:, D_FF:])], axis=1))
    a["w_down"] = f("w_down")[0].reshape(FT, P, D)
    a["ada_w"] = feature_tiles(f("ada_w_2")[0])
    da = np.split(f("da_w_in_2")[0], 4, axis=1)
    a["da_w_in"] = feature_tiles(np.concatenate([tile(m, j) for j in range(HEADS2) for m in da], axis=1))
    a["da_w_out"] = f("da_w_out_2")[0].reshape(KT, P, D)
    bf = np.zeros(P, np.float32)
    bf[32:40] = f("b_f")[0]
    a["cols"] = np.ascontiguousarray(np.concatenate(
        [column(f(n).reshape(-1)) for n in ("ln1", "ln2", "norm_gain_2", "pool_scale", "b_a", "gla_gn", "ada_b_2",
                                            "da_subln_gain_2", "c_2", "c_ctx_2")] + [column(bf)], axis=1))
    a["lam_rows"] = np.ascontiguousarray(np.concatenate([f("da_lam_q_2")[0], f("da_lam_k_2")[0]], axis=0))
    a["ln_f"] = np.ascontiguousarray(f("ln_f"))
    a["final_gain"] = np.ascontiguousarray(f("final_gain_2"))
    a["x"] = f("x").reshape(NT, P, D)
    a["ctx"] = f("ctx_2").reshape(2, P, D)
    a["shape_consts"], a["gla_mask"], a["rope"] = shape_constants()
    return a


def kernel(**inputs):
    import concourse.bacc as bacc
    from concourse.bass_utils import run_bass_kernel_spmd

    nc = bacc.Bacc("TRN2", target_bir_lowering=False, num_devices=1)
    arrays = layout(inputs)
    d = {n: nc.dram_tensor(f"in_{n}", a.shape, mybir.dt.from_np(a.dtype), kind="ExternalInput").ap()
         for n, a in arrays.items()}
    for n in ("x1", "x3", "o_feat"):
        d[n] = nc.dram_tensor(f"kept_{n}", (NT, P, D), F32, kind="Internal").ap()
    d["out"] = nc.dram_tensor("out_0", (NT, P, D), F32, kind="ExternalOutput").ap()
    program(nc, d)
    r = run_bass_kernel_spmd(nc, [{f"in_{n}": a for n, a in arrays.items()}], core_ids=[0])
    return r.results[0]["out_0"].reshape(1, SEQ, D)
```

```python
import math
from contextlib import ExitStack

import numpy as np

import concourse.bass as bass
from concourse import mybir

F32 = mybir.dt.float32
F32R = mybir.dt.float32r
U32 = mybir.dt.uint32
ACT = mybir.ActivationFunctionType
ALU = mybir.AluOpType
AX = mybir.AxisListType

P = 128
D = 1024
KT = D // P
SEQ = 1024
NT = SEQ // P
HALF = SEQ // 2
CTX = 256
NKEY = SEQ + CTX
NKT = NKEY // P
DH = 64
HEADS2 = 8
D_FF = 2816
FT = D_FF // P
CHUNK = 64
NCH = SEQ // CHUNK
EPS = 1e-6
SUB_EPS = 1e-5
LAMBDA_INIT = 0.8 - 0.6 * math.exp(-0.3 * 0)
NEG = -2.0 ** 120

C_LN1, C_LN2, C_NG, C_POOL, C_BA, C_GN, C_ADA, C_SUB, C_C, C_CC, C_BF = 0, 8, 16, 24, 26, 28, 30, 54, 55, 63, 71
NCOLS = 72
K_ID, K_BLK, K_NEG, K_INVC, K_INVW, K_SEL = 0, 128, 256, 384, 416, 418
NK = 426


class Steps:

    def __init__(self, eng, sem, per=0, i=0):
        self.eng, self.sem, self.base, self.n, self.per = eng, sem, i * per, 0, per

    def __call__(self, ins):
        self.n += 1
        ins.then_inc(self.sem, 1)
        self.eng.wait_ge(self.sem, self.base + self.n)

    def end(self):
        assert self.n == self.per, (self.n, self.per)


class Core:

    def __init__(self, nc, ctx, dram):
        self.nc, self.ctx, self.d, self.sems = nc, ctx, dram, []
        self.hh = self.sb("h_hi", [P, KT, SEQ], F32R)
        self.hl = self.sb("h_lo", [P, KT, SEQ], F32R)
        self.raw = self.sb("w_raw", [P, 2, D], F32)
        self.wh = self.sb("w_hi", [P, 2, D], F32R)
        self.wl = self.sb("w_lo", [P, 2, D], F32R)
        self.cols = self.sb("cols_sb", [P, NCOLS], F32)
        self.ident = self.sb("ident", [P, P], F32)
        self.mods = self.sb("mods", [P, 24, 2], F32)
        self.eps = self.sb("eps_col", [P, 2], F32)
        self.neglam = self.sb("neglam", [P, 1], F32)
        self.subg = self.sb("subg", [P, 1], F32)
        self.psum = ctx.enter_context(nc.psum_tensor("psum", [P, 8 * 512], F32))
        self.ps = [self.psum[:, i * 512:(i + 1) * 512] for i in range(8)]

    def sb(self, name, shape, dt):
        return self.ctx.enter_context(self.nc.sbuf_tensor(name, shape, dt))

    def sem(self, name):
        self.sems.append(self.nc.alloc_semaphore(name))
        return self.sems[-1]

    def clear_semaphores(self):
        self.nc.clear_and_free_semaphores(self.sems)
        self.sems = []
        self.nc.all_engine_barrier()


class Phase:

    def __init__(self, core, name):
        self.core, self.name, self.stack = core, name, ExitStack()

    def __enter__(self):
        self.stack.__enter__()
        return self

    def __exit__(self, *a):
        return self.stack.__exit__(*a)

    def sb(self, name, shape, dt):
        return self.stack.enter_context(self.core.nc.sbuf_tensor(f"{self.name}_{name}", shape, dt))

    def sem(self, name):
        return self.core.sem(f"{self.name}_{name}")


class Weights:

    def __init__(self, ph, core, bufs, last, pieces):
        self.core, self.bufs, self.last, self.pieces = core, bufs, last, pieces
        self.loaded = [ph.sem(f"w_loaded{b}") for b in range(2)]
        self.hi = [ph.sem(f"w_hi{b}") for b in range(2)]
        self.lo = [ph.sem(f"w_lo{b}") for b in range(2)]
        self.piece_done = ph.sem("piece_done")
        self.uses = [max(bufs.count(b), 1) for b in range(2)]

    def nth(self, i, c):
        b = self.bufs[c]
        return i * self.uses[b] + self.bufs[:c].count(b)

    def load(self, sync, i, c, src):
        b = self.bufs[c]
        sync.wait_ge(self.lo[b], self.nth(i, c) + 1)
        sync.dma_start(self.core.raw[:, b, :], src).then_inc(self.loaded[b], 16)

    def round_hi(self, act, i, c):
        b = self.bufs[c]
        act.wait_ge(self.loaded[b], self.nth(i, c) * 16 + 16)
        before = [x for x in range(c) if self.bufs[x] == b]
        if before:
            act.wait_ge(self.piece_done, (i + 1) * self.pieces + self.last[before[-1]] + 1)
        else:
            final = [x for x in range(len(self.bufs)) if self.bufs[x] == b][-1]
            act.wait_ge(self.piece_done, i * self.pieces + self.last[final] + 1)
        act.activation(self.core.wh[:, b, :], self.core.raw[:, b, :], ACT.Copy).then_inc(self.hi[b], 1)

    def start_lo(self, pool):
        for b in range(2):
            pool.sem_inc(self.lo[b], 1)

    def subtract_lo(self, pool, i, c):
        b = self.bufs[c]
        pool.wait_ge(self.hi[b], self.nth(i, c) + 1)
        pool.tensor_tensor(self.core.wl[:, b, :], self.core.raw[:, b, :], self.core.wh[:, b, :].bitcast(F32),
                           ALU.subtract).then_inc(self.lo[b], 1)

    def start_pieces(self, pe):
        pe.sem_inc(self.piece_done, self.pieces)

    def wait_tile(self, pe, i, c):
        b = self.bufs[c]
        pe.wait_ge(self.lo[b], self.nth(i, c) + 2)

    def contract(self, pe, c, out, hi, lo, at, n, k):
        b = self.bufs[c]
        wh, wl = self.core.wh[:, b, k * P:(k + 1) * P], self.core.wl[:, b, k * P:(k + 1) * P]
        rh, rl = hi[:, k, at:at + n], lo[:, k, at:at + n]
        pe.matmul(out, wh, rh, start=(k == 0), stop=False)
        pe.matmul(out, wh, rl, start=False, stop=False)
        last = pe.matmul(out, wl, rh, start=False, stop=(k == KT - 1))
        if k == KT - 1:
            last.then_inc(self.piece_done, 1)

    def piece(self, pe, c, out, hi, lo, at, n):
        for k in range(KT):
            self.contract(pe, c, out, hi, lo, at, n, k)

    def done(self, i, p):
        return (i + 1) * self.pieces + p + 1


class Transposes:

    def __init__(self, ph, core, y, hi, lo, groups, width, gain, bias=None):
        self.core, self.y, self.hi_t, self.lo_t = core, y, hi, lo
        self.groups, self.width, self.gain, self.bias = groups, width, gain, bias
        self.ready = ph.sem("y_ready")
        self.turned = ph.sem("h_turned")
        self.hi = ph.sem("h_hi")
        self.lo = ph.sem("h_lo")
        self.tmp_done = ph.sem("h_tmp")
        self.tmp = ph.sb("h_tmp", [P, 2, width * P], F32) if bias else None

    def pe(self, pe, g):
        pe.wait_ge(self.ready, g + 1)
        for k in range(KT):
            n = g * KT + k
            if n >= 4:
                pe.wait_ge(self.lo, n - 3)
            for t in range(self.width):
                last = pe.transpose(self.core.ps[n % 4][:, t * P:(t + 1) * P],
                                    self.y[:, g * self.width + t, k * P:(k + 1) * P], self.core.ident[:, :])
            last.then_inc(self.turned, 1)

    def act(self, act, g):
        w = self.width * P
        for k in range(KT):
            n = g * KT + k
            act.wait_ge(self.turned, n + 1)
            act.activation(self.hi_t[:, k, g * w:(g + 1) * w], self.core.ps[n % 4][:, 0:w], ACT.Identity,
                           scale=self.gain(k), bias=self.bias(k) if self.bias else 0.0).then_inc(self.hi, 1)

    def dve(self, dve, g):
        w = self.width * P
        for k in range(KT):
            n = g * KT + k
            dve.wait_ge(self.hi, n + 1)
            src, hi, lo = self.core.ps[n % 4][:, 0:w], self.hi_t[:, k, g * w:(g + 1) * w], self.lo_t[:, k, g * w:(g + 1) * w]
            if self.bias:
                if n >= 2:
                    dve.wait_ge(self.lo, n - 1)
                dve.tensor_scalar(self.tmp[:, n % 2, :], src, self.gain(k), self.bias(k), ALU.mult, ALU.add)\
                   .then_inc(self.tmp_done, 1)
                dve.wait_ge(self.tmp_done, n + 1)
                dve.tensor_tensor(lo, self.tmp[:, n % 2, :], hi.bitcast(F32), ALU.subtract).then_inc(self.lo, 1)
            else:
                dve.scalar_tensor_tensor(lo, src, self.gain(k), hi.bitcast(F32), ALU.mult, ALU.subtract)\
                   .then_inc(self.lo, 1)


def modulation(core):
    nc, d = core.nc, core.d
    with Phase(core, "mod") as ph:
        cs = ph.sb("silu_c", [P, KT, 2], F32)
        lamr = ph.sb("lam_rows", [P, 4, DH], F32)
        lam = ph.sb("lam", [P, 8], F32)
        s_in, s_c, s_lam, s_lamsum, s_lamexp = (ph.sem(n) for n in ("in", "silu", "lam", "lam_sums", "lam_exp"))
        s_loaded = [ph.sem(f"loaded{b}") for b in range(2)]
        s_mm, s_ev, s_step, s_ready = ph.sem("mm"), ph.sem("read"), ph.sem("step"), ph.sem("ready")
        with nc.Block() as block:
            @block.sync
            def _(sync):
                sync.dma_start(core.cols[:, :], d["cols"]).then_inc(s_in, 16)
                sync.dma_start(core.ident[:, :], d["shape_consts"][:, K_ID:K_ID + P]).then_inc(s_in, 16)
                sync.dma_start(lamr[:, :, :], d["lam_rows"].partition_broadcast(P)).then_inc(s_in, 16)
                with sync.Fori(0, 12) as i:
                    for b in range(2):
                        sync.wait_ge(s_mm, i * 2 + b + 1)
                        sync.dma_start(core.raw[:, b, :], d["ada_w"][2 * i + b, :, :]).then_inc(s_loaded[b], 16)

            @block.scalar
            def _(act):
                act.wait_ge(s_in, 48)
                act.activation(cs[:, :, 0], core.cols[:, C_C:C_C + KT], ACT.Silu).then_inc(s_c, 1)
                act.activation(cs[:, :, 1], core.cols[:, C_CC:C_CC + KT], ACT.Silu).then_inc(s_c, 1)
                act.wait_ge(s_lamsum, 1)
                act.activation(lam[:, 2:4], lam[:, 0:2], ACT.Exp).then_inc(s_lamexp, 1)

            @block.tensor
            def _(pe):
                pe.wait_ge(s_c, 2)
                pe.sem_inc(s_mm, 2)
                with pe.Fori(0, 12) as i:
                    for b in range(2):
                        pe.wait_ge(s_loaded[b], i * 16 + 16)
                        pe.wait_ge(s_ev, i * 2 + b + 1)
                        for k in range(KT):
                            last = pe.matmul(core.ps[b][:, 0:2], core.raw[:, b, k * P:(k + 1) * P], cs[:, k, :],
                                             start=(k == 0), stop=(k == KT - 1))
                        last.then_inc(s_mm, 1)

            @block.vector
            def _(dve):
                step = Steps(dve, s_step)
                dve.sem_inc(s_ev, 2)
                dve.memset(core.eps[:, 0:1], EPS)
                step(dve.memset(core.eps[:, 1:2], SUB_EPS))
                dve.wait_ge(s_in, 48)
                step(dve.tensor_tensor(lamr[:, 0:2, :], lamr[:, 0:2, :], lamr[:, 2:4, :], ALU.mult))
                dve.tensor_reduce(lam[:, 0:2], lamr[:, 0:2, :], AX.X, ALU.add).then_inc(s_lamsum, 1)
                dve.wait_ge(s_lamexp, 1)
                step(dve.tensor_tensor(lam[:, 4:5], lam[:, 3:4], lam[:, 2:3], ALU.subtract))
                step(dve.tensor_scalar(core.neglam[:, :], lam[:, 4:5], -LAMBDA_INIT, None, ALU.add))
                step(dve.tensor_scalar(core.subg[:, :], core.cols[:, C_SUB:C_SUB + 1], 1.0 - LAMBDA_INIT, None, ALU.mult))
                with dve.Fori(0, 12) as i:
                    for b in range(2):
                        dve.wait_ge(s_mm, i * 2 + b + 3)
                        dve.tensor_copy(core.mods[:, 2 * i + b, :], core.ps[b][:, 0:2]).then_inc(s_ev, 1)
                dve.wait_ge(s_ev, 26)
                for j in range(2):
                    last = dve.tensor_tensor(core.mods[:, :, j], core.mods[:, :, j], core.cols[:, C_ADA:C_ADA + 24], ALU.add)
                step(last)
                for j in range(2):
                    last = dve.scalar_tensor_tensor(core.mods[:, 8:16, j], core.mods[:, 8:16, j], 1.0,
                                                    core.cols[:, C_NG:C_NG + KT], ALU.add, ALU.mult)
                step(last)


def norm_of_input(core):
    nc, d = core.nc, core.d
    with Phase(core, "in") as ph:
        y = ph.sb("y", [P, NT, D], F32)
        sq = ph.sb("sq", [P, D], F32)
        ss = ph.sb("ss", [P, NT], F32)
        s_x = [ph.sem(f"x{t}") for t in range(NT)]
        s_ss, s_ms, s_rt, s_step = ph.sem("squares"), ph.sem("means"), ph.sem("roots"), ph.sem("step")
        tr = Transposes(ph, core, y, core.hh, core.hl, 2, 4, lambda k: core.cols[:, C_LN1 + k:C_LN1 + k + 1])
        with nc.Block() as block:
            @block.sync
            def _(sync):
                for t in range(NT):
                    sync.dma_start(y[:, t, :], d["x"][t, :, :]).then_inc(s_x[t], 16)

            @block.scalar
            def _(act):
                for g in range(2):
                    for t in range(4 * g, 4 * g + 4):
                        act.wait_ge(s_x[t], 16)
                        act.activation(sq[:, :], y[:, t, :], ACT.Square, accum_out=ss[:, t:t + 1]).then_inc(s_ss, 1)
                        act.wait_ge(s_ss, t + 1)
                for g in range(2):
                    act.wait_ge(s_ms, g + 1)
                    act.activation(ss[:, 4 * g:4 * g + 4], ss[:, 4 * g:4 * g + 4], ACT.Sqrt).then_inc(s_rt, 1)
                    tr.act(act, g)

            @block.vector
            def _(dve):
                step = Steps(dve, s_step)
                for g in range(2):
                    c = slice(4 * g, 4 * g + 4)
                    dve.wait_ge(s_ss, 4 * g + 4)
                    dve.tensor_scalar(ss[:, c], ss[:, c], 1.0 / D, EPS, ALU.mult, ALU.add).then_inc(s_ms, 1)
                    dve.wait_ge(s_rt, g + 1)
                    step(dve.reciprocal(ss[:, c], ss[:, c]))
                    for t in range(4 * g, 4 * g + 4):
                        last = dve.tensor_scalar(y[:, t, :], y[:, t, :], ss[:, t:t + 1], None, ALU.mult)
                    last.then_inc(tr.ready, 1)
                    tr.dve(dve, g)

            @block.tensor
            def _(pe):
                for g in range(2):
                    tr.pe(pe, g)


def gates_and_pool(core, mix, la, tbase, rf):
    nc, d, ps = core.nc, core.d, core.ps
    with Phase(core, "gate") as ph:
        gaf = ph.sb("gaf", [P, SEQ], F32)
        u = ph.sb("u", [P, 2, SEQ], F32)
        pa = ph.sb("pool_a", [P, SEQ], F32)
        pb = ph.sb("pool_b", [P, SEQ], F32)
        wp = ph.sb("w_pool", [P, 2, P], F32)
        wa = ph.sb("w_a_up", [16, 2 * P], F32)
        kc = ph.sb("kc", [P, 34], F32)
        ab = ph.sb("abs", [P, HALF], F32)
        fl = ph.sb("logf", [P, 2, SEQ], F32)
        one = ph.sb("one", [P, SEQ], F32)
        ws = Weights(ph, core, [0, 1, 0], [1, 3, 5], 6)
        s_c, s_gaf, s_u, s_pool = ph.sem("consts"), ph.sem("gaf_copied"), ph.sem("u_copied"), ph.sem("pool_step")
        s_pooled, s_pm, s_pev = ph.sem("pooled"), ph.sem("pool_mm"), ph.sem("pool_out")
        s_lm, s_lact, s_ldve = ph.sem("la_mm"), ph.sem("la_act"), ph.sem("la_dve")
        s_f, s_fact = ph.sem("f_step"), ph.sem("f_act")
        with nc.Block() as block:
            @block.sync
            def _(sync):
                for c in range(3):
                    ws.load(sync, 0, c, d["w_in"][c, :, :])
                    if c == 1:
                        sync.dma_start(wp[:, :, :], d["w_pool"]).then_inc(s_c, 16)
                        sync.dma_start(wa[:, :], d["w_a_up"]).then_inc(s_c, 16)
                        sync.dma_start(kc[:, :], d["shape_consts"][:, K_INVC:K_INVC + 34]).then_inc(s_c, 16)

            @block.scalar
            def _(act):
                ws.round_hi(act, 0, 0)
                ws.round_hi(act, 0, 1)
                for p in range(2):
                    act.wait_ge(ws.piece_done, ws.done(0, p))
                    act.activation(gaf[:, p * HALF:(p + 1) * HALF], ps[6 + p % 2][:, :], ACT.Copy).then_inc(s_gaf, 1)
                ws.round_hi(act, 0, 2)
                for n, (func, scale, bias) in enumerate(((ACT.Abs, 1.0, core.cols[32:40, C_BF:C_BF + 1]),
                                                         (ACT.Exp, -1.0, 0.0), (ACT.Ln, 1.0, 1.0))):
                    act.wait_ge(s_gaf, 2) if n == 0 else act.wait_ge(s_fact, n)
                    act.activation(fl[32:40, 0, :], gaf[32:40, :] if n == 0 else fl[32:40, 0, :], func,
                                   bias=bias, scale=scale).then_inc(s_fact, 1)
                for p in range(2, 6):
                    act.wait_ge(ws.piece_done, ws.done(0, p))
                    act.activation(u[:, (p - 2) // 2, (p % 2) * HALF:(p % 2 + 1) * HALF], ps[6 + p % 2][:, :],
                                   ACT.Copy).then_inc(s_u, 1)
                for n in range(4):
                    pr, hf = n // 2, n % 2
                    act.wait_ge(s_lm, n + 1)
                    if n:
                        act.wait_ge(s_ldve, 2 * n)
                    for m, (func, scale, bias) in enumerate(((ACT.Abs, 1.0, core.cols[:, C_BA + pr:C_BA + pr + 1]),
                                                             (ACT.Exp, -1.0, 0.0), (ACT.Ln, 1.0, 1.0))):
                        act.activation(ab[:, :], ps[n][:, :] if m == 0 else ab[:, :], func, bias=bias, scale=scale)\
                           .then_inc(s_lact, 1)
                        act.wait_ge(s_lact, 3 * n + m + 1)
                for n in range(4):
                    c, hf = n // 2, n % 2
                    act.wait_ge(s_pm, n + 1)
                    act.activation(mix[:, c, hf * HALF:(hf + 1) * HALF], ps[4 + n % 2][:, :], ACT.Copy,
                                   scale=core.cols[:, C_POOL + c:C_POOL + c + 1]).then_inc(s_pev, 1)

            @block.vector
            def _(dve):
                f = Steps(dve, s_f)
                dve.memset(one[:, :], 1.0)
                dve.memset(tbase[:, :], 0.0)
                f(dve.memset(rf[:, :].bitcast(F32), 0.0))
                for q in (0, 64):
                    dve.memset(tbase[q:q + 8, :], 1.0)
                    last = dve.memset(rf[q + 32:q + 40, :].bitcast(F32), 1.0)
                f(last)
                dve.wait_ge(s_gaf, 2)
                f(dve.tensor_scalar(fl[32:40, 1, :], gaf[32:40, :], core.cols[32:40, C_BF:C_BF + 1], 0.0, ALU.add, ALU.min))
                dve.wait_ge(s_fact, 3)
                f(dve.tensor_tensor(fl[32:40, 1, :], fl[32:40, 1, :], fl[32:40, 0, :], ALU.subtract))
                f(dve.tensor_tensor_scan(fl[32:40, 0, :], one[32:40, :], fl[32:40, 1, :], 0.0, ALU.mult, ALU.add))
                f(dve.tensor_scalar(rf[0:8, :], fl[32:40, 0, :], -1.0, None, ALU.mult))
                f(dve.tensor_scalar(tbase[32:40, :], rf[0:8, :].bitcast(F32), -1.0, None, ALU.mult))
                f(dve.tensor_tensor(tbase[96:104, :], fl[32:40, 0, :], tbase[32:40, :], ALU.subtract))
                f(dve.tensor_scalar(rf[64:72, :], tbase[96:104, :], -1.0, None, ALU.mult))
                for n in range(4):
                    pr, hf = n // 2, n % 2
                    dst = la[:, pr, hf * HALF:(hf + 1) * HALF]
                    dve.wait_ge(s_lact, 3 * n + 3)
                    dve.tensor_scalar(dst, ps[n][:, :], core.cols[:, C_BA + pr:C_BA + pr + 1], 0.0, ALU.add, ALU.min)\
                       .then_inc(s_ldve, 1)
                    dve.wait_ge(s_ldve, 2 * n + 1)
                    dve.tensor_tensor(dst, dst, ab[:, :], ALU.subtract).then_inc(s_ldve, 1)

            @block.gpsimd
            def _(pool):
                ws.start_lo(pool)
                for c in range(3):
                    ws.subtract_lo(pool, 0, c)
                step = Steps(pool, s_pool)
                pool.wait_ge(s_c, 48)
                for c in range(2):
                    pool.wait_ge(s_u, 2 * c + 2)
                    src = u[:, c, :]
                    spans = ((1, 0), (2, 64)) if c == 0 else ((1, 0), (2, 0), (4, 0), (8, 64))
                    bufs = (pa, pb)
                    for n, (lag, q) in enumerate(spans):
                        dst = bufs[n % 2]
                        pool.tensor_copy(dst[q:P, 0:lag], src[q:P, 0:lag])
                        if q:
                            pool.tensor_copy(dst[0:q, :], src[0:q, :])
                        step(pool.tensor_tensor(dst[q:P, lag:SEQ], src[q:P, lag:SEQ], src[q:P, 0:SEQ - lag], ALU.add))
                        src = dst
                    dst = bufs[len(spans) % 2]
                    pool.tensor_tensor(dst[:, 0:16], src[:, 0:16], kc[:, 16 * c:16 * c + 16], ALU.mult)
                    step(pool.tensor_scalar(dst[:, 16:SEQ], src[:, 16:SEQ], kc[:, 32 + c:33 + c], 1.0, ALU.mult, ALU.mult))
                    step(pool.tensor_tensor(u[:, c, :], dst[:, :], u[:, c, :], ALU.subtract))
                    pool.sem_inc(s_pooled, 1)

            @block.tensor
            def _(pe):
                ws.start_pieces(pe)
                for p in range(6):
                    if p % 2 == 0:
                        ws.wait_tile(pe, 0, p // 2)
                    if p in (2, 3):
                        pe.wait_ge(s_gaf, p - 1)
                    if p in (4, 5):
                        pe.wait_ge(s_u, p - 3)
                    ws.piece(pe, p // 2, ps[6 + p % 2][:, :], core.hh, core.hl, (p % 2) * HALF, HALF)
                pe.wait_ge(s_c, 48)
                pe.wait_ge(s_gaf, 2)
                for n in range(4):
                    pr, hf = n // 2, n % 2
                    pe.matmul(ps[n][:, :], wa[:, pr * P:(pr + 1) * P], gaf[0:16, hf * HALF:(hf + 1) * HALF],
                              start=True, stop=True).then_inc(s_lm, 1)
                for n in range(4):
                    c, hf = n // 2, n % 2
                    pe.wait_ge(s_pooled, c + 1)
                    if n >= 2:
                        pe.wait_ge(s_pev, n - 1)
                    pe.matmul(ps[4 + n % 2][:, :], wp[:, c, :], u[:, c, hf * HALF:(hf + 1) * HALF],
                              start=True, stop=True).then_inc(s_pm, 1)


def linear_attention(core, mix, la):
    nc, d, ps = core.nc, core.d, core.ps
    with Phase(core, "gla") as ph:
        qkvg = ph.sb("qkvg", [P, 2, 4, SEQ], F32)
        e = ph.sb("exps", [P, SEQ], F32)
        qi = ph.sb("q_in", [P, SEQ], F32)
        qx = ph.sb("q_x", [P, SEQ], F32)
        ki = ph.sb("k_in", [P, SEQ], F32)
        kd = ph.sb("k_dec", [P, SEQ], F32)
        kdt = ph.sb("k_dec_tok", [P, NT, P], F32)
        vt = ph.sb("v_tok", [P, NT, P], F32)
        att = ph.sb("att", [P, 2, NT, P], F32)
        dec = ph.sb("dec", [P, NCH], F32)
        blk = ph.sb("blk", [P, P], F32)
        msk = ph.sb("mask", [P, 512], U32)
        ob, sq = qi, qx
        reset = e
        state = lambda pr: chunks(la[:, pr, :])
        ws = Weights(ph, core, [0, 1] * 4, [2 * c + 1 for c in range(8)], 16)
        s_c, s_ev, s_att0 = ph.sem("consts"), ph.sem("copied"), ph.sem("att_zeroed")
        s_dve, s_exp, s_tm, s_tev = ph.sem("dve_step"), ph.sem("exps"), ph.sem("turned"), ph.sem("turned_copied")
        s_arg, s_prod = ph.sem("exp_args"), ph.sem("products")
        s_am, s_aev, s_kv, s_st = ph.sem("att_mm"), ph.sem("att_masked"), ph.sem("kv_mm"), ph.sem("state_step")
        s_om, s_oev, s_sm, s_rs, s_y = ph.sem("o_mm"), ph.sem("o_act"), ph.sem("squares_mm"), ph.sem("rstd"), ph.sem("y_step")
        chunks = lambda ap: ap.rearrange("p (n c) -> p n c", c=CHUNK)
        with nc.Block() as block:
            @block.sync
            def _(sync):
                sync.dma_start(blk[:, :], d["shape_consts"][:, K_BLK:K_BLK + P]).then_inc(s_c, 16)
                sync.dma_start(msk[:, :], d["gla_mask"]).then_inc(s_c, 16)
                for c in range(8):
                    ws.load(sync, 0, c, d["w_in"][3 + c, :, :])

            @block.scalar
            def _(act):
                def copies(c):
                    for hf in range(2):
                        p = 2 * c + hf
                        act.wait_ge(ws.piece_done, ws.done(0, p))
                        act.activation(qkvg[:, c // 4, c % 4, hf * HALF:(hf + 1) * HALF], ps[6 + p % 2][:, :],
                                       ACT.Silu if c % 4 == 3 else ACT.Copy).then_inc(s_ev, 1)

                def exps(pr):
                    bc = la[:, pr, :]
                    for n, (src, scale) in enumerate(((e, 1.0), (e, -1.0), (e, 1.0), (bc, 1.0))):
                        if n < 3:
                            act.wait_ge(s_arg, 4 * pr + n + 1)
                        else:
                            act.wait_ge(s_prod, pr + 1)
                        dst = kd if n < 2 else e
                        act.wait_ge(s_exp, 5 * pr + n) if 5 * pr + n else None
                        act.activation(dst[:, :], src[:, :] if n < 3 else bc, ACT.Exp, scale=scale / 16.0).then_inc(s_exp, 1)
                    act.activation(dec[:, :], chunks(bc)[:, :, CHUNK - 1], ACT.Exp, scale=1.0 / 16.0).then_inc(s_exp, 1)

                def finish(pr):
                    for n in range(2):
                        act.wait_ge(s_om, 2 * pr + n + 1)
                        s = slice(n * HALF, (n + 1) * HALF)
                        act.activation(ob[:, s], ps[6 + n][:, :], ACT.Copy).then_inc(s_oev, 1)
                        act.activation(sq[:, s], ps[6 + n][:, :], ACT.Square).then_inc(s_oev, 1)
                    for n in range(2):
                        s = slice(n * HALF, (n + 1) * HALF)
                        act.wait_ge(s_sm, 2 * pr + n + 1)
                        act.activation(e[:, s], ps[4 + n][:, :], ACT.Ln, scale=1.0 / DH, bias=core.eps[:, 0:1]).then_inc(s_rs, 1)
                        act.wait_ge(s_rs, 4 * pr + 2 * n + 1)
                        act.activation(e[:, s], e[:, s], ACT.Exp, scale=-0.5).then_inc(s_rs, 1)

                act.wait_ge(s_c, 32)
                for c in range(8):
                    ws.round_hi(act, 0, c)
                    if c:
                        copies(c - 1)
                copies(7)
                for pr in range(2):
                    exps(pr)
                    finish(pr)

            @block.gpsimd
            def _(pool):
                ws.start_lo(pool)
                pool.memset(att[:, :, :, :], 0.0).then_inc(s_att0, 1)
                for c in range(8):
                    ws.subtract_lo(pool, 0, c)

            @block.vector
            def _(dve):
                step = Steps(dve, s_dve)
                step(dve.memset(reset[:, :], 1.0))
                step(dve.memset(chunks(reset[:, :])[:, :, 0:1], 0.0))
                for pr in range(2):
                    step(dve.tensor_tensor_scan(la[:, pr, :], reset[:, :], la[:, pr, :], 0.0, ALU.mult, ALU.add))
                for pr in range(2):
                    bc = la[:, pr, :]
                    q, k = qkvg[:, pr, 0, :], qkvg[:, pr, 1, :]
                    at = lambda col: chunks(bc)[:, :, col:col + 1].to_broadcast([P, NCH, CHUNK])
                    dve.tensor_tensor(chunks(e[:, :]), chunks(bc), at(CHUNK // 2 - 1), ALU.subtract).then_inc(s_arg, 1)
                    dve.wait_ge(s_ev, 8 * pr + 4)
                    dve.wait_ge(s_exp, 5 * pr + 1)
                    dve.scalar_tensor_tensor(qi[:, :], q, DH ** -0.5, kd[:, :], ALU.mult, ALU.mult).then_inc(s_arg, 1)
                    dve.wait_ge(s_exp, 5 * pr + 2)
                    step(dve.tensor_tensor(ki[:, :], k, kd[:, :], ALU.mult))
                    dve.tensor_tensor(chunks(e[:, :]), at(CHUNK - 1), chunks(bc), ALU.subtract).then_inc(s_arg, 1)
                    dve.wait_ge(s_exp, 5 * pr + 3)
                    dve.tensor_tensor(kd[:, :], k, e[:, :], ALU.mult).then_inc(s_prod, 1)
                    dve.wait_ge(s_exp, 5 * pr + 4)
                    dve.scalar_tensor_tensor(qx[:, :], q, DH ** -0.5, e[:, :], ALU.mult, ALU.mult).then_inc(s_arg, 1)
                    dve.wait_ge(s_att0, 1)
                    for n in range(4):
                        dve.wait_ge(s_tm, 4 * pr + n + 1)
                        dst = (kdt, vt)[n // 2][:, (n % 2) * 4:(n % 2) * 4 + 4, :]
                        dve.tensor_copy(dst, ps[n][:, :].rearrange("p (t m) -> p t m", t=4)).then_inc(s_tev, 1)
                    for n in range(4):
                        dve.wait_ge(s_am, 4 * pr + n + 1)
                        dve.copy_predicated(att[:, n // 2, (n % 2) * 4:(n % 2) * 4 + 4, :].rearrange("p t m -> p (t m)"),
                                            msk[:, :], ps[n][:, :]).then_inc(s_aev, 1)
                    dve.wait_ge(s_exp, 5 * pr + 5)
                    st = state(pr)
                    step(dve.memset(st[:, 0, :], 0.0))
                    for n in range(NCH - 1):
                        if n % 8 == 0:
                            dve.wait_ge(s_kv, 4 * pr + n // 4 + 2)
                        bank, c0 = ps[2 * (n // 8) + n % 2], n % 8 // 2 * P
                        for h in range(2):
                            r = slice(h * DH, (h + 1) * DH)
                            last = dve.scalar_tensor_tensor(
                                st[r, n + 1, :], st[r, n, :], dec[r, n:n + 1],
                                bank[r, c0 + h * DH:c0 + (h + 1) * DH], ALU.mult, ALU.add)
                        last.then_inc(s_st, 1)
                        dve.wait_ge(s_st, 15 * pr + n + 1)
                    for n in range(2):
                        s = slice(n * HALF, (n + 1) * HALF)
                        y = mix[:, 2 + pr, s]
                        dve.wait_ge(s_rs, 4 * pr + 2 * n + 2)
                        dve.scalar_tensor_tensor(y, ob[:, s], core.cols[:, C_GN + pr:C_GN + pr + 1], e[:, s],
                                                 ALU.mult, ALU.mult).then_inc(s_y, 1)
                        dve.wait_ge(s_y, 4 * pr + 2 * n + 1)
                        dve.tensor_tensor(y, y, qkvg[:, pr, 3, s], ALU.mult).then_inc(s_y, 1)
                        dve.wait_ge(s_y, 4 * pr + 2 * n + 2)

            @block.tensor
            def _(pe):
                ws.start_pieces(pe)
                for p in range(16):
                    if p % 2 == 0:
                        ws.wait_tile(pe, 0, p // 2)
                    if p >= 2:
                        pe.wait_ge(s_ev, p - 1)
                    ws.piece(pe, p // 2, ps[6 + p % 2][:, :], core.hh, core.hl, (p % 2) * HALF, HALF)
                for pr in range(2):
                    if pr == 0:
                        pe.wait_ge(s_ev, 16)
                    pe.wait_ge(s_prod, pr + 1)
                    if pr:
                        pe.wait_ge(s_st, 15)
                    for n in range(4):
                        src = kd[:, :] if n < 2 else qkvg[:, pr, 2, :]
                        for t in range(4):
                            at = ((n % 2) * 4 + t) * P
                            last = pe.transpose(ps[n][:, t * P:(t + 1) * P], src[:, at:at + P], core.ident[:, :])
                        last.then_inc(s_tm, 1)
                    pe.wait_ge(s_arg, 4 * pr + 4)
                    for n in range(4):
                        pe.wait_ge(s_tev, 4 * pr + n + 1)
                        r = slice((n // 2) * DH, (n // 2 + 1) * DH)
                        for t in range(4):
                            at = ((n % 2) * 4 + t) * P
                            last = pe.matmul(ps[n][:, t * P:(t + 1) * P], ki[r, at:at + P], qi[r, at:at + P],
                                             start=True, stop=True)
                        last.then_inc(s_am, 1)
                    for n in range(4):
                        pe.wait_ge(s_aev, 4 * pr + n + 1)
                        for c in range(4):
                            ch = 8 * (n // 2) + 2 * c + n % 2
                            r = slice((ch % 2) * CHUNK, (ch % 2 + 1) * CHUNK)
                            last = pe.matmul(ps[n][:, c * P:(c + 1) * P], kdt[r, ch // 2, :], vt[r, ch // 2, :],
                                             start=True, stop=True)
                        last.then_inc(s_kv, 1)
                    if pr:
                        pe.wait_ge(s_rs, 4)
                    st = state(pr)
                    for hf in range(2):
                        pe.wait_ge(s_st, 15 * pr + 7 + 8 * hf)
                        for h in range(2):
                            r = slice(h * DH, (h + 1) * DH)
                            for t in range(4 * hf, 4 * hf + 4):
                                o = ps[6 + hf][r, (t % 4) * P:(t % 4 + 1) * P]
                                pe.matmul(o, vt[:, t, r], att[:, h, t, :], start=True, stop=False)
                                for c in range(2):
                                    ch = 2 * t + c
                                    last = pe.matmul(ps[6 + hf][r, (ch % 8) * CHUNK:(ch % 8 + 1) * CHUNK], st[r, ch, :],
                                                     qx[r, ch * CHUNK:(ch + 1) * CHUNK], start=False, stop=(c == 1))
                        last.then_inc(s_om, 1)
                    for n in range(2):
                        pe.wait_ge(s_oev, 4 * pr + 2 * n + 2)
                        pe.matmul(ps[4 + n][:, :], blk[:, :], sq[:, n * HALF:(n + 1) * HALF], start=True, stop=True)\
                          .then_inc(s_sm, 1)


def forgetting_attention(core, mix, tbase, rf):
    nc, d, ps = core.nc, core.d, core.ps
    PAIRS, UNITS = 4, 16
    with Phase(core, "fox") as ph:
        q = [ph.sb(n, [P, SEQ], F32R) for n in ("q_hi", "q_lo")]
        k = [ph.sb(n, [P, SEQ], F32R) for n in ("k_hi", "k_lo")]
        v = [ph.sb(n, [P, NT, P], F32R) for n in ("v_hi", "v_lo")]
        vT = ph.sb("v_feat", [P, SEQ], F32)
        th = ph.sb("f_rows", [P, SEQ], F32R)
        pe_s = ph.sb("p_small", [P, 4, HALF], F32)
        pe_l = ph.sb("p_large", [P, 4, SEQ], F32)
        pt = [ph.sb(n, [P, 2, HALF], F32R) for n in ("pt_hi", "pt_lo")]
        sel = ph.sb("sel", [P, 8, 1], F32)
        idr = ph.sb("ident_r", [P, P], F32R)
        ngr = ph.sb("causal_r", [P, P], F32R)
        cst = ph.sb("causal", [P, P], F32)
        nm = ph.sb("neg_max", [P, 2], F32)
        rs = ph.sb("row_sum", [P, 2], F32)
        ws = Weights(ph, core, [0, 1, 0], [1, 3, 5], 6)
        names = ("consts consts_r q_hi k_hi q_done k_done v_copied v_turned v_hi v_done f_rows scored maxed probs recips scaled "
                 "pt_turned pt_hi pt_lo pv_done o_read")
        s = {n: ph.sem(n) for n in names.split()}
        nkt = (4, 8)
        nth_pt = lambda i, h, g, kt: i * 24 + h * 12 + g * 4 + kt
        def slot(qb):
            return pe_s[:, qb, :] if qb < 4 else pe_l[:, qb - 4, :]
        with nc.Block() as block:
            @block.sync
            def _(sync):
                sync.dma_start(sel[:, :, 0], d["shape_consts"][:, K_SEL:K_SEL + 8]).then_inc(s["consts"], 16)
                sync.dma_start(cst[:, :], d["shape_consts"][:, K_NEG:K_NEG + P]).then_inc(s["consts"], 16)
                with sync.Fori(0, PAIRS) as i:
                    for c in range(3):
                        ws.load(sync, i, c, d["w_in"][11 + 3 * i + c, :, :])

            @block.gpsimd
            def _(pool):
                ws.start_lo(pool)
                pool.sem_inc(s["scaled"], 2)
                with pool.Fori(0, PAIRS) as i:
                    for c in range(3):
                        ws.subtract_lo(pool, i, c)
                    for h in range(2):
                        for qb in range(8):
                            u = i * UNITS + h * 8 + qb
                            n = (qb + 1) * P
                            pool.wait_ge(s["recips"], u + 1)
                            pool.nop(nofuse=True)
                            pool.tensor_scalar(slot(qb)[:, 0:n], slot(qb)[:, 0:n], rs[:, qb % 2:qb % 2 + 1], 1.0,
                                               ALU.mult, ALU.mult).then_inc(s["scaled"], 1)

            @block.scalar
            def _(act):
                act.sem_inc(s["probs"], 2)
                act.wait_ge(s["consts"], 32)
                act.activation(idr[:, :], core.ident[:, :], ACT.Copy)
                act.activation(ngr[:, :], cst[:, :], ACT.Copy).then_inc(s["consts_r"], 1)
                with act.Fori(0, PAIRS) as i:
                    def split_hi(p, dst, scale, name):
                        act.wait_ge(ws.piece_done, ws.done(i, p))
                        act.activation(dst[:, (p % 2) * HALF:(p % 2 + 1) * HALF], ps[6 + p % 2][:, :], ACT.Copy,
                                       scale=scale).then_inc(s[name], 1)
                    ws.round_hi(act, i, 0)
                    ws.round_hi(act, i, 1)
                    for p in range(2):
                        split_hi(p, q[0], DH ** -0.5, "q_hi")
                    ws.round_hi(act, i, 2)
                    for p in range(2, 4):
                        split_hi(p, k[0], 1.0, "k_hi")
                    for p in range(4, 6):
                        split_hi(p, vT, 1.0, "v_copied")
                    for n in range(2):
                        act.wait_ge(s["v_turned"], 2 * i + n + 1)
                        act.activation(v[0][:, 4 * n:4 * n + 4, :], ps[n][:, :].rearrange("p (t m) -> p t m", t=4),
                                       ACT.Copy).then_inc(s["v_hi"], 1)

                    def probs(h, qb):
                        u = i * UNITS + h * 8 + qb
                        n = (qb + 1) * P
                        act.wait_ge(s["maxed"], u + 1)
                        g = qb // 4
                        act.wait_ge(s["pt_turned"], nth_pt(i, h, g, nkt[g] - 1) + 1)
                        act.wait_ge(s["scaled"], u + 1)
                        src = core.psum[:, 1024 * (qb % 2):1024 * (qb % 2) + n]
                        act.activation(slot(qb)[:, 0:n], src, ACT.Exp, bias=nm[:, qb % 2:qb % 2 + 1],
                                       accum_out=rs[:, qb % 2:qb % 2 + 1]).then_inc(s["probs"], 1)

                    def turned(h, g, kt):
                        n = nth_pt(i, h, g, kt)
                        c0 = max(kt - 4 * g, 0) * P
                        act.wait_ge(s["pt_turned"], n + 13)
                        act.wait_ge(s["pv_done"], n + 1)
                        act.activation(pt[0][:, kt % 2, c0:HALF], ps[4 + kt % 2][:, c0:HALF], ACT.Copy).then_inc(s["pt_hi"], 1)

                    for h in range(2):
                        for qb in range(4):
                            probs(h, qb)
                        for qb in range(4, 8):
                            probs(h, qb)
                            turned(h, 0, qb - 4)
                        for kt in range(8):
                            turned(h, 1, kt)

            @block.vector
            def _(dve):
                dve.sem_inc(s["pt_lo"], 2)
                dve.sem_inc(s["o_read"], 2)
                dve.wait_ge(s["consts"], 32)
                with dve.Fori(0, PAIRS) as i:
                    def gate_rows(h):
                        dve.tensor_scalar(th[:, :], tbase[:, :], sel[:, 2 * i + h, :], None, ALU.mult)\
                           .then_inc(s["f_rows"], 1)

                    def split_lo(p, dst, scale, hi_name, name):
                        o = slice((p % 2) * HALF, (p % 2 + 1) * HALF)
                        dve.wait_ge(s[hi_name], 2 * i + p % 2 + 1)
                        dve.scalar_tensor_tensor(dst[1][:, o], ps[6 + p % 2][:, :], scale, dst[0][:, o].bitcast(F32),
                                                 ALU.mult, ALU.subtract).then_inc(s[name], 1)

                    def maxes(h, qb):
                        u = i * UNITS + h * 8 + qb
                        dve.wait_ge(s["scored"], u + 1)
                        at = 1024 * (qb % 2)
                        dve.tensor_reduce(nm[:, qb % 2:qb % 2 + 1], core.psum[:, at:at + (qb + 1) * P], AX.X, ALU.max,
                                          negate=True).then_inc(s["maxed"], 1)

                    def recip(h, qb):
                        u = i * UNITS + h * 8 + qb
                        dve.wait_ge(s["probs"], u + 3)
                        dve.reciprocal(rs[:, qb % 2:qb % 2 + 1], rs[:, qb % 2:qb % 2 + 1]).then_inc(s["recips"], 1)

                    def turned(h, g, kt):
                        n = nth_pt(i, h, g, kt)
                        c0 = max(kt - 4 * g, 0) * P
                        dve.wait_ge(s["pt_hi"], n + 1)
                        dve.tensor_tensor(pt[1][:, kt % 2, c0:HALF], ps[4 + kt % 2][:, c0:HALF],
                                          pt[0][:, kt % 2, c0:HALF].bitcast(F32), ALU.subtract).then_inc(s["pt_lo"], 1)

                    def output(h, g):
                        dve.wait_ge(s["pv_done"], nth_pt(i, h, g, nkt[g] - 1) + 3)
                        r = slice(h * DH, (h + 1) * DH)
                        dve.tensor_copy(mix[r, 4 + i, g * HALF:(g + 1) * HALF], ps[6 + g][r, :]).then_inc(s["o_read"], 1)

                    gate_rows(0)
                    for p in range(2):
                        split_lo(p, q, DH ** -0.5, "q_hi", "q_done")
                    for p in range(2, 4):
                        split_lo(p, k, 1.0, "k_hi", "k_done")
                    for n in range(2):
                        dve.wait_ge(s["v_hi"], 2 * i + n + 1)
                        dve.tensor_tensor(v[1][:, 4 * n:4 * n + 4, :], ps[n][:, :].rearrange("p (t m) -> p t m", t=4),
                                          v[0][:, 4 * n:4 * n + 4, :].bitcast(F32), ALU.subtract).then_inc(s["v_done"], 1)
                    for h in range(2):
                        for qb in range(8):
                            maxes(h, qb)
                            if qb:
                                recip(h, qb - 1)
                            if qb >= 4:
                                turned(h, 0, qb - 4)
                        recip(h, 7)
                        if h == 0:
                            gate_rows(1)
                        output(h, 0)
                        for kt in range(8):
                            turned(h, 1, kt)
                        output(h, 1)

            @block.tensor
            def _(pe):
                ws.start_pieces(pe)
                pe.sem_inc(s["pt_turned"], 12)
                pe.sem_inc(s["pv_done"], 2)
                pe.wait_ge(s["consts_r"], 1)
                with pe.Fori(0, PAIRS) as i:
                    for p in range(6):
                        if p % 2 == 0:
                            ws.wait_tile(pe, i, p // 2)
                        if p == 0:
                            pe.wait_ge(s["o_read"], i * 4 + 2)
                        elif p >= 2:
                            pe.wait_ge(s["q_done" if p < 4 else "k_done"], 2 * i + p % 2 + 1)
                        ws.piece(pe, p // 2, ps[6 + p % 2], core.hh, core.hl, (p % 2) * HALF, HALF)
                    pe.wait_ge(s["probs"], i * UNITS + 2)
                    for n in range(2):
                        pe.wait_ge(s["v_copied"], 2 * i + n + 1)
                        for t in range(4):
                            at = (4 * n + t) * P
                            last = pe.transpose(ps[n][:, t * P:(t + 1) * P], vT[:, at:at + P], core.ident[:, :])
                        last.then_inc(s["v_turned"], 1)
                    pe.wait_ge(s["k_done"], 2 * i + 2)
                    pe.wait_ge(s["v_done"], 2 * i + 2)

                    def score(h, qb):
                        u = i * UNITS + h * 8 + qb
                        pe.wait_ge(s["probs"], u + 1)
                        r, c0 = slice(h * DH, (h + 1) * DH), slice(qb * P, (qb + 1) * P)
                        keys = (qb + 1) * P
                        for a in range(0, keys, HALF):
                            n = min(HALF, keys - a)
                            at = 1024 * (qb % 2) + a
                            out = core.psum[:, at:at + n]
                            pe.matmul(out, q[0][r, c0], k[0][r, a:a + n], start=True, stop=False)
                            pe.matmul(out, q[0][r, c0], k[1][r, a:a + n], start=False, stop=False)
                            pe.matmul(out, q[1][r, c0], k[0][r, a:a + n], start=False, stop=False)
                            pe.matmul(out, th[:, c0], rf[:, a:a + n], start=False, stop=(a + n < keys))
                        last = pe.matmul(core.psum[:, at + n - P:at + n], idr[:, :], ngr[:, :], start=False, stop=True)
                        last.then_inc(s["scored"], 1)

                    def turn(h, g, kt):
                        n = nth_pt(i, h, g, kt)
                        if kt == 0:
                            pe.wait_ge(s["scaled"], i * UNITS + h * 8 + 4 * g + 6)
                        pe.wait_ge(s["pt_lo"], n + 1)
                        for b in range(max(kt - 4 * g, 0), 4):
                            last = pe.transpose(ps[4 + kt % 2][:, b * P:(b + 1) * P],
                                                slot(4 * g + b)[:, kt * P:(kt + 1) * P], core.ident[:, :])
                        last.then_inc(s["pt_turned"], 1)

                    def times_v(h, g, kt):
                        n = nth_pt(i, h, g, kt)
                        c0 = max(kt - 4 * g, 0) * P
                        if kt == 0:
                            pe.wait_ge(s["o_read"], i * 4 + h * 2 + g + 1)
                        pe.wait_ge(s["pt_lo"], n + 3)
                        out, b = ps[6 + g][:, c0:HALF], kt % 2
                        pe.matmul(out, v[0][:, kt, :], pt[0][:, b, c0:HALF], start=(kt == 0), stop=False)
                        pe.matmul(out, v[0][:, kt, :], pt[1][:, b, c0:HALF], start=False, stop=False)
                        pe.matmul(out, v[1][:, kt, :], pt[0][:, b, c0:HALF], start=False, stop=(kt == nkt[g] - 1))\
                          .then_inc(s["pv_done"], 1)

                    for h in range(2):
                        pe.wait_ge(s["f_rows"], 2 * i + h + 1)
                        for qb in range(8):
                            score(h, qb)
                            if qb > 4:
                                times_v(h, 0, qb - 5)
                            if qb >= 4:
                                turn(h, 0, qb - 4)
                        times_v(h, 0, 3)
                        turn(h, 1, 0)
                        for kt in range(8):
                            if kt < 7:
                                turn(h, 1, kt + 1)
                            times_v(h, 1, kt)


class OutProjection:

    def __init__(self, ph, core, feat, w_src):
        self.core, self.feat, self.w_src = core, feat, w_src
        self.wh = ph.sb("w_all_hi", [P, KT, D], F32R)
        self.wl = ph.sb("w_all_lo", [P, KT, D], F32R)
        self.loaded = [ph.sem(f"row_loaded{b}") for b in range(2)]
        self.fhi, self.flo, self.whi, self.wlo = (ph.sem(n) for n in ("feat_hi", "feat_lo", "row_hi", "row_lo"))
        self.mm, self.read = ph.sem("tile_mm"), ph.sem("tile_read")

    def sync(self, sync):
        for k in range(KT):
            if k >= 2:
                sync.wait_ge(self.wlo, k - 1)
            sync.dma_start(self.core.raw[:, k % 2, :], self.w_src[k, :, :]).then_inc(self.loaded[k % 2], 16)

    def act(self, act, feat_ready):
        for k in range(KT):
            feat_ready(act, k)
            act.activation(self.core.hh[:, k, :], self.feat[:, k, :], ACT.Copy).then_inc(self.fhi, 1)
            act.wait_ge(self.loaded[k % 2], 16 * (k // 2) + 16)
            act.activation(self.wh[:, k, :], self.core.raw[:, k % 2, :], ACT.Copy).then_inc(self.whi, 1)

    def pool(self, pool):
        for k in range(KT):
            pool.wait_ge(self.whi, k + 1)
            pool.tensor_tensor(self.wl[:, k, :], self.core.raw[:, k % 2, :], self.wh[:, k, :].bitcast(F32),
                               ALU.subtract).then_inc(self.wlo, 1)

    def dve(self, dve):
        for k in range(KT):
            dve.wait_ge(self.fhi, k + 1)
            dve.tensor_tensor(self.core.hl[:, k, :], self.feat[:, k, :], self.core.hh[:, k, :].bitcast(F32),
                              ALU.subtract).then_inc(self.flo, 1)

    def pe(self, pe):
        ps, hh, hl = self.core.ps, self.core.hh, self.core.hl
        for g in range(2):
            for k in range(KT):
                if g == 0:
                    pe.wait_ge(self.flo, k + 1)
                    pe.wait_ge(self.wlo, k + 1)
                for t in range(4):
                    if g and k == 0:
                        pe.wait_ge(self.read, t + 1)
                    c0 = (4 * g + t) * P
                    for f, w, m in ((hh, self.wh, 0), (hh, self.wl, 1), (hl, self.wh, 2)):
                        for c in range(2):
                            last = pe.matmul(ps[2 * t + c][:, :], f[:, k, c0:c0 + P], w[:, k, c * 512:(c + 1) * 512],
                                             start=(k == 0 and m == 0), stop=(k == KT - 1 and m == 2))
                    if k == KT - 1:
                        last.then_inc(self.mm, 1)

    def banks(self, t):
        return self.core.psum[:, (t % 4) * 1024:(t % 4) * 1024 + 1024]


def mixer_output(core, mix):
    nc, d = core.nc, core.d
    with Phase(core, "wo") as ph:
        op = OutProjection(ph, core, mix, d["w_o"])
        x = ph.sb("x", [P, 2, D], F32)
        sq = ph.sb("sq", [P, D], F32)
        ss = ph.sb("ss", [P, NT], F32)
        y = mix
        s_x = [ph.sem(f"x_loaded{b}") for b in range(2)]
        s_st = ph.sem("x1_stored")
        s_ss, s_ms, s_rt, s_step = ph.sem("squares"), ph.sem("means"), ph.sem("roots"), ph.sem("step")
        tr = Transposes(ph, core, y, core.hh, core.hl, 2, 4, lambda k: core.cols[:, C_LN2 + k:C_LN2 + k + 1])
        with nc.Block() as block:
            @block.sync
            def _(sync):
                op.sync(sync)

            @block.gpsimd
            def _(pool):
                op.pool(pool)
                for t in range(NT):
                    if t >= 2:
                        pool.wait_ge(op.read, t - 1)
                    pool.dma_start(x[:, t % 2, :], d["x"][t, :, :]).then_inc(s_x[t % 2], 16)
                    if t >= 1:
                        pool.wait_ge(op.read, t)
                        pool.dma_start(d["x1"][t - 1, :, :], y[:, t - 1, :]).then_inc(s_st, 16)
                pool.wait_ge(op.read, NT)
                pool.dma_start(d["x1"][NT - 1, :, :], y[:, NT - 1, :]).then_inc(s_st, 16)
                pool.wait_ge(s_st, 16 * NT)

            @block.scalar
            def _(act):
                op.act(act, lambda act, k: None)
                for t in range(NT):
                    act.wait_ge(op.read, t + 1)
                    act.activation(sq[:, :], y[:, t, :], ACT.Square, accum_out=ss[:, t:t + 1]).then_inc(s_ss, 1)
                    act.wait_ge(s_ss, t + 1)
                act.wait_ge(s_ms, 1)
                act.activation(ss[:, :], ss[:, :], ACT.Sqrt).then_inc(s_rt, 1)
                for g in range(2):
                    tr.act(act, g)

            @block.vector
            def _(dve):
                op.dve(dve)
                for t in range(NT):
                    dve.wait_ge(op.mm, t + 1)
                    dve.wait_ge(s_x[t % 2], 16 * (t // 2) + 16)
                    dve.tensor_tensor(y[:, t, :], op.banks(t), x[:, t % 2, :], ALU.add).then_inc(op.read, 1)
                step = Steps(dve, s_step)
                dve.wait_ge(s_ss, NT)
                dve.tensor_scalar(ss[:, :], ss[:, :], 1.0 / D, EPS, ALU.mult, ALU.add).then_inc(s_ms, 1)
                dve.wait_ge(s_rt, 1)
                step(dve.reciprocal(ss[:, :], ss[:, :]))
                dve.wait_ge(s_st, 16 * NT)
                for g in range(2):
                    for t in range(4 * g, 4 * g + 4):
                        last = dve.tensor_scalar(y[:, t, :], y[:, t, :], ss[:, t:t + 1], None, ALU.mult)
                    last.then_inc(tr.ready, 1)
                    tr.dve(dve, g)

            @block.tensor
            def _(pe):
                op.pe(pe)
                pe.wait_ge(op.read, NT)
                for g in range(2):
                    tr.pe(pe, g)


def gate_and_up(core, hid):
    nc, d, ps = core.nc, core.d, core.ps
    with Phase(core, "gu") as ph:
        ws = Weights(ph, core, [0, 1], [1, 3], 4)
        s_silu, s_prod = ph.sem("silu_done"), ph.sem("product_done")
        with nc.Block() as block:
            @block.sync
            def _(sync):
                with sync.Fori(0, FT) as i:
                    for c in range(2):
                        ws.load(sync, i, c, d["w_gu"][2 * i + c, :, :])

            @block.gpsimd
            def _(pool):
                ws.start_lo(pool)
                with pool.Fori(0, FT) as i:
                    for c in range(2):
                        ws.subtract_lo(pool, i, c)

            @block.scalar
            def _(act):
                act.sem_inc(s_silu, 2)
                with act.Fori(0, FT) as i:
                    for c in range(2):
                        ws.round_hi(act, i, c)
                    for p in range(2):
                        act.wait_ge(ws.piece_done, ws.done(i, p))
                        act.activation(hid[:, i, p * HALF:(p + 1) * HALF], ps[p][:, :], ACT.Silu).then_inc(s_silu, 1)

            @block.vector
            def _(dve):
                dve.sem_inc(s_prod, 2)
                with dve.Fori(0, FT) as i:
                    for p in range(2):
                        dve.wait_ge(s_silu, 2 * i + p + 3)
                        dve.wait_ge(ws.piece_done, ws.done(i, p + 2))
                        o = slice(p * HALF, (p + 1) * HALF)
                        dve.tensor_tensor(hid[:, i, o], ps[2 + p][:, :], hid[:, i, o], ALU.mult).then_inc(s_prod, 1)

            @block.tensor
            def _(pe):
                ws.start_pieces(pe)
                with pe.Fori(0, FT) as i:
                    for p in range(4):
                        if p % 2 == 0:
                            ws.wait_tile(pe, i, p // 2)
                        pe.wait_ge(s_silu if p < 2 else s_prod, 2 * i + p % 2 + 1)
                        ws.piece(pe, p // 2, ps[p][:, :], core.hh, core.hl, (p % 2) * HALF, HALF)


def down(core, hid):
    nc, d = core.nc, core.d
    with Phase(core, "down") as ph:
        y0 = ph.sb("y", [P, 4, D], F32)
        lnf = ph.sb("ln_f", [P, D], F32)
        ss = ph.sb("ss", [P, NT], F32)
        loaded = [ph.sem(f"w_loaded{b}") for b in range(2)]
        whi, wlo, ahi, alo, mm = (ph.sem(n) for n in ("w_hi", "w_lo", "act_hi", "act_lo", "mm"))
        s_x = [ph.sem(f"x{t}") for t in range(NT)]
        s_row, s_add, s_ss, s_ms, s_rt, s_step = (ph.sem(n) for n in ("row", "added", "squares", "means", "roots", "step"))
        s_x3, s_st = ph.sem("x3_ready"), ph.sem("x3_stored")

        class Tiles:
            def __getitem__(self, at):
                _, t, c = at
                return y0[:, t, c] if t < 4 else hid[:, t, c]
        y = Tiles()
        ah = [core.hh[:, b, HALF:SEQ] for b in range(2)]
        al = [core.hl[:, b, HALF:SEQ] for b in range(2)]
        tr = Transposes(ph, core, y, core.hh, core.hl, 2, 4,
                        lambda k: core.mods[:, 8 + k, 0:1], lambda k: core.mods[:, k, 0:1])

        def rounds(eng, g, body):
            body(0, True, False)
            with eng.Fori(1, FT // 2 - 1) as i:
                body(i, False, False)
            body(FT // 2 - 1, False, True)
        with nc.Block() as block:
            @block.sync
            def _(sync):
                sync.dma_start(lnf[:, :], d["ln_f"].partition_broadcast(P)).then_inc(s_row, 16)
                for t in range(4):
                    sync.dma_start(y0[:, t, :], d["x1"][t, :, :]).then_inc(s_x[t], 16)
                for g in range(2):
                    def body(i, first, last):
                        for b in range(2):
                            sync.wait_ge(wlo, g * FT + 2 * i + b + 1)
                            sync.dma_start(core.raw[:, b, :], d["w_down"][2 * i + b, :, :]).then_inc(loaded[b], 16)
                    rounds(sync, g, body)
                sync.wait_ge(ahi, 2 * FT)
                sync.wait_ge(alo, 2 * FT)
                for t in range(4, NT):
                    sync.dma_start(y[:, t, slice(0, D)], d["x1"][t, :, :]).then_inc(s_x[t], 16)
                for t in range(NT):
                    sync.wait_ge(s_x3, t + 1)
                    sync.dma_start(d["x3"][t, :, :], y[:, t, slice(0, D)]).then_inc(s_st, 16)
                sync.wait_ge(s_st, 16 * NT)

            @block.scalar
            def _(act):
                for g in range(2):
                    def body(i, first, last):
                        for b in range(2):
                            n = g * FT + 2 * i + b
                            act.wait_ge(loaded[b], (g * (FT // 2) + i) * 16 + 16)
                            act.wait_ge(mm, n + 1)
                            act.activation(core.wh[:, b, :], core.raw[:, b, :], ACT.Copy).then_inc(whi, 1)
                            act.activation(ah[b], hid[:, 2 * i + b, g * HALF:(g + 1) * HALF], ACT.Copy).then_inc(ahi, 1)
                    rounds(act, g, body)
                    for t in range(4 * g, 4 * g + 4) if g == 0 else ():
                        act.wait_ge(s_add, t + 1)
                        act.activation(core.psum[:, (t % 4) * 1024:(t % 4 + 1) * 1024], y[:, t, slice(0, D)], ACT.Square,
                                       accum_out=ss[:, t:t + 1]).then_inc(s_ss, 1)
                for t in range(4, NT):
                    act.wait_ge(s_add, t + 1)
                    act.activation(core.psum[:, (t % 4) * 1024:(t % 4 + 1) * 1024], y[:, t, slice(0, D)], ACT.Square,
                                   accum_out=ss[:, t:t + 1]).then_inc(s_ss, 1)
                act.wait_ge(s_ms, 1)
                act.activation(ss[:, :], ss[:, :], ACT.Sqrt).then_inc(s_rt, 1)
                for t in range(NT):
                    act.wait_ge(s_x3, t + 1)
                    act.activation(core.psum[:, (t % 4) * 1024:(t % 4 + 1) * 1024], y[:, t, slice(0, D)], ACT.Square,
                                   accum_out=ss[:, t:t + 1]).then_inc(s_ss, 1)
                    act.wait_ge(s_ss, NT + t + 1)
                act.wait_ge(s_ms, 2)
                act.activation(ss[:, :], ss[:, :], ACT.Sqrt).then_inc(s_rt, 1)
                for g in range(2):
                    tr.act(act, g)

            @block.gpsimd
            def _(pool):
                pool.sem_inc(wlo, 2)
                for g in range(2):
                    def body(i, first, last):
                        for b in range(2):
                            pool.wait_ge(whi, g * FT + 2 * i + b + 1)
                            pool.tensor_tensor(core.wl[:, b, :], core.raw[:, b, :], core.wh[:, b, :].bitcast(F32),
                                               ALU.subtract).then_inc(wlo, 1)
                    rounds(pool, g, body)

            @block.vector
            def _(dve):
                step = Steps(dve, s_step)
                for g in range(2):
                    def body(i, first, last):
                        for b in range(2):
                            dve.wait_ge(ahi, g * FT + 2 * i + b + 1)
                            dve.tensor_tensor(al[b], hid[:, 2 * i + b, g * HALF:(g + 1) * HALF], ah[b].bitcast(F32),
                                              ALU.subtract).then_inc(alo, 1)
                    rounds(dve, g, body)
                    dve.wait_ge(mm, (g + 1) * FT + 2)
                    for t in range(4 * g, 4 * g + 4):
                        dve.wait_ge(s_x[t], 16)
                        yt = y[:, t, slice(0, D)]
                        dve.tensor_tensor(yt, core.psum[:, (t % 4) * 1024:(t % 4 + 1) * 1024], yt, ALU.add)\
                           .then_inc(s_add, 1)
                dve.wait_ge(s_ss, NT)
                dve.tensor_scalar(ss[:, :], ss[:, :], 1.0 / D, EPS, ALU.mult, ALU.add).then_inc(s_ms, 1)
                dve.wait_ge(s_rt, 1)
                step(dve.reciprocal(ss[:, :], ss[:, :]))
                dve.wait_ge(s_row, 16)
                for t in range(NT):
                    yt = y[:, t, slice(0, D)]
                    dve.scalar_tensor_tensor(yt, yt, ss[:, t:t + 1], lnf[:, :], ALU.mult, ALU.mult).then_inc(s_x3, 1)
                dve.wait_ge(s_ss, 2 * NT)
                dve.tensor_scalar(ss[:, :], ss[:, :], 1.0 / D, EPS, ALU.mult, ALU.add).then_inc(s_ms, 1)
                dve.wait_ge(s_rt, 2)
                step(dve.reciprocal(ss[:, :], ss[:, :]))
                dve.wait_ge(s_st, 16 * NT)
                for g in range(2):
                    for t in range(4 * g, 4 * g + 4):
                        yt = y[:, t, slice(0, D)]
                        last = dve.tensor_scalar(yt, yt, ss[:, t:t + 1], None, ALU.mult)
                    last.then_inc(tr.ready, 1)
                    tr.dve(dve, g)

            @block.tensor
            def _(pe):
                pe.sem_inc(mm, 2)
                for g in range(2):
                    def body(i, first, last):
                        for b in range(2):
                            n = g * FT + 2 * i + b
                            pe.wait_ge(wlo, n + 3)
                            pe.wait_ge(alo, n + 1)
                            if g and first and b == 0:
                                pe.wait_ge(s_ss, 4)
                            for t in range(4):
                                for f, w, m in ((ah, core.wh, 0), (ah, core.wl, 1), (al, core.wh, 2)):
                                    for c in range(2):
                                        mmul = pe.matmul(core.ps[2 * t + c][:, :], f[b][:, t * P:(t + 1) * P],
                                                         w[:, b, c * 512:(c + 1) * 512],
                                                         start=(first and b == 0 and m == 0), stop=(last and b == 1 and m == 2))
                            mmul.then_inc(mm, 1)
                    rounds(pe, g, body)
                pe.wait_ge(s_ss, 2 * NT)
                for g in range(2):
                    tr.pe(pe, g)


def context_norm(core, hc):
    nc, d = core.nc, core.d
    with Phase(core, "ctx") as ph:
        y = ph.sb("y", [P, 2, D], F32)
        sq = ph.sb("sq", [P, D], F32)
        ss = ph.sb("ss", [P, 2], F32)
        s_x, s_ss, s_ms, s_rt, s_step = (ph.sem(n) for n in ("x", "squares", "means", "roots", "step"))
        tr = Transposes(ph, core, y, hc[0], hc[1], 1, 2,
                        lambda k: core.mods[:, 8 + k, 1:2], lambda k: core.mods[:, k, 1:2])
        with nc.Block() as block:
            @block.sync
            def _(sync):
                sync.dma_start(y[:, :, :], d["ctx"].rearrange("t p n -> p t n")).then_inc(s_x, 16)

            @block.scalar
            def _(act):
                act.wait_ge(s_x, 16)
                for t in range(2):
                    act.activation(sq[:, :], y[:, t, :], ACT.Square, accum_out=ss[:, t:t + 1]).then_inc(s_ss, 1)
                    act.wait_ge(s_ss, t + 1)
                act.wait_ge(s_ms, 1)
                act.activation(ss[:, :], ss[:, :], ACT.Sqrt).then_inc(s_rt, 1)
                tr.act(act, 0)

            @block.vector
            def _(dve):
                step = Steps(dve, s_step)
                dve.wait_ge(s_ss, 2)
                dve.tensor_scalar(ss[:, :], ss[:, :], 1.0 / D, EPS, ALU.mult, ALU.add).then_inc(s_ms, 1)
                dve.wait_ge(s_rt, 1)
                step(dve.reciprocal(ss[:, :], ss[:, :]))
                for t in range(2):
                    last = dve.tensor_scalar(y[:, t, :], y[:, t, :], ss[:, t:t + 1], None, ALU.mult)
                last.then_inc(tr.ready, 1)
                tr.dve(dve, 0)

            @block.tensor
            def _(pe):
                tr.pe(pe, 0)


def differential_attention(core, hc):
    nc, d, ps = core.nc, core.d, core.ps
    STEPS = 2 * NKT
    PIECES = 10
    TILE = (0, 0, 1, 1, 1, 2, 2, 2, 3, 3)
    BANK = (1, 2, 1, 2, 1, 2, 1, 2, 6, 7)
    TURN_BANK, O_BANK, SS_BANK, VT_BANK = (6, 7), (0, 3), (4, 4), (6, 7, 5)
    VT = ((2, 2), (0, 4), (1, 4))

    cost = [(p, k, 0.5 if p in (4, 7) else 1.0) for p in range(8) for k in range(KT)]
    share, spent, chunks = sum(c[2] for c in cost) / STEPS, 0.0, [[] for _ in range(STEPS)]
    for p, k, c in cost:
        chunks[min(int(spent / share), STEPS - 1)].append((p, k))
        spent += c
    end = [max(n for n in range(STEPS) if (p, KT - 1) in chunks[n]) for p in range(8)]

    with Phase(core, "diff") as ph:
        q = [ph.sb(n, [P, SEQ], F32R) for n in ("q_hi", "q_lo")]
        k = [ph.sb(n, [P, NKEY], F32R) for n in ("k_hi", "k_lo")]
        v = [ph.sb(n, [P, NKT, P], F32R) for n in ("v_hi", "v_lo")]
        zs = ph.sb("silu_z", [P, SEQ], F32)
        pr = ph.sb("probs", [P, 8, NKEY], F32)
        p1 = ph.sb("probs_1", [P, NKEY], F32)
        pt = [ph.sb(n, [P, 2, HALF], F32R) for n in ("pt_hi", "pt_lo")]
        rope = ph.sb("rope", [P, 2, SEQ], F32)
        rc = ph.sb("rope_cos", [P, HALF], F32)
        rsn = ph.sb("rope_sin", [P, HALF], F32)
        ob = ph.sb("o", [P, HALF], F32)
        rt = ph.sb("rstd", [P, HALF], F32)
        ones = ph.sb("ones", [P, P], F32)
        nm = ph.sb("neg_max", [P, 2, 2], F32)
        rs = ph.sb("row_sum", [P, 2, 2], F32)
        rr = ph.sb("recip", [P, 2, 2], F32)
        nl = ph.sb("neg_lam_recip", [P, 2], F32)
        vT = p1
        ws = Weights(ph, core, [0, 1, 0, 1], [1, 4, 7, 9], PIECES)
        names = ("consts cos_term shuffled sin_term rotated qk_hi qk_done v_copied z_done v_turned v_hi v_done score0 score1 "
                 "max0 max1 prob0 prob1 rsum nl p1 comb pt_turned pt_hi pt_lo pv_done o_copied ss_done ln rstd o_step o_ready "
                 "o_stored")
        s = {n: ph.sem(n) for n in names.split()}
        swap = [(j + 16) % 32 for j in range(32)]

        def heads(eng, body):
            with eng.Fori(0, HEADS2 - 1) as i:
                body(i, True)
            body(HEADS2 - 1, False)

        with nc.Block() as block:
            @block.sync
            def _(sync):
                sync.sem_inc(s["o_stored"], 16)
                sync.dma_start(rope[:, :, :], d["rope"]).then_inc(s["consts"], 16)
                load = lambda h, c: ws.load(sync, h, c, d["da_w_in"][4 * h + c, :, :])
                for c in range(4):
                    load(0, c)

                def body(i, more):
                    if more:
                        for c in range(3):
                            load(i + 1, c)
                    sync.wait_ge(s["o_ready"], 2 * i + 1)
                    sync.dma_start(d["o_feat"][i, :, 0:HALF], rt[:, :]).then_inc(s["o_stored"], 16)
                    if more:
                        load(i + 1, 3)
                    sync.wait_ge(s["o_ready"], 2 * i + 2)
                    sync.dma_start(d["o_feat"][i, :, HALF:SEQ], rt[:, :]).then_inc(s["o_stored"], 16)
                heads(sync, body)
                sync.wait_ge(s["o_stored"], 16 * (2 * HEADS2 + 1))

            @block.gpsimd
            def _(pool):
                def sine_term(h, j):
                    o = slice((j % 2) * HALF, (j % 2 + 1) * HALF)
                    pool.wait_ge(s["shuffled"], 4 * h + j + 1)
                    pool.tensor_tensor(rsn[:, :], rsn[:, :], rope[:, 1, o], ALU.mult).then_inc(s["sin_term"], 1)
                ws.start_lo(pool)
                pool.wait_ge(s["consts"], 16)
                for c in range(3):
                    ws.subtract_lo(pool, 0, c)
                    if c < 2:
                        sine_term(0, 2 * c)
                        sine_term(0, 2 * c + 1)

                def body(i, more):
                    for qb in range(8):
                        if qb == 0:
                            ws.subtract_lo(pool, i, 3)
                        if qb == 7 and more:
                            ws.subtract_lo(pool, i + 1, 0)
                        pool.wait_ge(s["nl"], i * 8 + qb + 1)
                        pool.nop(nofuse=True)
                        pool.tensor_scalar(p1[:, :], p1[:, :], nl[:, qb % 2:qb % 2 + 1], 1.0, ALU.mult, ALU.mult)\
                            .then_inc(s["p1"], 1)
                    if more:
                        ws.subtract_lo(pool, i + 1, 1)
                        for j in range(4):
                            if j == 3:
                                ws.subtract_lo(pool, i + 1, 2)
                            sine_term(i + 1, j)
                heads(pool, body)

            @block.scalar
            def _(act):
                act.sem_inc(s["prob0"], 1)
                act.sem_inc(s["prob1"], 1)
                act.sem_inc(s["z_done"], 2)

                def qk_hi(h, j):
                    if j < 4:
                        act.wait_ge(s["rotated"], 4 * h + j + 1)
                        src = rc[:, :]
                    else:
                        act.wait_ge(ws.piece_done, ws.done(h, 4))
                        src = ps[BANK[4]][:, 0:CTX]
                    dst = q[0][:, j * HALF:(j + 1) * HALF] if j < 2 else k[0][:, (j - 2) * HALF:min((j - 1) * HALF, NKEY)]
                    act.activation(dst, src, ACT.Copy, scale=DH ** -0.5 if j < 2 else 1.0).then_inc(s["qk_hi"], 1)

                def v_copy(h, j):
                    n = CTX if j == 2 else HALF
                    act.wait_ge(ws.piece_done, ws.done(h, 5 + j))
                    if j == 0:
                        act.wait_ge(s["comb"], h * 8 + 1)
                    act.activation(vT[:, j * HALF:j * HALF + n], ps[BANK[5 + j]][:, 0:n], ACT.Copy).then_inc(s["v_copied"], 1)

                def v_hi(h, j):
                    b, n = VT[j]
                    act.wait_ge(s["v_turned"], 3 * h + j + 1)
                    act.activation(v[0][:, 4 * b:4 * b + n, :], ps[VT_BANK[b]][:, 0:n * P].rearrange("p (t m) -> p t m", t=n),
                                   ACT.Copy).then_inc(s["v_hi"], 1)

                def next_head(h, n):
                    for p in range(4):
                        if n == end[p] + 2:
                            qk_hi(h, p)
                    for p in range(4, 8):
                        if n == end[p]:
                            qk_hi(h, 4) if p == 4 else v_copy(h, p - 5)
                    if n == 0:
                        ws.round_hi(act, h, 1)
                    if n == 9:
                        ws.round_hi(act, h, 2)

                ws.round_hi(act, 0, 0)
                ws.round_hi(act, 0, 1)
                qk_hi(0, 0)
                qk_hi(0, 1)
                ws.round_hi(act, 0, 2)
                for j in range(2, 5):
                    qk_hi(0, j)
                for j in range(3):
                    v_copy(0, j)
                for j in range(3):
                    v_hi(0, j)

                def body(i, more):
                    def hi(n):
                        b = n % 2
                        act.wait_ge(s["pt_turned"], STEPS * (i + 1) + n + 1)
                        act.wait_ge(s["pv_done"], STEPS * i + n + 1)
                        act.activation(pt[0][:, b, :], ps[TURN_BANK[b]][:, :], ACT.Copy).then_inc(s["pt_hi"], 1)

                    def prob(qb, z):
                        u = i * 8 + qb
                        act.wait_ge(s[f"max{z}"], u + 1)
                        if z == 0:
                            act.wait_ge(s["pt_turned"], STEPS * i + NKT * (qb // 4) + NKT)
                        else:
                            act.wait_ge(s["comb"], u + 1)
                            if qb == 0:
                                act.wait_ge(s["v_turned"], 3 * i + 3)
                        dst = pr[:, qb, :] if z == 0 else p1[:, :]
                        act.activation(dst, core.psum[:, 1536 * z:1536 * z + NKEY], ACT.Exp, bias=nm[:, qb % 2, z:z + 1],
                                       accum_out=rs[:, qb % 2, z:z + 1]).then_inc(s[f"prob{z}"], 1)

                    def silu_z(j):
                        act.wait_ge(ws.piece_done, ws.done(i, 8 + j))
                        act.activation(zs[:, j * HALF:(j + 1) * HALF], ps[BANK[8 + j]][:, :], ACT.Silu).then_inc(s["z_done"], 1)

                    def outputs(g):
                        act.wait_ge(s["pv_done"], STEPS * i + NKT * (g + 1) + 2)
                        act.wait_ge(s["o_step"], 2 * i + g + 1)
                        act.activation(ob[:, :], ps[O_BANK[g]][:, :], ACT.Copy).then_inc(s["o_copied"], 1)
                        act.wait_ge(s["o_stored"], 16 * (2 * i + g) + 16)
                        act.activation(rt[:, :], ps[O_BANK[g]][:, :], ACT.Square).then_inc(s["o_copied"], 1)

                    def rstd(g):
                        act.wait_ge(s["ss_done"], 2 * i + g + 1)
                        act.activation(rt[:, :], ps[SS_BANK[g]][:, :], ACT.Ln, scale=1.0 / P, bias=core.eps[:, 1:2])\
                           .then_inc(s["ln"], 1)
                        act.wait_ge(s["ln"], 2 * i + g + 1)
                        act.activation(rt[:, :], rt[:, :], ACT.Exp, scale=-0.5).then_inc(s["rstd"], 1)

                    ws.round_hi(act, i, 3)
                    for qb in range(8):
                        prob(qb, 0)
                        prob(qb, 1)
                        if qb == 6 and more:
                            ws.round_hi(act, i + 1, 0)
                    silu_z(0)
                    silu_z(1)
                    hi(0)
                    for n in range(STEPS):
                        if n + 1 < STEPS:
                            hi(n + 1)
                        if more:
                            next_head(i + 1, n)
                        if n == 10:
                            outputs(0)
                        if n == 13:
                            rstd(0)
                    outputs(1)
                    if more:
                        v_hi(i + 1, 0)
                        v_hi(i + 1, 1)
                    rstd(1)
                    if more:
                        v_hi(i + 1, 2)
                heads(act, body)

            @block.vector
            def _(dve):
                dve.sem_inc(s["comb"], 1)
                dve.sem_inc(s["pt_lo"], 2)
                dve.sem_inc(s["o_step"], 1)
                dve.memset(ones[:, :], 1.0)
                dve.wait_ge(s["consts"], 16)

                def terms(h, j):
                    o = slice((j % 2) * HALF, (j % 2 + 1) * HALF)
                    dve.wait_ge(ws.piece_done, ws.done(h, j))
                    if j:
                        dve.wait_ge(s["qk_done"], 5 * h + j)
                    dve.tensor_tensor(rc[:, :], ps[BANK[j]][:, :], rope[:, 0, o], ALU.mult).then_inc(s["cos_term"], 1)
                    dve.stream_shuffle(rsn[:, :], ps[BANK[j]][:, :], swap).then_inc(s["shuffled"], 1)

                def rotated(h, j):
                    dve.wait_ge(s["cos_term"], 4 * h + j + 1)
                    dve.wait_ge(s["sin_term"], 4 * h + j + 1)
                    dve.tensor_tensor(rc[:, :], rc[:, :], rsn[:, :], ALU.add).then_inc(s["rotated"], 1)

                def qk_lo(h, j):
                    src = rc[:, :] if j < 4 else ps[BANK[4]][:, 0:CTX]
                    x = q if j < 2 else k
                    o = slice(j * HALF, (j + 1) * HALF) if j < 2 else slice((j - 2) * HALF, min((j - 1) * HALF, NKEY))
                    dve.wait_ge(s["qk_hi"], 5 * h + j + 1)
                    dve.scalar_tensor_tensor(x[1][:, o], src, DH ** -0.5 if j < 2 else 1.0, x[0][:, o].bitcast(F32),
                                             ALU.mult, ALU.subtract).then_inc(s["qk_done"], 1)

                def v_lo(h, j):
                    b, n = VT[j]
                    dve.wait_ge(s["v_hi"], 3 * h + j + 1)
                    dve.tensor_tensor(v[1][:, 4 * b:4 * b + n, :], ps[VT_BANK[b]][:, 0:n * P].rearrange("p (t m) -> p t m", t=n),
                                      v[0][:, 4 * b:4 * b + n, :].bitcast(F32), ALU.subtract).then_inc(s["v_done"], 1)

                def next_head(h, n):
                    for p in range(4):
                        if n == end[p] + 2:
                            qk_lo(h, p)
                        if n == end[p] + 1:
                            rotated(h, p)
                        if n == end[p]:
                            terms(h, p)
                    if n == end[4]:
                        qk_lo(h, 4)

                for j in range(4):
                    terms(0, j)
                    rotated(0, j)
                    qk_lo(0, j)
                qk_lo(0, 4)
                for j in range(3):
                    v_lo(0, j)

                def body(i, more):
                    def maxes(qb, z):
                        dve.wait_ge(s[f"score{z}"], i * 8 + qb + 1)
                        dve.tensor_reduce(nm[:, qb % 2, z:z + 1], core.psum[:, 1536 * z:1536 * z + NKEY], AX.X, ALU.max,
                                          negate=True).then_inc(s[f"max{z}"], 1)

                    def recips(qb):
                        u = i * 8 + qb
                        b = qb % 2
                        dve.wait_ge(s["prob0"], u + 2)
                        dve.wait_ge(s["prob1"], u + 2)
                        dve.reciprocal(rr[:, b, :], rs[:, b, :]).then_inc(s["rsum"], 1)
                        dve.wait_ge(s["rsum"], u + 1)
                        dve.tensor_tensor(nl[:, b:b + 1], rr[:, b, 1:2], core.neglam[:, :], ALU.mult).then_inc(s["nl"], 1)

                    def combine(qb):
                        u = i * 8 + qb
                        dve.wait_ge(s["p1"], u + 1)
                        dve.scalar_tensor_tensor(pr[:, qb, :], pr[:, qb, :], rr[:, qb % 2, 0:1], p1[:, :],
                                                 ALU.mult, ALU.add).then_inc(s["comb"], 1)

                    def lo(n):
                        b = n % 2
                        dve.wait_ge(s["pt_hi"], STEPS * i + n + 1)
                        dve.tensor_tensor(pt[1][:, b, :], ps[TURN_BANK[b]][:, :], pt[0][:, b, :].bitcast(F32), ALU.subtract)\
                           .then_inc(s["pt_lo"], 1)

                    def gated(g):
                        c = 2 * i + g
                        dve.wait_ge(s["rstd"], c + 1)
                        dve.wait_ge(s["z_done"], 2 * i + 4)
                        dve.scalar_tensor_tensor(rt[:, :], ob[:, :], core.subg[:, 0:1], rt[:, :], ALU.mult, ALU.mult)\
                           .then_inc(s["o_step"], 1)
                        dve.wait_ge(s["o_step"], c + 2)
                        dve.tensor_tensor(rt[:, :], rt[:, :], zs[:, g * HALF:(g + 1) * HALF], ALU.mult).then_inc(s["o_ready"], 1)

                    for qb in range(8):
                        maxes(qb, 0)
                        if qb:
                            recips(qb - 1)
                        maxes(qb, 1)
                        if qb:
                            combine(qb - 1)
                    recips(7)
                    lo(0)
                    combine(7)
                    for n in range(STEPS):
                        if n + 1 < STEPS:
                            lo(n + 1)
                        if more:
                            next_head(i + 1, n)
                        if n == 14:
                            gated(0)
                    if more:
                        v_lo(i + 1, 0)
                        v_lo(i + 1, 1)
                    gated(1)
                    if more:
                        v_lo(i + 1, 2)
                heads(dve, body)

            @block.tensor
            def _(pe):
                ws.start_pieces(pe)
                pe.sem_inc(s["pt_turned"], STEPS)
                pe.sem_inc(s["pv_done"], 2)

                def contract(h, p, k):
                    c, ctx = TILE[p], p in (4, 7)
                    if k == 0:
                        if p == 0 or TILE[p - 1] != c:
                            ws.wait_tile(pe, h, c)
                        if p == 0 or p == 1:
                            pe.wait_ge(s["prob0"], h * 8 + 1)
                        elif p < 7:
                            pe.wait_ge(s["qk_done" if p == 6 else "shuffled"], 5 * h + 5 if p == 6 else 4 * h + p - 1)
                        elif p == 7:
                            pe.wait_ge(s["v_copied"], 3 * h + 1)
                        elif p == 8:
                            pe.wait_ge(s["v_done"], 3 * h + 3)
                    n = CTX if ctx else HALF
                    at = 0 if ctx else (p - TILE.index(c)) * HALF
                    hi, lo = (hc[0], hc[1]) if ctx else (core.hh, core.hl)
                    ws.contract(pe, c, ps[BANK[p]][:, 0:n], hi, lo, at, n, k)

                def turn_v(h):
                    for j, (b, n) in enumerate(VT):
                        pe.wait_ge(s["v_copied"], 3 * h + 3)
                        for t in range(n):
                            at = (4 * b + t) * P
                            last = pe.transpose(ps[VT_BANK[b]][:, t * P:(t + 1) * P], vT[:, at:at + P], core.ident[:, :])
                        last.then_inc(s["v_turned"], 1)

                for p in range(8):
                    for kk in range(KT):
                        contract(0, p, kk)
                turn_v(0)

                def body(i, more):
                    def score(qb, z):
                        u = i * 8 + qb
                        pe.wait_ge(s[f"prob{z}"], u + 1)
                        if qb == 0 and z == 0:
                            pe.wait_ge(s["qk_done"], 5 * i + 5)
                            pe.wait_ge(s["v_copied"], 3 * i + 3)
                        if qb == 0 and z == 1:
                            pe.wait_ge(s["v_done"], 3 * i + 1)
                            pe.wait_ge(s["ln"], 2 * i)
                        r, c0 = slice(z * DH, (z + 1) * DH), slice(qb * P, (qb + 1) * P)
                        for a in range(0, NKEY, HALF):
                            n = min(HALF, NKEY - a)
                            out = core.psum[:, 1536 * z + a:1536 * z + a + n]
                            pe.matmul(out, q[0][r, c0], k[0][r, a:a + n], start=True, stop=False)
                            pe.matmul(out, q[0][r, c0], k[1][r, a:a + n], start=False, stop=False)
                            last = pe.matmul(out, q[1][r, c0], k[0][r, a:a + n], start=False, stop=True)
                        last.then_inc(s[f"score{z}"], 1)

                    def turn(n):
                        g, kt = n // NKT, n % NKT
                        if kt == 0:
                            pe.wait_ge(s["comb"], i * 8 + 4 * g + 5)
                        if n < 2:
                            pe.wait_ge(s["z_done"], 2 * i + 3 + n)
                        pe.wait_ge(s["pt_lo"], STEPS * i + n + 1)
                        for b in range(4):
                            last = pe.transpose(ps[TURN_BANK[n % 2]][:, b * P:(b + 1) * P],
                                                pr[:, 4 * g + b, kt * P:(kt + 1) * P], core.ident[:, :])
                        last.then_inc(s["pt_turned"], 1)

                    def times_v(n):
                        g, kt, b = n // NKT, n % NKT, n % 2
                        if kt == 0:
                            pe.wait_ge(s[f"prob{g}"], i * 8 + 9)
                        pe.wait_ge(s["pt_lo"], STEPS * i + n + 3)
                        out = ps[O_BANK[g]][:, :]
                        pe.matmul(out, v[0][:, kt, :], pt[0][:, b, :], start=(kt == 0), stop=False)
                        pe.matmul(out, v[0][:, kt, :], pt[1][:, b, :], start=False, stop=False)
                        pe.matmul(out, v[1][:, kt, :], pt[0][:, b, :], start=False, stop=(kt == NKT - 1))\
                          .then_inc(s["pv_done"], 1)

                    def squares(g):
                        pe.wait_ge(s["o_copied"], 2 * (2 * i + g) + 2)
                        pe.matmul(ps[SS_BANK[g]][:, :], ones[:, :], rt[:, :], start=True, stop=True)\
                          .then_inc(s["ss_done"], 1)

                    for slot in range(16):
                        score(slot // 2, slot % 2)
                        contract(i, 8 + slot // KT, slot % KT)
                    turn(0)
                    for n in range(STEPS):
                        if n + 1 < STEPS:
                            turn(n + 1)
                        times_v(n)
                        if more:
                            for p, kk in chunks[n]:
                                contract(i + 1, p, kk)
                        if n == 11:
                            squares(0)
                    if more:
                        turn_v(i + 1)
                    squares(1)
                heads(pe, body)


def block_output(core, feat):
    nc, d, ps = core.nc, core.d, core.ps
    with Phase(core, "out") as ph:
        op = OutProjection(ph, core, feat, d["da_w_out"])
        x = ph.sb("x", [P, 2, D], F32)
        gt = ph.sb("gt_row", [P, D], F32)
        fg = ph.sb("final_gain", [P, D], F32)
        diag = ph.sb("gt_diag", [P, P], F32)
        ones = ph.sb("ones", [P, P], F32)
        ss = ph.sb("ss", [P, NT], F32)
        y = feat
        s_f = [ph.sem(f"feat{k}") for k in range(KT)]
        s_x = [ph.sem(f"x_loaded{b}") for b in range(2)]
        s_row, s_ss, s_ms, s_rt, s_step, s_diag, s_gm, s_y = (
            ph.sem(n) for n in ("row", "squares", "means", "roots", "step", "diag", "gt_mm", "y_ready"))
        s_t, s_out, s_g = ph.sem("scaled"), ph.sem("stored"), ph.sem("gt_copied")
        with nc.Block() as block:
            @block.sync
            def _(sync):
                op.sync(sync)

            @block.gpsimd
            def _(pool):
                for k in range(KT):
                    pool.dma_start(feat[:, k, :], d["o_feat"][k, :, :]).then_inc(s_f[k], 16)
                pool.dma_start(fg[:, :], d["final_gain"].partition_broadcast(P)).then_inc(s_row, 16)
                op.pool(pool)
                for t in range(NT):
                    if t >= 2:
                        pool.wait_ge(s_ss, t - 1)
                    pool.dma_start(x[:, t % 2, :], d["x3"][t, :, :]).then_inc(s_x[t % 2], 16)
                for t in range(NT):
                    pool.wait_ge(s_y, t + 1)
                    pool.dma_start(d["out"][t, :, :], y[:, t, :]).then_inc(s_out, 16)
                pool.wait_ge(s_out, 16 * NT)

            @block.scalar
            def _(act):
                op.act(act, lambda act, k: act.wait_ge(s_f[k], 16))
                for t in range(NT):
                    act.wait_ge(s_t, t + 1)
                    act.activation(x[:, t % 2, :], y[:, t, :], ACT.Square, accum_out=ss[:, t:t + 1]).then_inc(s_ss, 1)
                    act.wait_ge(s_ms, t + 1)
                    act.activation(ss[:, t:t + 1], ss[:, t:t + 1], ACT.Sqrt).then_inc(s_rt, 1)

            @block.vector
            def _(dve):
                dve.memset(ones[:, :], 1.0)
                for k in range(KT):
                    if k:
                        dve.wait_ge(s_gm, k)
                    dve.tensor_scalar(diag[:, :], core.ident[:, :], core.mods[:, 16 + k, 0:1], None, ALU.mult)\
                       .then_inc(s_diag, 1)
                dve.wait_ge(s_gm, KT)
                dve.tensor_copy(gt[:, :], core.psum[:, 0:D]).then_inc(s_g, 1)
                op.dve(dve)
                step = Steps(dve, s_step)
                dve.wait_ge(s_row, 16)
                for t in range(NT):
                    dve.wait_ge(op.mm, t + 1)
                    dve.wait_ge(s_x[t % 2], 16 * (t // 2) + 16)
                    dve.tensor_tensor(y[:, t, :], op.banks(t), gt[:, :], ALU.mult).then_inc(op.read, 1)
                    dve.wait_ge(op.read, t + 1)
                    dve.tensor_tensor(y[:, t, :], y[:, t, :], x[:, t % 2, :], ALU.add).then_inc(s_t, 1)
                    dve.wait_ge(s_ss, t + 1)
                    dve.tensor_scalar(ss[:, t:t + 1], ss[:, t:t + 1], 1.0 / D, EPS, ALU.mult, ALU.add).then_inc(s_ms, 1)
                    dve.wait_ge(s_rt, t + 1)
                    step(dve.reciprocal(ss[:, t:t + 1], ss[:, t:t + 1]))
                    dve.scalar_tensor_tensor(y[:, t, :], y[:, t, :], ss[:, t:t + 1], fg[:, :], ALU.mult, ALU.mult)\
                       .then_inc(s_y, 1)

            @block.tensor
            def _(pe):
                for k in range(KT):
                    pe.wait_ge(s_diag, k + 1)
                    pe.matmul(core.psum[:, k * P:(k + 1) * P], ones[:, :], diag[:, :], start=True, stop=True)\
                      .then_inc(s_gm, 1)
                pe.wait_ge(s_g, 1)
                op.pe(pe)


def program(nc, d, upto="out"):
    with ExitStack() as ctx:
        core = Core(nc, ctx, d)
        modulation(core)
        norm_of_input(core)
        with ExitStack() as first:
            mix = first.enter_context(nc.sbuf_tensor("mix", [P, KT, SEQ], F32))
            with ExitStack() as gates:
                tbase = gates.enter_context(nc.sbuf_tensor("gate_rows", [P, SEQ], F32))
                rf = gates.enter_context(nc.sbuf_tensor("gate_rows_key", [P, SEQ], F32R))
                with ExitStack() as decays:
                    la = decays.enter_context(nc.sbuf_tensor("log_decay", [P, 2, SEQ], F32))
                    gates_and_pool(core, mix, la, tbase, rf)
                    linear_attention(core, mix, la)
                forgetting_attention(core, mix, tbase, rf)
            mixer_output(core, mix)
        core.clear_semaphores()
        with ExitStack() as mlp:
            hid = mlp.enter_context(nc.sbuf_tensor("hid", [P, FT, SEQ], F32))
            gate_and_up(core, hid)
            down(core, hid)
        with ExitStack() as second:
            hc = [second.enter_context(nc.sbuf_tensor(n, [P, KT, CTX], F32R)) for n in ("hc_hi", "hc_lo")]
            context_norm(core, hc)
            differential_attention(core, hc)
        with ExitStack() as last:
            feat = last.enter_context(nc.sbuf_tensor("feat", [P, KT, SEQ], F32))
            block_output(core, feat)


def feature_tiles(w):
    k, n = w.shape[0] // P, w.shape[1] // P
    return np.ascontiguousarray(w.reshape(k, P, n, P).transpose(2, 1, 0, 3).reshape(n, P, k * P))


def column(v):
    return v.reshape(-1, P).T


def shape_constants():
    c = np.zeros((P, NK), np.float32)
    p = np.arange(P)
    c[:, K_ID:K_ID + P] = np.eye(P)
    c[:, K_BLK:K_BLK + P] = p[:, None] // DH == p[None, :] // DH
    c[:, K_NEG:K_NEG + P] = np.where(p[None, :] > p[:, None], np.float32(NEG), 0)
    for t in range(2):
        window = np.where(p < 64, (2, 8)[t], (4, 16)[t])
        c[:, K_INVC + 16 * t:K_INVC + 16 * t + 16] = 1.0 / np.minimum(np.arange(1, 17)[None, :], window[:, None])
        c[:, K_INVW + t] = 1.0 / window
    c[:, K_SEL:K_SEL + 8] = p[:, None] % 32 == np.arange(8)[None, :]
    same = (p[:, None] // CHUNK == p[None, :] // CHUNK) & (p[:, None] <= p[None, :])
    mask = np.tile(same.astype(np.uint32), (1, 4))
    n = np.arange(SEQ)
    inv = (np.float32(10000.0) ** (-np.arange(0, 32, 2, dtype=np.float32) / np.float32(32))).astype(np.float32)
    pos = np.stack([n // 64, n % 64]).astype(np.float32)
    ang = (pos[(p % 64) // 32][:, :] * inv[p % 16][:, None]).astype(np.float32)
    sign = np.where((p % 32) < 16, -1.0, 1.0).astype(np.float32)[:, None]
    rope = np.ascontiguousarray(np.stack([np.cos(ang), sign * np.sin(ang)], axis=1).astype(np.float32))
    return c, mask, rope


def layout(i):
    f = lambda n: np.asarray(i[n])
    a = {}
    w = f("w_in")[0]
    pad = lambda *blocks: np.concatenate(blocks, axis=1)
    zeros = lambda n: np.zeros((D, n), w.dtype)
    pool, gq, gk, gv, gg, ga, fq, fk, fv, ff = np.split(w, np.cumsum([256, 256, 256, 256, 256, 16, 512, 512, 512]), axis=1)
    tile = lambda m, j: m[:, j * P:(j + 1) * P]
    order = [pad(ga, zeros(16), ff, zeros(88)), pool]
    for j in range(2):
        order += [tile(m, j) for m in (gq, gk, gv, gg)]
    for j in range(4):
        order += [tile(m, j) for m in (fq, fk, fv)]
    a["w_in"] = feature_tiles(np.concatenate(order, axis=1))
    wp = np.zeros((P, 2, P), w.dtype)
    for g in range(4):
        r = slice((g % 2) * 64, (g % 2 + 1) * 64)
        wp[r, g // 2, r] = f("w_pool")[0, g]
    a["w_pool"] = wp
    a["w_a_up"] = np.ascontiguousarray(f("w_a_up")[0])
    a["w_o"] = f("w_o")[0].reshape(KT, P, D)
    gu = f("w_gu")[0]
    a["w_gu"] = feature_tiles(np.concatenate([tile(m, j) for j in range(FT) for m in (gu[:, :D_FF], gu[:, D_FF:])], axis=1))
    a["w_down"] = f("w_down")[0].reshape(FT, P, D)
    a["ada_w"] = feature_tiles(f("ada_w_2")[0])
    da = np.split(f("da_w_in_2")[0], 4, axis=1)
    a["da_w_in"] = feature_tiles(np.concatenate([tile(m, j) for j in range(HEADS2) for m in da], axis=1))
    a["da_w_out"] = f("da_w_out_2")[0].reshape(KT, P, D)
    bf = np.zeros(P, np.float32)
    bf[32:40] = f("b_f")[0]
    a["cols"] = np.ascontiguousarray(np.concatenate(
        [column(f(n).reshape(-1)) for n in ("ln1", "ln2", "norm_gain_2", "pool_scale", "b_a", "gla_gn", "ada_b_2",
                                            "da_subln_gain_2", "c_2", "c_ctx_2")] + [column(bf)], axis=1))
    a["lam_rows"] = np.ascontiguousarray(np.concatenate([f("da_lam_q_2")[0], f("da_lam_k_2")[0]], axis=0))
    a["ln_f"] = np.ascontiguousarray(f("ln_f"))
    a["final_gain"] = np.ascontiguousarray(f("final_gain_2"))
    a["x"] = f("x").reshape(NT, P, D)
    a["ctx"] = f("ctx_2").reshape(2, P, D)
    a["shape_consts"], a["gla_mask"], a["rope"] = shape_constants()
    return a


def kernel(**inputs):
    import concourse.bacc as bacc
    from concourse.bass_utils import run_bass_kernel_spmd

    nc = bacc.Bacc("TRN2", target_bir_lowering=False, num_devices=1)
    arrays = layout(inputs)
    d = {n: nc.dram_tensor(f"in_{n}", a.shape, mybir.dt.from_np(a.dtype), kind="ExternalInput").ap()
         for n, a in arrays.items()}
    for n in ("x1", "x3", "o_feat"):
        d[n] = nc.dram_tensor(f"kept_{n}", (NT, P, D), F32, kind="Internal").ap()
    d["out"] = nc.dram_tensor("out_0", (NT, P, D), F32, kind="ExternalOutput").ap()
    program(nc, d)
    r = run_bass_kernel_spmd(nc, [{f"in_{n}": a for n, a in arrays.items()}], core_ids=[0])
    return r.results[0]["out_0"].reshape(1, SEQ, D)
```
